# Optimizing a Trainium2 kernel written in Bass

```python
import math
import jax, jax.numpy as jnp
from jax import lax
import numpy as np

D_MODEL = 1024
BATCH = 1
SEQ = 256
DEPTH = 1

HEAD_DIM = 64
N_HEADS_DSA = 8
N_HEADS_MOBA = 8
N_IDX_HEADS = 4
IDX_DIM = 64
DSA_TOPK = 256
MOBA_BLOCK = 256
MOBA_TOPK = 3
N_BUCKETS = 32
MAX_DISTANCE = 128
D_FF = 2816
Q_BLOCK = 128
MOBA_Q_CHUNK = 32
EPS = 1e-6

W_DSA = N_HEADS_DSA * HEAD_DIM
W_MOBA = N_HEADS_MOBA * HEAD_DIM
W_IDX_Q = N_IDX_HEADS * IDX_DIM
SPLIT_SIZES = (W_DSA, W_DSA, W_DSA, W_MOBA, W_MOBA, W_MOBA, W_IDX_Q, IDX_DIM, N_IDX_HEADS, 2 * D_MODEL)
SPLIT_POINTS = tuple(int(v) for v in np.cumsum(SPLIT_SIZES)[:-1])
D_IN = int(sum(SPLIT_SIZES))


def rmsnorm(x, g):
    xf = x.astype(jnp.float32)
    y = xf * lax.rsqrt(jnp.mean(xf * xf, axis=-1, keepdims=True) + EPS)
    return (y * g.astype(jnp.float32)).astype(x.dtype)

def swiglu(x, w_gu, w_down):
    gate, up = jnp.split(x @ w_gu, 2, axis=-1)
    return (jax.nn.silu(gate) * up) @ w_down

def t5_bucket(dist):
    max_exact = N_BUCKETS // 2
    d = jnp.maximum(dist, 0)
    df = jnp.maximum(d, 1).astype(jnp.float32)
    large = max_exact + (jnp.log(df / max_exact) / math.log(MAX_DISTANCE / max_exact)
                         * (N_BUCKETS - max_exact)).astype(jnp.int32)
    large = jnp.minimum(large, N_BUCKETS - 1)
    return jnp.where(d < max_exact, d, large)

def dsa_attention(q, k, v, q_idx, k_idx, w_idx, bias_tab):
    B, S, H, Dh = q.shape
    topk = min(DSA_TOPK, S // 4)
    scale = Dh ** -0.5
    key_pos = jnp.arange(S)
    b_ix = jnp.arange(B)[:, None, None]
    k_idx_f = k_idx.astype(jnp.float32)

    def block(i):
        t0 = i * Q_BLOCK
        qb = lax.dynamic_slice_in_dim(q, t0, Q_BLOCK, axis=1)
        qib = lax.dynamic_slice_in_dim(q_idx, t0, Q_BLOCK, axis=1).astype(jnp.float32)
        wib = lax.dynamic_slice_in_dim(w_idx, t0, Q_BLOCK, axis=1).astype(jnp.float32)
        q_pos = t0 + jnp.arange(Q_BLOCK)
        dots = jnp.einsum('bqhd,bsd->bqhs', qib, k_idx_f) * (IDX_DIM ** -0.5)
        scores = jnp.einsum('bqh,bqhs->bqs', wib, jax.nn.relu(dots))
        causal = key_pos[None, :] <= q_pos[:, None]
        scores = jnp.where(causal[None], scores, -jnp.inf)
        _, idx = lax.top_k(scores, topk)
        k_sel = k[b_ix, idx]
        v_sel = v[b_ix, idx]
        logits = jnp.einsum('bqhd,bqkhd->bqhk', qb, k_sel).astype(jnp.float32) * scale
        dist = q_pos[None, :, None] - idx
        bias = bias_tab[t5_bucket(dist)].astype(jnp.float32)
        logits = logits + jnp.transpose(bias, (0, 1, 3, 2))
        logits = jnp.where((dist >= 0)[:, :, None, :], logits, -jnp.inf)
        p = jax.nn.softmax(logits, axis=-1)
        return jnp.einsum('bqhk,bqkhd->bqhd', p.astype(v.dtype), v_sel)

    outs = lax.map(block, jnp.arange(S // Q_BLOCK))
    return jnp.transpose(outs, (1, 0, 2, 3, 4)).reshape(B, S, H * Dh)

def moba_attention(q, k, v, bias_tab):
    B, S, H, Dh = q.shape
    scale = Dh ** -0.5
    nb = -(-S // MOBA_BLOCK)
    pad = nb * MOBA_BLOCK - S
    kp = jnp.pad(k, ((0, 0), (0, pad), (0, 0), (0, 0))).reshape(B, nb, MOBA_BLOCK, H, Dh)
    vp = jnp.pad(v, ((0, 0), (0, pad), (0, 0), (0, 0))).reshape(B, nb, MOBA_BLOCK, H, Dh)
    counts = jnp.minimum(S - jnp.arange(nb) * MOBA_BLOCK, MOBA_BLOCK).astype(jnp.float32)
    k_mean = kp.astype(jnp.float32).sum(axis=2) / counts[None, :, None, None]
    kbT = jnp.transpose(kp, (0, 3, 1, 2, 4))
    vbT = jnp.transpose(vp, (0, 3, 1, 2, 4))
    n_sel = min(MOBA_TOPK, nb - 1)
    C = MOBA_Q_CHUNK
    b_ix = jnp.arange(B)[:, None, None, None]
    h_ix = jnp.arange(H)[None, None, :, None]
    h_ix5 = jnp.arange(H)[None, None, :, None, None]
    blk_ids = jnp.arange(nb)
    offs = jnp.arange(MOBA_BLOCK)

    def chunk(i):
        t0 = i * C
        qc = lax.dynamic_slice_in_dim(q, t0, C, axis=1)
        q_pos = t0 + jnp.arange(C)
        own = q_pos // MOBA_BLOCK
        own_b = jnp.broadcast_to(own[None, :, None, None], (B, C, H, 1))
        if n_sel > 0:
            gate = jnp.einsum('bqhd,bnhd->bqhn', qc.astype(jnp.float32), k_mean)
            past = blk_ids[None, :] < own[:, None]
            gate = jnp.where(past[None, :, None, :], gate, -jnp.inf)
            _, sel = lax.top_k(gate, n_sel)
            blocks = jnp.concatenate([sel, own_b], axis=-1)
            blk_valid = jnp.concatenate([sel < own[None, :, None, None],
                                         jnp.ones((B, C, H, 1), bool)], axis=-1)
        else:
            blocks = own_b
            blk_valid = jnp.ones((B, C, H, 1), bool)
        k_g = kbT[b_ix, h_ix, blocks]
        v_g = vbT[b_ix, h_ix, blocks]
        logits = jnp.einsum('bqhd,bqhjld->bqhjl', qc, k_g).astype(jnp.float32) * scale
        key_pos = blocks[..., None] * MOBA_BLOCK + offs
        dist = q_pos[None, :, None, None, None] - key_pos
        logits = logits + bias_tab[t5_bucket(dist), h_ix5].astype(jnp.float32)
        valid = (dist >= 0) & blk_valid[..., None]
        logits = jnp.where(valid, logits, -jnp.inf)
        J = blocks.shape[-1]
        p = jax.nn.softmax(logits.reshape(B, C, H, J * MOBA_BLOCK), axis=-1)
        p = p.reshape(B, C, H, J, MOBA_BLOCK).astype(v.dtype)
        return jnp.einsum('bqhjl,bqhjld->bqhd', p, v_g)

    outs = lax.map(chunk, jnp.arange(S // C))
    return jnp.transpose(outs, (1, 0, 2, 3, 4)).reshape(B, S, H * Dh)

def first_inputs(seed: int = 0) -> dict:
    key = jax.random.key(seed)
    ks = jax.random.split(key, 20)
    f32 = jnp.float32
    L = DEPTH

    def dense(k, shape):
        return jax.random.normal(k, shape, f32) * (shape[-2] ** -0.5)

    def gain(k, shape):
        return 1.0 + 0.02 * jax.random.normal(k, shape, f32)

    return {
        'x': jax.random.normal(ks[0], (BATCH, SEQ, D_MODEL), f32),
        'ffn1_norm': gain(ks[1], (L, D_MODEL)),
        'ffn1_w_gu': dense(ks[2], (L, D_MODEL, 2 * D_FF)),
        'ffn1_w_down': dense(ks[3], (L, D_FF, D_MODEL)),
        'mix_norm': gain(ks[4], (L, D_MODEL)),
        'w_in': dense(ks[5], (L, D_MODEL, D_IN)),
        'b_gate': 0.1 * jax.random.normal(ks[6], (L, 2 * D_MODEL), f32),
        'q_norm_dsa': gain(ks[7], (L, HEAD_DIM)),
        'k_norm_dsa': gain(ks[8], (L, HEAD_DIM)),
        'q_norm_moba': gain(ks[9], (L, HEAD_DIM)),
        'k_norm_moba': gain(ks[10], (L, HEAD_DIM)),
        'w_branch_dsa': dense(ks[11], (L, W_DSA, D_MODEL)),
        'w_branch_moba': dense(ks[12], (L, W_MOBA, D_MODEL)),
        'w_out': dense(ks[13], (L, D_MODEL, D_MODEL)),
        'ffn2_norm': gain(ks[14], (L, D_MODEL)),
        'ffn2_w_gu': dense(ks[15], (L, D_MODEL, 2 * D_FF)),
        'ffn2_w_down': dense(ks[16], (L, D_FF, D_MODEL)),
        'rel_bias': 0.1 * jax.random.normal(ks[17], (N_BUCKETS, N_HEADS_DSA + N_HEADS_MOBA), f32),
    }

def first_block(x, ffn1_norm, ffn1_w_gu, ffn1_w_down, mix_norm, w_in, b_gate,
              q_norm_dsa, k_norm_dsa, q_norm_moba, k_norm_moba,
              w_branch_dsa, w_branch_moba, w_out,
              ffn2_norm, ffn2_w_gu, ffn2_w_down, rel_bias):
    B, S, _ = x.shape
    bias_dsa = rel_bias[:, :N_HEADS_DSA]
    bias_moba = rel_bias[:, N_HEADS_DSA:]
    h = x
    for l in range(DEPTH):
        h = h + 0.5 * swiglu(rmsnorm(h, ffn1_norm[l]), ffn1_w_gu[l], ffn1_w_down[l])
        u = rmsnorm(h, mix_norm[l])
        qa, ka, va, qb, kb, vb, qi, ki, wi, g = jnp.split(u @ w_in[l], SPLIT_POINTS, axis=-1)
        qa = rmsnorm(qa.reshape(B, S, N_HEADS_DSA, HEAD_DIM), q_norm_dsa[l])
        ka = rmsnorm(ka.reshape(B, S, N_HEADS_DSA, HEAD_DIM), k_norm_dsa[l])
        va = va.reshape(B, S, N_HEADS_DSA, HEAD_DIM)
        qb = rmsnorm(qb.reshape(B, S, N_HEADS_MOBA, HEAD_DIM), q_norm_moba[l])
        kb = rmsnorm(kb.reshape(B, S, N_HEADS_MOBA, HEAD_DIM), k_norm_moba[l])
        vb = vb.reshape(B, S, N_HEADS_MOBA, HEAD_DIM)
        qi = qi.reshape(B, S, N_IDX_HEADS, IDX_DIM)
        wi = wi * (N_IDX_HEADS ** -0.5)
        out_a = dsa_attention(qa, ka, va, qi, ki, wi, bias_dsa)
        out_b = moba_attention(qb, kb, vb, bias_moba)
        gates = jax.nn.sigmoid((g + b_gate[l]).astype(jnp.float32)).astype(h.dtype)
        g_a, g_b = jnp.split(gates, 2, axis=-1)
        mixed = g_a * (out_a @ w_branch_dsa[l]) + g_b * (out_b @ w_branch_moba[l])
        h = h + mixed @ w_out[l]
        h = h + 0.5 * swiglu(rmsnorm(h, ffn2_norm[l]), ffn2_w_gu[l], ffn2_w_down[l])
    return h


DEPTH_2 = 2

N_MIXERS = 2
N_MLA_LAYERS = (DEPTH_2 + 1) // 2
N_SB_LAYERS = DEPTH_2 // 2
BLOCK_Q = 128
MLA_HEADS = 8
MLA_Q_LORA = 384
MLA_KV_LORA = 256
MLA_NOPE = 128
MLA_ROPE = 64
MLA_V = 128
ROPE_THETA = 10000.0
POS_OFFSET_MAX = 4096
SB_HEADS = 8
SB_HEAD_DIM = D_MODEL // SB_HEADS
MEM_LEN = 256
MEM_HEADS = 4
MEM_HEAD_DIM = 128
D_FF_2 = 4 * D_MODEL


NEG_BIG = -1e30

def rmsnorm_2(x, g):
    xf = x.astype(jnp.float32)
    y = xf * lax.rsqrt(jnp.mean(xf * xf, axis=-1, keepdims=True) + EPS)
    return (y * g.astype(jnp.float32)).astype(x.dtype)

def rope_tables(positions):
    inv_freq = ROPE_THETA ** (-jnp.arange(0, MLA_ROPE, 2, dtype=jnp.float32) / MLA_ROPE)
    ang = positions.astype(jnp.float32)[..., None] * inv_freq
    return jnp.cos(ang)[:, :, None, :], jnp.sin(ang)[:, :, None, :]

def apply_rope(x, cos, sin):
    half = x.shape[-1] // 2
    x1, x2 = x[..., :half], x[..., half:]
    c = cos.astype(x.dtype)
    s = sin.astype(x.dtype)
    return jnp.concatenate([x1 * c - x2 * s, x1 * s + x2 * c], axis=-1)

def blocked_causal_softmax_attn(q, k, v, scale):
    S = q.shape[1]
    outs = []
    for i in range(S // BLOCK_Q):
        lo, hi = i * BLOCK_Q, (i + 1) * BLOCK_Q
        s = jnp.einsum('bqhd,bkhd->bhqk', q[:, lo:hi], k[:, :hi]).astype(jnp.float32) * scale
        causal = (lo + jnp.arange(BLOCK_Q))[:, None] >= jnp.arange(hi)[None, :]
        p = jax.nn.softmax(jnp.where(causal, s, NEG_BIG), axis=-1).astype(v.dtype)
        outs.append(jnp.einsum('bhqk,bkhd->bqhd', p, v[:, :hi]))
    return jnp.concatenate(outs, axis=1)

def mla_mixer(h, cos, sin, w_dkv, g_q, g_kv, w_uq, w_ukv, w_o):
    B, S, _ = h.shape
    lat = h @ w_dkv
    c_q = rmsnorm_2(lat[..., :MLA_Q_LORA], g_q)
    c_kv = rmsnorm_2(lat[..., MLA_Q_LORA:MLA_Q_LORA + MLA_KV_LORA], g_kv)
    k_pe = lat[..., MLA_Q_LORA + MLA_KV_LORA:][:, :, None, :]
    q = (c_q @ w_uq).reshape(B, S, MLA_HEADS, MLA_NOPE + MLA_ROPE)
    kv = (c_kv @ w_ukv).reshape(B, S, MLA_HEADS, MLA_NOPE + MLA_V)
    q_pe = apply_rope(q[..., MLA_NOPE:], cos, sin)
    k_pe = apply_rope(k_pe, cos, sin)
    q = jnp.concatenate([q[..., :MLA_NOPE], q_pe], axis=-1)
    k = jnp.concatenate([kv[..., :MLA_NOPE],
                         jnp.broadcast_to(k_pe, (B, S, MLA_HEADS, MLA_ROPE))], axis=-1)
    v = kv[..., MLA_NOPE:]
    o = blocked_causal_softmax_attn(q, k, v, (MLA_NOPE + MLA_ROPE) ** -0.5)
    return o.reshape(B, S, MLA_HEADS * MLA_V) @ w_o

def stick_breaking_mixer(h, w_qkv, w_o):
    B, S, _ = h.shape
    qkv = (h @ w_qkv).reshape(B, S, 3, SB_HEADS, SB_HEAD_DIM)
    q, k, v = qkv[:, :, 0], qkv[:, :, 1], qkv[:, :, 2]
    scale = SB_HEAD_DIM ** -0.5
    outs = []
    for i in range(S // BLOCK_Q):
        lo, hi = i * BLOCK_Q, (i + 1) * BLOCK_Q
        z = jnp.einsum('bqhd,bkhd->bhqk', q[:, lo:hi], k[:, :hi]).astype(jnp.float32) * scale
        strict = jnp.arange(hi)[None, :] < (lo + jnp.arange(BLOCK_Q))[:, None]
        log_fail = jnp.where(strict, -jax.nn.softplus(z), 0.0)
        excl = lax.cumsum(log_fail, axis=3, reverse=True) - log_fail
        a = jnp.where(strict, jnp.exp(jax.nn.log_sigmoid(z) + excl), 0.0)
        outs.append(jnp.einsum('bhqk,bkhd->bqhd', a.astype(v.dtype), v[:, :hi]))
    o = jnp.concatenate(outs, axis=1)
    return o.reshape(B, S, SB_HEADS * SB_HEAD_DIM) @ w_o

def mem_cross_attn(h, m, w_q, w_kv, w_o):
    B, S, _ = h.shape
    q = (h @ w_q).reshape(B, S, MEM_HEADS, MEM_HEAD_DIM)
    kv = (m @ w_kv).reshape(B, m.shape[1], 2, MEM_HEADS, MEM_HEAD_DIM)
    s = jnp.einsum('bqhd,bmhd->bhqm', q, kv[:, :, 0]).astype(jnp.float32) * MEM_HEAD_DIM ** -0.5
    p = jax.nn.softmax(s, axis=-1).astype(h.dtype)
    o = jnp.einsum('bhqm,bmhd->bqhd', p, kv[:, :, 1])
    return o.reshape(B, S, MEM_HEADS * MEM_HEAD_DIM) @ w_o

def sq_relu_mlp(h, w_in, w_out):
    return jnp.square(jax.nn.relu(h @ w_in)) @ w_out

def second_inputs(seed: int = 0) -> dict:
    key = jax.random.key(seed)
    ks = iter(jax.random.split(key, 32))
    f32 = jnp.float32

    def w(shape, fan_in):
        return jax.random.normal(next(ks), shape, f32) * (fan_in ** -0.5)

    def gain(shape):
        return 1.0 + 0.02 * jax.random.normal(next(ks), shape, f32)

    x = jax.random.normal(next(ks), (BATCH, SEQ, D_MODEL), f32)
    mem = jax.random.normal(next(ks), (BATCH, MEM_LEN, D_MODEL), f32)
    offset = jax.random.randint(next(ks), (BATCH, 1), 0, POS_OFFSET_MAX, dtype=jnp.int32)
    positions = (offset + jnp.arange(SEQ, dtype=jnp.int32)[None, :]).astype(jnp.int32)
    return {
        "x": x,
        "mem": mem,
        "positions": positions,
        "norm_mix": gain((DEPTH_2, D_MODEL)),
        "norm_cross": gain((DEPTH_2, D_MODEL)),
        "norm_mem": gain((DEPTH_2, D_MODEL)),
        "norm_mlp": gain((DEPTH_2, D_MODEL)),
        "norm_final": gain((D_MODEL,)),
        "mla_w_dkv": w((N_MLA_LAYERS, D_MODEL, MLA_Q_LORA + MLA_KV_LORA + MLA_ROPE), D_MODEL),
        "mla_g_q": gain((N_MLA_LAYERS, MLA_Q_LORA)),
        "mla_g_kv": gain((N_MLA_LAYERS, MLA_KV_LORA)),
        "mla_w_uq": w((N_MLA_LAYERS, MLA_Q_LORA, MLA_HEADS * (MLA_NOPE + MLA_ROPE)), MLA_Q_LORA),
        "mla_w_ukv": w((N_MLA_LAYERS, MLA_KV_LORA, MLA_HEADS * (MLA_NOPE + MLA_V)), MLA_KV_LORA),
        "mla_w_o": w((N_MLA_LAYERS, MLA_HEADS * MLA_V, D_MODEL), MLA_HEADS * MLA_V),
        "sb_w_qkv": w((N_SB_LAYERS, D_MODEL, 3 * SB_HEADS * SB_HEAD_DIM), D_MODEL),
        "sb_w_o": w((N_SB_LAYERS, SB_HEADS * SB_HEAD_DIM, D_MODEL), SB_HEADS * SB_HEAD_DIM),
        "xa_w_q": w((DEPTH_2, D_MODEL, MEM_HEADS * MEM_HEAD_DIM), D_MODEL),
        "xa_w_kv": w((DEPTH_2, D_MODEL, 2 * MEM_HEADS * MEM_HEAD_DIM), D_MODEL),
        "xa_w_o": w((DEPTH_2, MEM_HEADS * MEM_HEAD_DIM, D_MODEL), MEM_HEADS * MEM_HEAD_DIM),
        "mlp_w_in": w((DEPTH_2, D_MODEL, D_FF_2), D_MODEL),
        "mlp_w_out": w((DEPTH_2, D_FF_2, D_MODEL), D_FF_2),
    }

def second_block(x, mem, positions, norm_mix, norm_cross, norm_mem, norm_mlp, norm_final,
              mla_w_dkv, mla_g_q, mla_g_kv, mla_w_uq, mla_w_ukv, mla_w_o,
              sb_w_qkv, sb_w_o, xa_w_q, xa_w_kv, xa_w_o, mlp_w_in, mlp_w_out):
    cos, sin = rope_tables(positions)
    h = x
    for i in range(DEPTH_2):
        a = rmsnorm_2(h, norm_mix[i])
        j = i // N_MIXERS
        if i % N_MIXERS == 0:
            h = h + mla_mixer(a, cos, sin, mla_w_dkv[j], mla_g_q[j], mla_g_kv[j],
                              mla_w_uq[j], mla_w_ukv[j], mla_w_o[j])
        else:
            h = h + stick_breaking_mixer(a, sb_w_qkv[j], sb_w_o[j])
        h = h + mem_cross_attn(rmsnorm_2(h, norm_cross[i]), rmsnorm_2(mem, norm_mem[i]),
                               xa_w_q[i], xa_w_kv[i], xa_w_o[i])
        h = h + sq_relu_mlp(rmsnorm_2(h, norm_mlp[i]), mlp_w_in[i], mlp_w_out[i])
    return rmsnorm_2(h, norm_final)


def setup_inputs(seed=0):
    out = dict(first_inputs(seed))
    for name, value in second_inputs(seed + 1).items():
        if name != "x":
            out[name + "_2"] = value
    return out


def reference(
    x, ffn1_norm, ffn1_w_gu, ffn1_w_down, mix_norm, w_in, b_gate, q_norm_dsa, k_norm_dsa,
    q_norm_moba, k_norm_moba, w_branch_dsa, w_branch_moba, w_out, ffn2_norm, ffn2_w_gu,
    ffn2_w_down, rel_bias, mem_2, positions_2, norm_mix_2, norm_cross_2, norm_mem_2, norm_mlp_2,
    norm_final_2, mla_w_dkv_2, mla_g_q_2, mla_g_kv_2, mla_w_uq_2, mla_w_ukv_2, mla_w_o_2,
    sb_w_qkv_2, sb_w_o_2, xa_w_q_2, xa_w_kv_2, xa_w_o_2, mlp_w_in_2, mlp_w_out_2,
):
    x = first_block(
        x, ffn1_norm, ffn1_w_gu, ffn1_w_down, mix_norm, w_in, b_gate, q_norm_dsa, k_norm_dsa,
        q_norm_moba, k_norm_moba, w_branch_dsa, w_branch_moba, w_out, ffn2_norm, ffn2_w_gu,
        ffn2_w_down, rel_bias,
    )
    return second_block(
        x, mem_2, positions_2, norm_mix_2, norm_cross_2, norm_mem_2, norm_mlp_2, norm_final_2,
        mla_w_dkv_2, mla_g_q_2, mla_g_kv_2, mla_w_uq_2, mla_w_ukv_2, mla_w_o_2, sb_w_qkv_2,
        sb_w_o_2, xa_w_q_2, xa_w_kv_2, xa_w_o_2, mlp_w_in_2, mlp_w_out_2,
    )


_drawn_inputs = setup_inputs


def setup_inputs(seed=0):
    import zlib

    import numpy as np

    out = dict(_drawn_inputs(seed))
    spreads = {}
    factors = {'ffn1_norm': 3.446,
     'mix_norm': 3.247,
     'b_gate': 6.108,
     'q_norm_dsa': 8.0,
     'k_norm_dsa': 8.0,
     'q_norm_moba': 8.0,
     'k_norm_moba': 8.0,
     'ffn2_norm': 6.235,
     'rel_bias': 3.632,
     'norm_mix_2': 4.822,
     'norm_cross_2': 8.0,
     'norm_mem_2': 8.0,
     'norm_final_2': 7.877,
     'mla_g_q_2': 8.0,
     'mla_g_kv_2': 8.0,
     'norm_mlp_2': 8.0}
    for name, (base, spread) in spreads.items():
        noise = np.random.default_rng([zlib.crc32(name.encode()), seed]).standard_normal(out[name].shape)
        drawn = base * np.exp(spread * noise) if base else spread * noise
        out[name] = __import__('jax').numpy.asarray(drawn.astype(out[name].dtype))
    for name, factor in factors.items():
        out[name] = (out[name] * factor).astype(out[name].dtype)
    return out
```

```python
from contextlib import ExitStack

import numpy as np

import concourse.bass as bass
from concourse import mybir

F32 = mybir.dt.float32
F32R = mybir.dt.float32r
I32 = mybir.dt.int32
ALU = mybir.AluOpType
ACT = mybir.ActivationFunctionType
AX = mybir.AxisListType

P = 128
S = 256
NT = S // P
D = 1024
KC = D // P
TW = 512
NB = D // TW
RING = 4
EPS = 1e-6
NEG = -1e30
TAKEN = -3e38
FF1, FF2 = 2816, 4096
H1, HD1 = 8, 64
TOPK = 64
H2, HD2 = 8, 128
ROPE, HALF = 64, 32
MLA_SCALE = (HD2 + ROPE) ** -0.5
SB_SCALE = HD2 ** -0.5
MEM_SCALE = 128 ** -0.5
NXH = 4
QL, KL = 384, 256
NPARTS, NBUCK = 4, 32

NORMS = ["ffn1", "mix", "ffn2", "mla", "mem0", "cross0", "mlp0", "sb", "mem1", "cross1", "mlp1", "final"]
NORM = {n: i for i, n in enumerate(NORMS)}
QG_A, KG_A, QG_B, KG_B, QG_L, KG_L = 96, 97, 98, 99, 100, 103
NGAIN = 105


def weight_plan():
    plan, at = [], {}

    def add(section, array, tiles, width=TW):
        at.setdefault(section, len(plan))
        first = sum(1 for c in plan if c[0] == array)
        plan.extend((array, first + i, n, width) for i, n in enumerate(tiles))

    def ffn(name, steps, out_tiles):
        add(name, name + "_first", [2] * 4)
        add(name + "_mid", name + "_mid", [(8 + out_tiles) // 4] * 4 * (steps - 1))
        add(name + "_tail", name + "_tail", [out_tiles // 4] * 4)

    ffn("ffn1", 11, 4)
    add("idx", "w_idx", [2] * 4, 324)
    add("qkv", "w_qkv", [4] * 12)
    add("br_a", "w_br_a", [4] * 2)
    add("gate_a", "w_gate_a", [4] * 4)
    add("br_b", "w_br_b", [4] * 2)
    add("gate_b", "w_gate_b", [4] * 4)
    add("w_out", "w_out", [4] * 4)
    ffn("ffn2", 11, 4)
    add("dq", "w_dq", [4] * 2, QL)
    add("dkv", "w_dkv", [4] * 2, KL + ROPE)
    add("uq", "w_uq", [3] * 3)
    add("ukv", "w_ukv", [2] * 4)
    add("mla_o", "w_mla_o", [4] * 4)
    for i in range(2):
        if i == 1:
            add("sb_qkv", "w_sb_qkv", [4] * 12)
            add("sb_o", "w_sb_o", [4] * 4)
        add(f"xkv{i}", f"w_xkv{i}", [4] * 4)
        add(f"xq{i}", f"w_xq{i}", [4] * 2)
        add(f"xo{i}", f"w_xo{i}", [4] * 2)
        ffn(f"mlp{i}", 8, 8)
    return plan, at


PLAN, AT = weight_plan()


def t5_buckets(dist):
    d = np.maximum(dist, 0)
    large = 16 + (np.log(np.maximum(d, 1) / 16.0) / np.log(8.0) * 16).astype(np.int64)
    return np.where(d < 16, d, np.minimum(large, 31))


C_ID, C_CAUSAL, C_STRICT, C_SUFFIX, C_ONES, C_FREQ, C_BUCK = 0, 128, 384, 768, 896, 1024, 1056
RELW = 383
NCONST = C_BUCK + 384


def constants():
    c = np.zeros((P, NCONST), np.float32)
    row, col = np.arange(P)[:, None], np.arange(P)[None, :]
    c[:, C_ID:C_ID + P] = row == col
    c[:, C_CAUSAL + P:C_CAUSAL + 2 * P] = np.where(col <= row, 0.0, NEG)
    strict = np.where(row < col, 0.0, NEG)
    c[:, C_STRICT:C_STRICT + P] = strict
    c[:, C_STRICT + 2 * P:C_STRICT + 3 * P] = strict
    c[:, C_SUFFIX:C_SUFFIX + P] = np.where(row >= col, -1.0, 0.0)
    c[:, C_ONES:C_ONES + P] = -1.0
    exponent = -np.arange(0, ROPE, 2, dtype=np.float32) / np.float32(ROPE)
    c[:, C_FREQ:C_FREQ + HALF] = (10000.0 ** exponent.astype(np.float64)).astype(np.float32)
    dist = 255 - np.arange(RELW)
    for x, (d, b) in enumerate(zip(dist, t5_buckets(dist))):
        c[b if d >= 0 else NBUCK, C_BUCK + x] = 1.0
    return c


def chunked(a, tiles):
    u, p, t, w = a.shape
    return np.ascontiguousarray(
        a.reshape(u, p, t // tiles, tiles * w).transpose(0, 2, 1, 3).reshape(-1, p, tiles * w))


def by_block(w, width=TW):
    k, n = w.shape
    return w.reshape(k // P, P, n // width, width).transpose(2, 1, 0, 3)


def by_row(w, steps=1):
    k, n = w.shape
    return w.reshape(steps, k // P // steps, P, NB, TW).transpose(0, 2, 1, 3, 4).reshape(steps, P, -1, TW)


def ffn_arrays(name, up, down):
    n = up.shape[0]
    each = (8 + down.shape[2]) // 4
    return {name + "_first": chunked(up[:1], 2),
            name + "_mid": chunked(np.concatenate([up[1:], down[:n - 1]], axis=2), each),
            name + "_tail": chunked(down[n - 1:], down.shape[2] // 4)}


def host_arrays(x):
    out = {"x": np.ascontiguousarray(x["x"][0].reshape(NT, P, D).transpose(1, 0, 2)),
           "mem": np.ascontiguousarray(x["mem_2"][0].reshape(NT, P, D).transpose(1, 0, 2)),
           "positions": np.ascontiguousarray(x["positions_2"].astype(np.int32)[0].reshape(NT, P).T),
           "consts": constants()}
    for n in ("ffn1", "ffn2"):
        gu = x[n + "_w_gu"][0]
        up = gu.reshape(KC, P, 2, 11, 256).transpose(3, 1, 0, 2, 4).reshape(11, P, KC, TW)
        out.update(ffn_arrays(n, up, by_row(x[n + "_w_down"][0], 11)))
    w = x["w_in"][0]
    out["w_idx"] = chunked(by_block(w[:, 3072:3396], 324), 2)
    order = [3, 4, 0, 1, 5, 2]
    out["w_qkv"] = chunked(by_block(w[:, :3072])[order], 4)
    gates = by_block(w[:, 3396:])
    out["w_gate_a"], out["w_gate_b"] = chunked(gates[:2], 4), chunked(gates[2:], 4)
    out["w_br_a"] = chunked(by_row(x["w_branch_dsa"][0]), 4)
    out["w_br_b"] = chunked(by_row(x["w_branch_moba"][0]), 4)
    out["w_out"] = chunked(by_row(x["w_out"][0]), 4)
    dkv = x["mla_w_dkv_2"][0]
    out["w_dq"] = chunked(by_block(dkv[:, :QL], QL), 4)
    out["w_dkv"] = chunked(by_block(dkv[:, QL:], KL + ROPE), 4)
    uq = x["mla_w_uq_2"][0].reshape(QL, H2, HD2 + ROPE)
    parts = [uq[:, :, :HD2], uq[:, :, HD2:HD2 + HALF], uq[:, :, HD2 + HALF:]]
    out["w_uq"] = chunked(by_block(np.concatenate([p.reshape(QL, -1) for p in parts], axis=1)), 3)
    ukv = x["mla_w_ukv_2"][0].reshape(KL, H2, 2, HD2).transpose(0, 2, 1, 3).reshape(KL, -1)
    out["w_ukv"] = chunked(by_block(ukv), 2)
    out["w_mla_o"] = chunked(by_row(x["mla_w_o_2"][0]), 4)
    out["w_sb_qkv"] = chunked(by_block(x["sb_w_qkv_2"][0]), 4)
    out["w_sb_o"] = chunked(by_row(x["sb_w_o_2"][0]), 4)
    for i in range(2):
        out[f"w_xkv{i}"] = chunked(by_block(x["xa_w_kv_2"][i]), 4)
        out[f"w_xq{i}"] = chunked(by_block(x["xa_w_q_2"][i]), 4)
        out[f"w_xo{i}"] = chunked(by_row(x["xa_w_o_2"][i]), 4)
        out.update(ffn_arrays(f"mlp{i}", by_block(x["mlp_w_in_2"][i]), by_row(x["mlp_w_out_2"][i], 8)))
    gains = [x["ffn1_norm"][0], x["mix_norm"][0], x["ffn2_norm"][0], x["norm_mix_2"][0],
             x["norm_mem_2"][0], x["norm_cross_2"][0], x["norm_mlp_2"][0], x["norm_mix_2"][1],
             x["norm_mem_2"][1], x["norm_cross_2"][1], x["norm_mlp_2"][1], x["norm_final_2"]]
    columns = [g.reshape(KC, P).T for g in gains]
    for n in ("q_norm_dsa", "k_norm_dsa", "q_norm_moba", "k_norm_moba"):
        columns.append(np.concatenate([x[n][0], x[n][0]])[:, None])
    columns += [x["mla_g_q_2"][0].reshape(-1, P).T, x["mla_g_kv_2"][0].reshape(-1, P).T]
    out["gains"] = np.ascontiguousarray(np.concatenate(columns, axis=1))
    out["b_gate"] = np.ascontiguousarray(x["b_gate"])
    out["norm_final"] = np.ascontiguousarray(x["norm_final_2"][None, :])
    out["rel_bias"] = np.ascontiguousarray(x["rel_bias"])
    return out


class Count:

    def __init__(self, sem):
        self.sem, self.n = sem, 0

    def inc(self, ins):
        ins.then_inc(self.sem, 1)
        self.n += 1
        return self.n


def build(nc, dram, out):
    ctx = ExitStack()
    with ctx:
        def sb(name, shape, dt=F32):
            return ctx.enter_context(nc.sbuf_tensor(name, shape, dt))

        def sem(name):
            return ctx.enter_context(nc.semaphore(name))

        w_raw = sb("w_raw", [P, RING, 4 * TW])
        whi = sb("whi", [P, RING, 4 * TW], F32R)
        wlo = sb("wlo", [P, RING, 4 * TW], F32R)
        h = sb("h", [P, NT, D])
        xt_h = sb("xt_h", [P, KC, S], F32R)
        xt_l = sb("xt_l", [P, KC, S], F32R)
        ot_h = sb("ot_h", [P, KC, S], F32R)
        ot_l = sb("ot_l", [P, KC, S], F32R)
        qt = sb("qt", [P, KC, S])
        kt = sb("kt", [P, KC, S])
        v = sb("v", [P, NT, D])
        pet = sb("pet", [P, 5, S])
        rel = sb("rel", [P, 16, S])
        nat = sb("nat", [P, 2, NT, TW])
        lg = sb("lg", [P, 2, TW])
        pt = sb("pt", [P, 2, TW])
        score = sb("score", [P, NT, S])
        const = sb("const", [P, C_BUCK])
        gain = sb("gain", [P, NGAIN])
        ms = sb("ms", [P, 2 * len(NORMS) + 4])
        rs = sb("rs", [P, 2 * len(NORMS) + 4])
        col = sb("col", [P, 3])
        hs = sb("hs", [P, NT, 16])
        nmax = sb("nmax", [P, 32])
        rsum = sb("rsum", [P, 32])
        rinv = sb("rinv", [P, 32])
        top8 = sb("top8", [P, NT, 8])
        wi = sb("wi", [P, NT, NPARTS])
        trig = sb("trig", [P, 2, NT, HALF])
        pos = sb("pos", [P, 4])

        ps = ctx.enter_context(nc.psum_tensor("ps", [P, 8, TW], F32))
        bankA = [ps[:, 0], ps[:, 1]]
        bankT = [ps[:, 2], ps[:, 3]]
        bankD = [[ps[:, 4], ps[:, 5]], [ps[:, 6], ps[:, 7]]]
        ident = const[:, C_ID:C_ID + P]

        w_loaded = [sem(f"w_loaded{s}") for s in range(RING)]
        w_hi = sem("w_hi")
        w_lo = sem("w_lo")
        w_used = sem("w_used")
        consts_in = sem("consts_in")
        x_in = sem("x_in")
        col_set = sem("col_set")
        mem_in = sem("mem_in")
        h_ready = sem("h_ready")
        xt_ps = sem("xt_ps")
        xt_hi = sem("xt_hi")
        xt_lo = sem("xt_lo")
        rs_ready = sem("rs_ready")
        rows_made = sem("rows_made")
        rows_ps = sem("rows_ps")
        rows_hi = sem("rows_hi")
        rows_lo = sem("rows_lo")
        all_fins = []
        out_full = sem("out_full")
        out_projects = []
        act_own = Count(sem("act_own"))
        dve_own = Count(sem("dve_own"))

        def own(eng, counter, ins):
            eng.wait_ge(counter.sem, counter.inc(ins))

        ends = {}

        def used(ins, n):
            if n not in ends:
                back = 1
                while n - back in ends:
                    back += 1
                ins.then_inc(w_used, back)

        def slot_of(n):
            return n % RING

        def load_chunk(sp, n, r=0):
            array, k, tiles, width = PLAN[n]
            if n >= RING:
                sp.wait_ge(w_hi, r * RING + (n - RING + 1))
                sp.wait_ge(w_lo, r * RING + (n - RING + 1))
            if isinstance(r, int):
                src = dram[array][k + r * RING]
            else:
                src = dram[array][bass.ds(r * RING + k, 1)].rearrange("a p n -> p (a n)")
            sp.dma_start(w_raw[:, slot_of(n), 0:tiles * width], src).then_inc(w_loaded[slot_of(n)], 16)

        def split_hi(act, n, r=0):
            _, _, tiles, width = PLAN[n]
            s = slot_of(n)
            act.wait_ge(w_loaded[s], r * 16 + 16 * (n // RING + 1))
            if n - RING in ends:
                done, value, each = ends[n - RING]
                act.wait_ge(done, r * each + value)
            elif n >= RING:
                act.wait_ge(w_used, r * RING + (n - RING + 1))
            nc.scalar.activation(whi[:, s, 0:tiles * width], w_raw[:, s, 0:tiles * width],
                                 ACT.Copy).then_inc(w_hi, 1)

        def split_lo(dve, n, r=0):
            _, _, tiles, width = PLAN[n]
            s = slot_of(n)
            dve.wait_ge(w_hi, r * RING + (n + 1))
            nc.vector.tensor_tensor(wlo[:, s, 0:tiles * width], w_raw[:, s, 0:tiles * width],
                                    whi[:, s, 0:tiles * width].bitcast(F32), ALU.subtract).then_inc(w_lo, 1)

        def next_hi(act, n, r=0):
            if n + RING < len(PLAN):
                split_hi(act, n + RING, r)

        def next_lo(dve, n, r=0):
            if n + RING < len(PLAN):
                split_lo(dve, n + RING, r)

        def take_chunk(pe, n, r=0):
            pe.wait_ge(w_hi, r * RING + (n + 1))
            pe.wait_ge(w_lo, r * RING + (n + 1))

        def mm3(acc, hi, lo, s, j, width, start, stop):
            c = slice(j * width, (j + 1) * width)
            nc.tensor.matmul(acc, hi, whi[:, s, c], start=start, stop=False)
            nc.tensor.matmul(acc, hi, wlo[:, s, c], start=False, stop=False)
            return nc.tensor.matmul(acc, lo, whi[:, s, c], start=False, stop=stop)

        def norm_banks(name):
            last = bankA if name.startswith("mem") else [bankD[0][0], bankD[0][1]]
            return [bankT[0], bankT[1], last[0], last[1]]

        def source_ready(eng, name, block):
            if name.startswith("mem"):
                eng.wait_ge(mem_in, 16 * (int(name[3]) + 1))
            elif name == "ffn1":
                eng.wait_ge(x_in, 16)
            else:
                updates = [n for n in NORMS[:NORM[name]] if not n.startswith("mem")]
                eng.wait_ge(h_ready, 4 * len(updates) - (2 if block == 0 else 0))

        def norm_tensor(pe, name):
            src = v if name.startswith("mem") else h
            for pair, bank in enumerate(norm_banks(name)):
                if pair % 2 == 0:
                    source_ready(pe, name, pair // 2)
                for j in range(2):
                    for t in range(NT):
                        k = 2 * pair + j
                        last = nc.tensor.transpose(bank[:, j * S + t * P:j * S + (t + 1) * P],
                                                   src[:, t, k * P:(k + 1) * P], ident)
                last.then_inc(xt_ps, 1)

        def norm_scalar(act, name):
            k0, to = 4 * NORM[name], ot_h if name.startswith("mem") else xt_h
            for pair, bank in enumerate(norm_banks(name)):
                act.wait_ge(xt_ps, k0 + pair + 1)
                for j in range(2):
                    k = 2 * pair + j
                    last = nc.scalar.activation(to[:, k], bank[:, j * S:(j + 1) * S], ACT.Copy,
                                                scale=gain[:, 8 * NORM[name] + k:8 * NORM[name] + k + 1])
                last.then_inc(xt_hi, 1)

        def rms_scalar(act, name, last_of=None):
            src, c = v if name.startswith("mem") else h, 2 * NORM[name]
            source_ready(act, name, 1)
            for t in range(NT):
                own(act, act_own, nc.scalar.activation(
                    lg[:, :, :].rearrange("p a n -> p (a n)"), src[:, t], ACT.Square,
                    scale=D ** -0.5, accum_out=ms[:, c + t:c + t + 1]))
            root_scalar(act, ms[:, c:c + 2], rs[:, c:c + 2]).then_inc(rs_ready, 1)

        def root_scalar(act, mean, to):
            nc.scalar.preload_act_table_set("natural_log_exp_and_others")
            own(act, act_own, nc.scalar.activation(mean, mean, ACT.Ln, bias=col[:, 0:1]))
            return nc.scalar.activation(to, mean, ACT.Exp, scale=-0.5)

        def norm_vector(dve, name):
            k0, (hi, lo) = 4 * NORM[name], (ot_h, ot_l) if name.startswith("mem") else (xt_h, xt_l)
            for pair, bank in enumerate(norm_banks(name)):
                dve.wait_ge(xt_hi, k0 + pair + 1)
                for j in range(2):
                    k = 2 * pair + j
                    g = gain[:, 8 * NORM[name] + k:8 * NORM[name] + k + 1]
                    last = nc.vector.scalar_tensor_tensor(
                        out=lo[:, k], in0=bank[:, j * S:(j + 1) * S], scalar=g,
                        in1=hi[:, k].bitcast(F32), op0=ALU.mult, op1=ALU.subtract)
                last.then_inc(xt_lo, 1)

        def xt_ready(pe, name, k):
            pe.wait_ge(xt_lo, 4 * NORM[name] + k // 2 + 1)

        def rms(name, t):
            return rs[:, 2 * NORM[name] + t:2 * NORM[name] + t + 1]

        def residual_vector(dve, full, scale, full0=0):
            for block in range(NB):
                for t in range(NT):
                    dve.wait_ge(full, full0 + NT * block + t + 1)
                    hb = h[:, t, block * TW:(block + 1) * TW]
                    nc.vector.scalar_tensor_tensor(out=hb, in0=bankD[t][block], scalar=scale, in1=hb,
                                                   op0=ALU.mult, op1=ALU.add).then_inc(h_ready, 1)

        class Ffn:
            def __init__(self, name, steps, hk, gated, scale):
                self.name, self.steps, self.hk, self.gated, self.scale = name, steps, hk, gated, scale
                self.n0 = AT[name]
                self.tiles = (8 + 2 * hk) // 4
                self.up_full = sem(name + "_up_full")
                self.acted = sem(name + "_acted")
                self.hidden = sem(name + "_hidden")
                self.hid_ps = sem(name + "_hid_ps")
                self.hid_hi = sem(name + "_hid_hi")
                self.hid_lo = sem(name + "_hid_lo")
                self.down_full = sem(name + "_down_full")
                ends[self.n0 + 3] = (self.up_full, NT, 0)
                tail = self.n0 + 4 * steps
                ends[tail + 3] = (self.down_full, NB * NT, 0)
                if gated:
                    ends[tail + 2] = (self.down_full, NT, 0)
                else:
                    for i in range(1, steps):
                        ends[self.n0 + 4 * i + 1] = (self.up_full, NT * (i + 1), NT)

            def up(self, pe, i, s, pos, ks, fresh):
                for t in range(NT):
                    if ks[0] == 0 and not fresh:
                        pe.wait_ge(self.hidden if self.gated else self.acted, i * NT + (t - 1))
                    for j, k in enumerate(ks):
                        if fresh and t == 0 and k % 2 == 0:
                            xt_ready(pe, self.name, k)
                        last = mm3(bankA[t], xt_h[:, k, t * P:(t + 1) * P], xt_l[:, k, t * P:(t + 1) * P],
                                   s, pos + j, TW, k == 0, k == KC - 1)
                    if ks[-1] == KC - 1:
                        last.then_inc(self.up_full, 1)
                return last

            def down(self, pe, s, pos, js, first, final):
                for a, j in enumerate(js):
                    k, block = j // NB, j % NB
                    for t in range(NT):
                        last = mm3(bankD[t][block], ot_h[:, k, t * P:(t + 1) * P],
                                   ot_l[:, k, t * P:(t + 1) * P], s, pos + a, TW,
                                   first and k == 0, final and k == self.hk - 1)
                        if final and k == self.hk - 1:
                            last.then_inc(self.down_full, 1)
                return last

            def turn(self, pe, i):
                pe.wait_ge(self.hidden, i * NT)
                if not isinstance(i, int) or i > 1:
                    pe.wait_ge(self.hid_lo, i - 1)
                for k in range(self.hk):
                    for t in range(NT):
                        at = (k % 2) * S + t * P
                        last = nc.tensor.transpose(bankT[k // 2][:, at:at + P],
                                                   nat[:, 0, t, k * P:(k + 1) * P], ident)
                last.then_inc(self.hid_ps, 1)

            def step_tensor(self, pe, i, n, r=0, first=False):
                self.turn(pe, i)
                for c in range(4):
                    take_chunk(pe, n + c, r)
                    tiles = list(range(c * self.tiles, (c + 1) * self.tiles))
                    ups, downs = [j for j in tiles if j < KC], [j - KC for j in tiles if j >= KC]
                    if ups:
                        last = self.up(pe, i, slot_of(n + c), 0, ups, False)
                    if downs:
                        if downs[0] == 0:
                            pe.wait_ge(self.hid_lo, i)
                        last = self.down(pe, slot_of(n + c), len(ups), downs, first, False)
                    used(last, n + c)

            def tensor(self, pe):
                norm_tensor(pe, self.name)
                for c in range(4):
                    take_chunk(pe, self.n0 + c)
                    used(self.up(pe, 0, slot_of(self.n0 + c), 0, [2 * c, 2 * c + 1], True), self.n0 + c)
                self.step_tensor(pe, 1, self.n0 + 4, first=True)
                with pe.Fori(0, self.steps - 2) as r:
                    self.step_tensor(pe, r + 2, self.n0 + 8, r)
                self.turn(pe, self.steps)
                pe.wait_ge(self.hid_lo, self.steps)
                n, each = self.n0 + 4 * self.steps, self.hk // 2
                for c in range(4):
                    take_chunk(pe, n + c)
                    used(self.down(pe, slot_of(n + c), 0, list(range(c * each, (c + 1) * each)),
                                   False, True), n + c)

            def take_up_scalar(self, act, i):
                for t in range(NT):
                    act.wait_ge(self.up_full, i * NT + (t + 1))
                    if not isinstance(i, int) or i > 0:
                        act.wait_ge(self.hidden, i * NT + (t - 1))
                    if self.gated:
                        ins = nc.scalar.activation(lg[:, t, 0:256], bankA[t][:, 0:256], ACT.Silu,
                                                   scale=rms(self.name, t))
                    else:
                        ins = nc.scalar.activation(lg[:, t], bankA[t], ACT.Relu, scale=rms(self.name, t))
                    ins.then_inc(self.acted, 1)

            def turned_scalar(self, act, i):
                act.wait_ge(self.hid_ps, i)
                for b in range(self.hk // 2):
                    last = nc.scalar.activation(ot_h[:, 2 * b:2 * b + 2],
                                                bankT[b].rearrange("p (k s) -> p k s", k=2), ACT.Copy)
                last.then_inc(self.hid_hi, 1)

            def step_scalar(self, act, i, n, r=0):
                self.turned_scalar(act, i)
                next_hi(act, n, r)
                next_hi(act, n + 1, r)
                self.take_up_scalar(act, i)
                next_hi(act, n + 2, r)
                next_hi(act, n + 3, r)

            def scalar(self, act):
                norm_scalar(act, self.name)
                rms_scalar(act, self.name)
                if self.gated:
                    nc.scalar.preload_act_table(ACT.Silu)
                act.wait_ge(rs_ready, NORM[self.name] + 1)
                for c in range(3):
                    next_hi(act, self.n0 + c)
                self.take_up_scalar(act, 0)
                next_hi(act, self.n0 + 3)
                with act.Fori(0, self.steps - 2) as r:
                    self.step_scalar(act, r + 1, self.n0 + 4, r)
                self.step_scalar(act, self.steps - 1, self.n0 + 4 * (self.steps - 1))
                self.turned_scalar(act, self.steps)
                for c in range(4):
                    next_hi(act, self.n0 + 4 * self.steps + c)

            def hide_vector(self, dve, i):
                for t in range(NT):
                    dve.wait_ge(self.acted, i * NT + (t + 1))
                    if not isinstance(i, int) or i > 0:
                        dve.wait_ge(self.hid_ps, i)
                    if self.gated:
                        ins = nc.vector.scalar_tensor_tensor(
                            out=nat[:, 0, t, 0:256], in0=bankA[t][:, 256:512], scalar=rms(self.name, t),
                            in1=lg[:, t, 0:256], op0=ALU.mult, op1=ALU.mult)
                    else:
                        ins = nc.vector.tensor_tensor(nat[:, 0, t], lg[:, t], lg[:, t], ALU.mult)
                    ins.then_inc(self.hidden, 1)

            def turned_vector(self, dve, i):
                dve.wait_ge(self.hid_hi, i)
                for b in range(self.hk // 2):
                    last = nc.vector.tensor_tensor(ot_l[:, 2 * b:2 * b + 2],
                                                   bankT[b].rearrange("p (k s) -> p k s", k=2),
                                                   ot_h[:, 2 * b:2 * b + 2].bitcast(F32), ALU.subtract)
                last.then_inc(self.hid_lo, 1)

            def step_vector(self, dve, i, n, r=0):
                self.turned_vector(dve, i)
                next_lo(dve, n, r)
                next_lo(dve, n + 1, r)
                self.hide_vector(dve, i)
                next_lo(dve, n + 2, r)
                next_lo(dve, n + 3, r)

            def vector(self, dve):
                norm_vector(dve, self.name)
                dve.wait_ge(rs_ready, NORM[self.name] + 1)
                for c in range(3):
                    next_lo(dve, self.n0 + c)
                self.hide_vector(dve, 0)
                next_lo(dve, self.n0 + 3)
                with dve.Fori(0, self.steps - 2) as r:
                    self.step_vector(dve, r + 1, self.n0 + 4, r)
                self.step_vector(dve, self.steps - 1, self.n0 + 4 * (self.steps - 1))
                self.turned_vector(dve, self.steps)
                n = self.n0 + 4 * self.steps
                for c in range(3):
                    next_lo(dve, n + c)
                residual_vector(dve, self.down_full, self.scale)
                next_lo(dve, n + 3)

            def sync(self, sp):
                n = self.n0
                for c in range(4):
                    load_chunk(sp, n + c)
                with sp.Fori(0, self.steps - 1) as r:
                    for c in range(4):
                        load_chunk(sp, n + 4 + c, r)
                for c in range(4):
                    load_chunk(sp, n + 4 * self.steps + c)

            def gpsimd(self, pool):
                pass

        class Unit:

            def __init__(self, kind, ks, width, chunks, to=None, gains=None, scale=1.0, rows=None, base=0):
                self.kind, self.ks, self.width, self.chunks = kind, ks, width, chunks
                self.to, self.gains, self.scale, self.rows, self.base = to, gains, scale, rows, base

        class Project:
            def __init__(self, name, section, units, stat_h, stat_l, norm=None, need=()):
                self.name, self.units, self.norm, self.need = name, units, norm, need
                self.stat_h, self.stat_l = stat_h, stat_l
                self.full = sem(name + "_full")
                self.evac = sem(name + "_evac")
                kinds = [unit.kind for unit in units]
                if "qk" in kinds:
                    self.sumsq = sem(name + "_sumsq")
                    self.root = sem(name + "_root")
                if {"qk", "dkv", "pe"} & set(kinds):
                    self.made = sem(name + "_made")
                self.turned = sem(name + "_turned")
                self.taken = sem(name + "_taken")
                self.lows = None
                if "latent" in kinds:
                    self.lows = sem(name + "_lows")
                n, made, turn, low = AT[section], 0, 0, 0
                for u, unit in enumerate(units):
                    unit.u, unit.n = u, []
                    k = unit.ks[0]
                    for tiles in unit.chunks:
                        unit.n.append((n, list(range(k, k + tiles))))
                        k, n = k + tiles, n + 1
                    ends[n - 1] = (self.full, NT * (u + 1), 0)
                    if unit.kind in ("qk", "dkv", "pe"):
                        unit.made, made = made, made + 1
                    if unit.kind != "v":
                        unit.turn, turn = turn, turn + 1
                    unit.low0 = NT * low
                    if unit.kind in ("latent", "dkv"):
                        low += 1
                self.turns, self.lowest = turn, low
                self.evac_ready = (self.evac, NT * len(units))
                self.turned_ready = (self.taken, NT * turn)
                self.split_ready = (self.lows, NT * low)

            def nat_of(self, unit, t):
                return nat[:, unit.u % 2, t]

            def multiply(self, pe, unit):
                for c, (n, ks) in enumerate(unit.n):
                    take_chunk(pe, n)
                    for t in range(NT):
                        if c == 0 and unit.u > 0:
                            pe.wait_ge(self.evac, NT * (unit.u - 1) + t + 1)
                        for j, k in enumerate(ks):
                            if self.norm and unit.u == 0 and t == 0 and k % 2 == 0:
                                xt_ready(pe, self.norm, k)
                            last = mm3(bankA[t][:, 0:unit.width], self.stat_h[:, k, t * P:(t + 1) * P],
                                       self.stat_l[:, k, t * P:(t + 1) * P], slot_of(n), j, unit.width,
                                       k == unit.ks[0], k == unit.ks[-1])
                        if k == unit.ks[-1]:
                            last.then_inc(self.full, 1)
                    used(last, n)

            def turn(self, pe, unit):
                for t in range(NT):
                    if unit.kind in ("qk", "dkv", "pe"):
                        pe.wait_ge(self.made, NT * unit.made + t + 1)
                    else:
                        pe.wait_ge(self.evac, NT * unit.u + t + 1)
                    if unit.turn > 0:
                        pe.wait_ge(self.taken, NT * (unit.turn - 1) + t + 1)
                    if unit.low0:
                        pe.wait_ge(self.lows, unit.low0 - NT + t + 1)
                    blocks = [self.nat_of(unit, t)[:, c * P:(c + 1) * P] for c in range(4)]
                    if unit.kind in ("idx", "latent"):
                        blocks = blocks[:3]
                    if unit.kind == "dkv":
                        blocks = blocks[:2] + [lg[:, t, 0:P]]
                    if unit.kind == "pe":
                        blocks = [lg[:, t, c * P:(c + 1) * P] for c in range(4)]
                    for c, b in enumerate(blocks):
                        last = nc.tensor.transpose(bankT[t][:, c * P:(c + 1) * P], b, ident)
                    last.then_inc(self.turned, 1)

            def tensor(self, pe):
                for s, value in self.need:
                    pe.wait_ge(s, value)
                before = None
                for unit in self.units:
                    self.multiply(pe, unit)
                    if before is not None:
                        self.turn(pe, before)
                    before = unit if unit.kind != "v" else None
                if before is not None:
                    self.turn(pe, before)

            def copy_out(self, act, unit):
                w = unit.width
                for t in range(NT):
                    act.wait_ge(self.full, NT * unit.u + t + 1)
                    row = unit.rows(t)
                    if unit.kind == "v":
                        nc.scalar.activation(v[:, t, unit.base:unit.base + w], bankA[t], ACT.Copy,
                                             scale=row).then_inc(self.evac, 1)
                    elif unit.kind == "idx":
                        to = self.nat_of(unit, t)
                        nc.scalar.activation(wi[:, t], bankA[t][:, 320:324], ACT.Copy, scale=row)
                        nc.scalar.activation(to[:, 320:384], bankA[t][:, 256:320], ACT.Copy, scale=row)
                        nc.scalar.activation(to[:, 0:320], bankA[t][:, 0:320], ACT.Copy,
                                             scale=row).then_inc(self.evac, 1)
                    else:
                        nc.scalar.activation(self.nat_of(unit, t)[:, 0:w], bankA[t][:, 0:w], ACT.Copy,
                                             scale=row).then_inc(self.evac, 1)

            def latent_root(self, act, unit):
                n = {"latent": QL, "dkv": KL}[unit.kind]
                c = 2 * len(NORMS) + (0 if unit.kind == "latent" else 2)
                act.wait_ge(self.evac, NT * (unit.u + 1))
                for t in range(NT):
                    own(act, act_own, nc.scalar.activation(
                        score[:, :, :].rearrange("p a n -> p (a n)")[:, 0:n], self.nat_of(unit, t)[:, 0:n], ACT.Square, scale=n ** -0.5,
                        accum_out=ms[:, c + t:c + t + 1]))
                own(act, act_own, root_scalar(act, ms[:, c:c + 2], rs[:, c:c + 2]))

            def head_root(self, act, unit):
                query = unit.scale != 1.0
                for t in range(NT):
                    act.wait_ge(self.sumsq, NT * unit.made + t + 1)
                    own(act, act_own, nc.scalar.activation(
                        hs[:, t, 8:16], hs[:, t, 0:8], ACT.Ln, bias=col[:, 1:2] if query else col[:, 0:1],
                        scale=1.0 if query else 1.0 / HD1))
                    nc.scalar.activation(hs[:, t, 0:8], hs[:, t, 8:16], ACT.Exp, scale=-0.5)\
                        .then_inc(self.root, 1)

            def take(self, act, unit):
                for t in range(NT):
                    act.wait_ge(self.turned, NT * unit.turn + t + 1)
                    bank, s = bankT[t].rearrange("p (c s) -> p c s", c=4), slice(t * P, (t + 1) * P)
                    if unit.kind in ("latent", "dkv"):
                        for c in range(unit.ks_out):
                            last = nc.scalar.activation(ot_h[:, unit.base + c, s], bank[:, c], ACT.Copy,
                                                        scale=gain[:, unit.gains + c:unit.gains + c + 1])
                        if unit.kind == "dkv":
                            last = nc.scalar.activation(pet[:, 4, s], bank[:, 2], ACT.Copy)
                    elif unit.kind == "idx":
                        last = nc.scalar.activation(pet[:, 0:3, s], bank[:, 0:3], ACT.Copy)
                    elif unit.kind == "qk":
                        last = nc.scalar.activation(unit.to[:, unit.base:unit.base + 4, s], bank, ACT.Copy,
                                                    scale=gain[:, unit.gains:unit.gains + 1])
                    else:
                        last = nc.scalar.activation(unit.to[:, unit.base:unit.base + 4, s], bank, ACT.Copy,
                                                    scale=unit.scale)
                    last.then_inc(self.taken, 1)

            def scalar(self, act):
                before = None
                for unit in self.units:
                    self.copy_out(act, unit)
                    for n, _ in unit.n:
                        next_hi(act, n)
                    if unit.kind in ("latent", "dkv"):
                        self.latent_root(act, unit)
                    if unit.kind == "qk":
                        self.head_root(act, unit)
                    if before is not None:
                        self.take(act, before)
                    before = unit if unit.kind != "v" else None
                if before is not None:
                    self.take(act, before)

            def squares(self, dve, unit):
                for t in range(NT):
                    dve.wait_ge(self.evac, NT * unit.u + t + 1)
                    rows = self.nat_of(unit, t)
                    own(dve, dve_own, nc.vector.tensor_tensor(lg[:, t], rows, rows, ALU.mult))
                    nc.vector.tensor_reduce(hs[:, t, 0:8], lg[:, t].rearrange("p (h d) -> p h d", d=HD1),
                                            AX.X, ALU.add).then_inc(self.sumsq, 1)

            def normalise(self, dve, unit):
                for t in range(NT):
                    dve.wait_ge(self.root, NT * unit.made + t + 1)
                    rows = self.nat_of(unit, t).rearrange("p (h d) -> p h d", d=HD1)
                    nc.vector.tensor_tensor(rows, rows, hs[:, t, 0:8].unsqueeze(2).to_broadcast([P, 8, HD1]),
                                            ALU.mult).then_inc(self.made, 1)

            def rotate(self, dve, unit):
                heads = 1 if unit.kind == "dkv" else H2
                at = KL if unit.kind == "dkv" else 0
                for t in range(NT):
                    dve.wait_ge(self.evac, NT * unit.u + t + 1)
                    if unit.made or t:
                        dve.wait_ge(self.made, NT * unit.made + t)
                    w = heads * HALF
                    x1, x2 = (self.nat_of(unit, t)[:, at + a * w:at + (a + 1) * w]
                              .rearrange("p (h d) -> p h d", h=heads) for a in range(2))
                    cos, sin = (trig[:, a, t].unsqueeze(1).to_broadcast([P, heads, HALF]) for a in range(2))
                    part = [pt[:, a // 2, (a % 2) * 256:(a % 2) * 256 + w].rearrange("p (h d) -> p h d", h=heads)
                            for a in range(4)]
                    nc.vector.tensor_tensor(part[0], x1, cos, ALU.mult)
                    nc.vector.tensor_tensor(part[1], x2, sin, ALU.mult)
                    nc.vector.tensor_tensor(part[2], x1, sin, ALU.mult)
                    own(dve, dve_own, nc.vector.tensor_tensor(part[3], x2, cos, ALU.mult))
                    copies = 2 if unit.kind == "dkv" else 1
                    for c in range(copies):
                        to = lg[:, t, c * ROPE:c * ROPE + heads * ROPE].rearrange("p (h d) -> p h d", h=heads)
                        nc.vector.tensor_tensor(to[:, :, 0:HALF], part[0], part[1], ALU.subtract)
                        last = nc.vector.tensor_tensor(to[:, :, HALF:ROPE], part[2], part[3], ALU.add)
                    last.then_inc(self.made, 1)

            def lower(self, dve, unit):
                for t in range(NT):
                    dve.wait_ge(self.taken, NT * unit.turn + t + 1)
                    s = slice(t * P, (t + 1) * P)
                    for c in range(unit.ks_out):
                        g = gain[:, unit.gains + c:unit.gains + c + 1]
                        last = nc.vector.scalar_tensor_tensor(
                            out=ot_l[:, unit.base + c, s], in0=bankT[t][:, c * P:(c + 1) * P], scalar=g,
                            in1=ot_h[:, unit.base + c, s].bitcast(F32), op0=ALU.mult, op1=ALU.subtract)
                    last.then_inc(self.lows, 1)

            def vector(self, dve):
                before = None
                for unit in self.units:
                    if unit.kind == "qk":
                        self.squares(dve, unit)
                    for n, _ in unit.n:
                        next_lo(dve, n)
                    if unit.kind == "qk":
                        self.normalise(dve, unit)
                    if unit.kind in ("dkv", "pe"):
                        self.rotate(dve, unit)
                    if before is not None and before.kind in ("latent", "dkv"):
                        self.lower(dve, before)
                    before = unit
                if before.kind in ("latent", "dkv"):
                    self.lower(dve, before)

            def sync(self, sp):
                for unit in self.units:
                    for n, _ in unit.n:
                        load_chunk(sp, n)

            def gpsimd(self, pool):
                pass

        class Finish:
            def __init__(self, fins, done, normalised):
                self.fins, self.done, self.normalised = fins, done, normalised
                self.f0 = sum(len(f) for f in all_fins)
                all_fins.append(fins)
                self.ready = (rows_lo, self.f0 + len(fins))

            def out_rows(self, dve, f):
                t, b, value, at, heads = self.fins[f]
                dve.wait_ge(self.done, value)
                same = [g for g in range(f) if self.fins[g][0] == t]
                if same:
                    dve.wait_ge(rows_ps, self.f0 + same[-1] + 1)
                if self.normalised:
                    own(dve, dve_own, nc.vector.reciprocal(rinv[:, at:at + heads], rsum[:, at:at + heads]))
                    nc.vector.tensor_tensor(
                        nat[:, 0, t].rearrange("p (h d) -> p h d", h=heads),
                        bankD[t][b].rearrange("p (h d) -> p h d", h=heads),
                        rinv[:, at:at + heads].unsqueeze(2).to_broadcast([P, heads, TW // heads]),
                        ALU.mult).then_inc(rows_made, 1)
                else:
                    nc.vector.tensor_copy(nat[:, 0, t], bankD[t][b]).then_inc(rows_made, 1)

            def turn(self, pe, f):
                t, b = self.fins[f][:2]
                pe.wait_ge(rows_made, self.f0 + f + 1)
                for c in range(4):
                    last = nc.tensor.transpose(bankD[t][b][:, c * P:(c + 1) * P],
                                               nat[:, 0, t, c * P:(c + 1) * P], ident)
                last.then_inc(rows_ps, 1)

            def take_hi(self, act, f):
                t, b = self.fins[f][:2]
                act.wait_ge(rows_ps, self.f0 + f + 1)
                nc.scalar.activation(ot_h[:, 4 * b:4 * b + 4, t * P:(t + 1) * P],
                                     bankD[t][b].rearrange("p (c s) -> p c s", c=4), ACT.Copy).then_inc(rows_hi, 1)

            def take_lo(self, dve, f):
                t, b = self.fins[f][:2]
                dve.wait_ge(rows_hi, self.f0 + f + 1)
                nc.vector.tensor_tensor(ot_l[:, 4 * b:4 * b + 4, t * P:(t + 1) * P],
                                        bankD[t][b].rearrange("p (c s) -> p c s", c=4),
                                        ot_h[:, 4 * b:4 * b + 4, t * P:(t + 1) * P].bitcast(F32),
                                        ALU.subtract).then_inc(rows_lo, 1)

        class Attend:
            def __init__(self, name, groups, fins, need, select=None):
                self.groups, self.need, self.select = groups, need, select
                self.scores = sem(name + "_scores")
                self.logits = sem(name + "_logits")
                self.probs = sem(name + "_probs")
                self.p_ps = sem(name + "_p_ps")
                self.p_sb = sem(name + "_p_sb")
                self.summed = sem(name + "_summed")
                self.fin = Finish([(t, b, g + 1, at, hh) for t, b, g, at, hh in fins], self.summed, True)
                self.last = [g for _, _, g, _, _ in fins]
                self.ready = self.fin.ready

            def score(self, pe, g):
                if g >= 2:
                    pe.wait_ge(self.logits, g - 1)
                for head in self.groups[g]:
                    for i, (q, k) in enumerate(head["qk"]):
                        last = nc.tensor.matmul(bankA[g % 2][:, head["at"]:head["at"] + head["width"]], q, k,
                                                start=i == 0, stop=i == len(head["qk"]) - 1)
                last.then_inc(self.scores, 1)

            def turn(self, pe, g):
                pe.wait_ge(self.probs, g + 1)
                if g >= 2:
                    pe.wait_ge(self.p_sb, g - 1)
                for c in range(4):
                    last = nc.tensor.transpose(bankT[g % 2][:, c * P:(c + 1) * P],
                                               lg[:, g % 2, c * P:(c + 1) * P], ident)
                last.then_inc(self.p_ps, 1)

            def value(self, pe, g):
                pe.wait_ge(self.p_sb, g + 1)
                for head in self.groups[g]:
                    for i, val in enumerate(head["v"]):
                        c = head["at"] + i * P
                        last = nc.tensor.matmul(head["out"], pt[:, g % 2, c:c + P], val,
                                                start=i == 0, stop=i == len(head["v"]) - 1)
                last.then_inc(self.summed, 1)

            def tensor(self, pe):
                for s, value in self.need:
                    pe.wait_ge(s, value)
                if self.select:
                    self.select.tensor(pe)
                self.score(pe, 0)
                for g in range(len(self.groups) + 3):
                    if g + 1 < len(self.groups):
                        self.score(pe, g + 1)
                    if g < len(self.groups):
                        self.turn(pe, g)
                    if 1 <= g <= len(self.groups):
                        self.value(pe, g - 1)
                    for f, last in enumerate(self.last):
                        if last == g - 2:
                            self.fin.turn(pe, f)

            def scalar(self, act):
                nc.scalar.preload_act_table_set("natural_log_exp_and_others")
                if self.select:
                    self.select.scalar(act)
                for g in range(len(self.groups) + 4):
                    if g < len(self.groups):
                        act.wait_ge(self.logits, g + 1)
                        for head in self.groups[g]:
                            rows = lg[:, g % 2, head["at"]:head["at"] + head["width"]]
                            c = head["col"]
                            last = nc.scalar.activation(rows, rows, ACT.Exp, bias=nmax[:, c:c + 1], scale=-1.0,
                                                        accum_out=rsum[:, c:c + 1])
                        last.then_inc(self.probs, 1)
                    for f, last in enumerate(self.last):
                        if last == g - 3:
                            self.fin.take_hi(act, f)

            def vector(self, dve):
                if self.select:
                    self.select.vector(dve)
                for g in range(len(self.groups) + 4):
                    if g < len(self.groups):
                        if self.select:
                            self.select.before_logits(dve, g)
                        dve.wait_ge(self.scores, g + 1)
                        if g >= 2:
                            dve.wait_ge(self.p_ps, g - 1)
                        for head in self.groups[g]:
                            c, a, w = head["col"], head["at"], head["width"]
                            last = nc.vector.tensor_tensor_reduce(
                                out=lg[:, g % 2, a:a + w], in0=bankA[g % 2][:, a:a + w], in1=head["bias"],
                                scale=-1.0, scalar=3e38, op0=ALU.add, op1=ALU.min,
                                accum_out=nmax[:, c:c + 1])
                        last.then_inc(self.logits, 1)
                    if 1 <= g <= len(self.groups):
                        dve.wait_ge(self.p_ps, g)
                        if g >= 3:
                            dve.wait_ge(self.summed, g - 2)
                        nc.vector.tensor_copy(pt[:, (g - 1) % 2], bankT[(g - 1) % 2]).then_inc(self.p_sb, 1)
                    for f, last in enumerate(self.last):
                        if last == g - 2:
                            self.fin.out_rows(dve, f)
                        if last == g - 3:
                            self.fin.take_lo(dve, f)
                    if self.select:
                        self.select.after_group(dve, g)

            def sync(self, sp):
                pass

            def gpsimd(self, pool):
                if self.select:
                    self.select.gpsimd(pool, self)

        class Select:
            ROUNDS = TOPK // 8

            def __init__(self, moba_groups):
                self.moba_groups = moba_groups
                self.dots = sem("idx_dots")
                self.relus = sem("idx_relus")
                self.summed = sem("idx_summed")
                self.selected = sem("idx_selected")
                self.biased = sem("idx_biased")
                self.passes = [(0, 0, [0, 2], P), (0, 1, [1, 3], P), (1, 0, [0, 2], S), (1, 1, [1, 3], S)]

            def tensor(self, pe):
                for i, (t, bank, heads, keys) in enumerate(self.passes):
                    if i >= 2:
                        pe.wait_ge(self.relus, i - 1)
                    for j, head in enumerate(heads):
                        half = slice(64 * (head % 2), 64 * (head % 2) + 64)
                        last = nc.tensor.matmul(bankD[bank][0][:, j * keys:(j + 1) * keys],
                                                pet[half, head // 2, t * P:(t + 1) * P],
                                                pet[half, 2, 0:keys], start=True, stop=True)
                    last.then_inc(self.dots, 1)

            def scalar(self, act):
                for i, (t, bank, heads, keys) in enumerate(self.passes):
                    act.wait_ge(self.dots, i + 1)
                    if i >= 2:
                        act.wait_ge(self.summed, i - 1)
                    nc.scalar.activation(pt[:, i % 2, 0:2 * keys], bankD[bank][0][:, 0:2 * keys], ACT.Relu,
                                         scale=0.125 * 0.5)\
                        .then_inc(self.relus, 1)

            def vector(self, dve):
                for i, (t, bank, heads, keys) in enumerate(self.passes):
                    dve.wait_ge(self.relus, i + 1)
                    for j, head in enumerate(heads):
                        to = score[:, t, 0:keys]
                        before = const[:, C_CAUSAL + S - keys:C_CAUSAL + S] if head == 0 else to
                        ins = nc.vector.scalar_tensor_tensor(
                            out=to, in0=pt[:, i % 2, j * keys:(j + 1) * keys],
                            scalar=wi[:, t, head:head + 1], in1=before, op0=ALU.mult, op1=ALU.add)
                        if j < len(heads) - 1:
                            own(dve, dve_own, ins)
                    ins.then_inc(self.summed, 1)
                    dve.wait_ge(self.summed, i + 1)

            def take_eight(self, dve):
                for t in range(NT):
                    last = nc.vector.max(top8[:, t], score[:, t, 0:(t + 1) * P])
                own(dve, dve_own, last)
                for t in range(NT):
                    rows = score[:, t, 0:(t + 1) * P]
                    last = nc.vector.match_replace(out=rows, in_to_replace=top8[:, t], in_values=rows,
                                                   imm_value=TAKEN)
                own(dve, dve_own, last)

            def after_group(self, dve, g):
                for r in range(2 * g, 2 * g + 2):
                    if r < self.ROUNDS:
                        self.take_eight(dve)
                if 2 * g + 2 == self.ROUNDS:
                    for t in range(NT):
                        rows = score[:, t, 0:(t + 1) * P]
                        nc.vector.tensor_scalar(rows, rows, -2e38, NEG, ALU.is_gt, ALU.mult)\
                            .then_inc(self.selected, 1)

            def before_logits(self, dve, g):
                if g >= self.moba_groups:
                    dve.wait_ge(self.biased, g - self.moba_groups + 1)

            def gpsimd(self, pool, attend):
                pool.wait_ge(self.selected, NT)
                for g in range(self.moba_groups, len(attend.groups)):
                    if g >= self.moba_groups + 2:
                        pool.wait_ge(attend.logits, g - 1)
                    first = attend.groups[g][0]
                    keys, n, t = first["width"], len(attend.groups[g]), first["tile"]
                    nc.gpsimd.tensor_tensor(
                        nat[:, 1, g % 2].rearrange("p (h k) -> p h k", h=n),
                        rel[:, first["head"]:first["head"] + 2 * n - 1:2, S - keys:S],
                        score[:, t, 0:keys].unsqueeze(1).to_broadcast([P, n, keys]),
                        ALU.add).then_inc(self.biased, 1)

        class Stick:
            def __init__(self, name, need):
                self.need = need
                self.scores = sem(name + "_scores")
                self.masked = sem(name + "_masked")
                self.logs = sem(name + "_logs")
                self.soft = sem(name + "_soft")
                self.sums = sem(name + "_sums")
                self.expo = sem(name + "_expo")
                self.weights = sem(name + "_weights")
                self.summed = sem(name + "_summed")
                self.fin = Finish([(t, b, 4 * b + 4, 0, 4) for b in range(2) for t in range(NT)],
                                  self.summed, False)
                self.ready = self.fin.ready

            def score(self, pe, g):
                if g >= 2:
                    pe.wait_ge(self.masked, g - 1)
                nc.tensor.matmul(bankA[g % 2][:, 0:S], kt[:, g, 0:P], qt[:, g], start=True, stop=True)
                nc.tensor.matmul(bankA[g % 2][:, S:S + P], kt[:, g, P:S], qt[:, g, P:S],
                                 start=True, stop=True).then_inc(self.scores, 1)

            def suffix(self, pe, g):
                pe.wait_ge(self.soft, g + 1)
                if g >= 2:
                    pe.wait_ge(self.expo, g - 1)
                suffix, ones = const[:, C_SUFFIX:C_SUFFIX + P], const[:, C_ONES:C_ONES + P]
                bank = bankT[g % 2]
                nc.tensor.matmul(bank[:, 0:S], suffix, pt[:, g % 2, 0:S], start=True, stop=False)
                nc.tensor.matmul(bank[:, P:S], ones, pt[:, g % 2, S:S + P], start=False, stop=True)
                nc.tensor.matmul(bank[:, S:S + P], suffix, pt[:, g % 2, S:S + P],
                                 start=True, stop=True).then_inc(self.sums, 1)

            def value(self, pe, g):
                pe.wait_ge(self.weights, g + 1)
                a, c = nat[:, 1, g % 2], slice(HD2 * (g % 4), HD2 * (g % 4) + HD2)
                vals = [v[:, k, HD2 * g:HD2 * (g + 1)] for k in range(2)]
                nc.tensor.matmul(bankD[0][g // 4][:, c], a[:, 0:P], vals[0], start=True, stop=True)
                nc.tensor.matmul(bankD[1][g // 4][:, c], a[:, P:S], vals[0], start=True, stop=False)
                nc.tensor.matmul(bankD[1][g // 4][:, c], a[:, S:S + P], vals[1], start=False,
                                 stop=True).then_inc(self.summed, 1)

            def tensor(self, pe):
                for s, value in self.need:
                    pe.wait_ge(s, value)
                self.score(pe, 0)
                for g in range(H2 + 3):
                    if g + 1 < H2:
                        self.score(pe, g + 1)
                    if g < H2:
                        self.suffix(pe, g)
                    if 1 <= g <= H2:
                        self.value(pe, g - 1)
                    for f in range(4):
                        if self.fin.fins[f][2] == g - 1:
                            self.fin.turn(pe, f)

            def scalar(self, act):
                nc.scalar.preload_act_table_set("natural_log_exp_and_others")
                for g in range(H2 + 4):
                    if g < H2:
                        e = pt[:, g % 2, 0:S + P]
                        act.wait_ge(self.masked, g + 1)
                        if g >= 2:
                            act.wait_ge(self.sums, g - 1)
                        own(act, act_own, nc.scalar.activation(e, lg[:, g % 2, 0:S + P], ACT.Abs))
                        own(act, act_own, nc.scalar.activation(e, e, ACT.Exp, scale=-1.0))
                        nc.scalar.activation(e, e, ACT.Ln, bias=col[:, 2:3]).then_inc(self.logs, 1)
                    if 1 <= g <= H2:
                        b = (g - 1) % 2
                        act.wait_ge(self.expo, g)
                        if g >= 3:
                            act.wait_ge(self.summed, g - 2)
                        nc.scalar.activation(nat[:, 1, b, 0:S + P], lg[:, b, 0:S + P], ACT.Exp)\
                            .then_inc(self.weights, 1)
                    for f in range(4):
                        if self.fin.fins[f][2] == g - 2:
                            self.fin.take_hi(act, f)

            def vector(self, dve):
                for g in range(H2 + 4):
                    if g < H2:
                        dve.wait_ge(self.scores, g + 1)
                        if g >= 2:
                            dve.wait_ge(self.weights, g - 1)
                        nc.vector.tensor_tensor(lg[:, g % 2, 0:S + P], bankA[g % 2][:, 0:S + P],
                                                const[:, C_STRICT:C_STRICT + S + P], ALU.add)\
                            .then_inc(self.masked, 1)
                    if 1 <= g <= H2:
                        b = (g - 1) % 2
                        dve.wait_ge(self.sums, g)
                        nc.vector.tensor_tensor(lg[:, b, 0:S + P], lg[:, b, 0:S + P], bankT[b][:, 0:S + P],
                                                ALU.add).then_inc(self.expo, 1)
                    if g < H2:
                        dve.wait_ge(self.logs, g + 1)
                        nc.vector.scalar_tensor_tensor(
                            out=pt[:, g % 2, 0:S + P], in0=lg[:, g % 2, 0:S + P], scalar=0.0,
                            in1=pt[:, g % 2, 0:S + P], op0=ALU.max, op1=ALU.add).then_inc(self.soft, 1)
                    for f in range(4):
                        if self.fin.fins[f][2] == g - 1:
                            self.fin.out_rows(dve, f)
                        if self.fin.fins[f][2] == g - 2:
                            self.fin.take_lo(dve, f)

            def sync(self, sp):
                pass

            def gpsimd(self, pool):
                pass

        class OutProject:
            def __init__(self, name, section, ks, stat_h, stat_l, need, residual=True):
                self.name, self.n0, self.ks, self.need = name, AT[section], ks, need
                self.stat_h, self.stat_l, self.residual = stat_h, stat_l, residual
                self.full0 = NB * NT * len(out_projects)
                out_projects.append(name)
                self.chunks = len(ks) // 2
                ends[self.n0 + self.chunks - 1] = (out_full, self.full0 + NB * NT, 0)

            def tensor(self, pe):
                for s, value in self.need:
                    pe.wait_ge(s, value)
                for c in range(self.chunks):
                    take_chunk(pe, self.n0 + c)
                    for j in range(2):
                        k = self.ks[2 * c + j]
                        for block in range(NB):
                            for t in range(NT):
                                last = mm3(bankD[t][block], self.stat_h[:, k, t * P:(t + 1) * P],
                                           self.stat_l[:, k, t * P:(t + 1) * P], slot_of(self.n0 + c),
                                           2 * j + block, TW, k == self.ks[0], k == self.ks[-1])
                                if k == self.ks[-1]:
                                    last.then_inc(out_full, 1)
                    used(last, self.n0 + c)

            def scalar(self, act):
                for c in range(self.chunks):
                    next_hi(act, self.n0 + c)

            def vector(self, dve):
                for c in range(self.chunks - 1):
                    next_lo(dve, self.n0 + c)
                if self.residual:
                    residual_vector(dve, out_full, 1.0, self.full0)
                next_lo(dve, self.n0 + self.chunks - 1)

            def sync(self, sp):
                for c in range(self.chunks):
                    load_chunk(sp, self.n0 + c)

            def gpsimd(self, pool):
                pass

        class Mixture:
            def __init__(self, attend):
                self.attend = attend
                self.full = sem("gate_full")
                self.raw = sem("gate_raw")
                self.gate = sem("gate_sigmoid")
                self.mixed = sem("gate_mixed")
                self.bias_in = sem("gate_bias_in")
                self.ps = sem("mix_ps")
                self.hi = sem("mix_hi")
                self.lo = sem("mix_lo")
                self.branch = []
                for b, section in enumerate(("br_a", "br_b")):
                    need = [attend.ready] if b == 0 else [(self.mixed, NB * NT)]
                    self.branch.append(OutProject(section, section, list(range(4 * b, 4 * b + 4)),
                                                  ot_h, ot_l, need, residual=False))
                for u in range(4):
                    ends[self.chunk(u) + 1] = (self.full, NT * (u + 1), 0)
                self.ready = (self.lo, 4)

            def chunk(self, u):
                return AT["gate_a" if u < 2 else "gate_b"] + 2 * (u % 2)

            def tensor(self, pe):
                for u in range(4):
                    if u % 2 == 0:
                        self.branch[u // 2].tensor(pe)
                    for c in range(2):
                        take_chunk(pe, self.chunk(u) + c)
                        for t in range(NT):
                            if c == 0 and u > 0:
                                pe.wait_ge(self.raw, NT * (u - 1) + t + 1)
                            for j in range(4):
                                k = 4 * c + j
                                last = mm3(bankA[t], xt_h[:, k, t * P:(t + 1) * P],
                                           xt_l[:, k, t * P:(t + 1) * P], slot_of(self.chunk(u) + c), j, TW,
                                           k == 0, k == KC - 1)
                            if c == 1:
                                last.then_inc(self.full, 1)
                        used(last, self.chunk(u) + c)
                pe.wait_ge(self.mixed, 4 * NT)
                for pair, bank in enumerate(bankT + bankA):
                    for j in range(2):
                        for t in range(NT):
                            k = 2 * pair + j
                            last = nc.tensor.transpose(bank[:, j * S + t * P:j * S + (t + 1) * P],
                                                       v[:, t, k * P:(k + 1) * P], ident)
                    last.then_inc(self.ps, 1)

            def scalar(self, act):
                nc.scalar.preload_act_table(ACT.Sigmoid)
                for u in range(4):
                    if u % 2 == 0:
                        self.branch[u // 2].scalar(act)
                    for t in range(NT):
                        act.wait_ge(self.raw, NT * u + t + 1)
                        nc.scalar.activation(lg[:, t], lg[:, t], ACT.Sigmoid).then_inc(self.gate, 1)
                    for c in range(2):
                        next_hi(act, self.chunk(u) + c)
                for pair, bank in enumerate(bankT + bankA):
                    act.wait_ge(self.ps, pair + 1)
                    nc.scalar.activation(xt_h[:, 2 * pair:2 * pair + 2],
                                         bank.rearrange("p (k s) -> p k s", k=2), ACT.Copy).then_inc(self.hi, 1)

            def vector(self, dve):
                dve.wait_ge(self.bias_in, 16)
                for u in range(4):
                    b, block = u // 2, u % 2
                    if block == 0:
                        self.branch[b].vector(dve)
                    for t in range(NT):
                        if u > 0:
                            dve.wait_ge(self.mixed, NT * (u - 1) + t + 1)
                        dve.wait_ge(self.full, NT * u + t + 1)
                        nc.vector.scalar_tensor_tensor(out=lg[:, t], in0=bankA[t], scalar=rms("mix", t),
                                                       in1=nat[:, b, block], op0=ALU.mult, op1=ALU.add)\
                            .then_inc(self.raw, 1)
                    for c in range(2):
                        next_lo(dve, self.chunk(u) + c)
                    for t in range(NT):
                        dve.wait_ge(self.gate, NT * u + t + 1)
                        dve.wait_ge(out_full, self.branch[b].full0 + NT * block + t + 1)
                        to = v[:, t, block * TW:(block + 1) * TW]
                        if b == 0:
                            nc.vector.tensor_tensor(to, lg[:, t], bankD[t][block], ALU.mult)\
                                .then_inc(self.mixed, 1)
                        else:
                            own(dve, dve_own, nc.vector.tensor_tensor(lg[:, t], lg[:, t], bankD[t][block],
                                                                      ALU.mult))
                            nc.vector.tensor_tensor(to, to, lg[:, t], ALU.add).then_inc(self.mixed, 1)
                for pair, bank in enumerate(bankT + bankA):
                    dve.wait_ge(self.hi, pair + 1)
                    nc.vector.tensor_tensor(xt_l[:, 2 * pair:2 * pair + 2],
                                            bank.rearrange("p (k s) -> p k s", k=2),
                                            xt_h[:, 2 * pair:2 * pair + 2].bitcast(F32),
                                            ALU.subtract).then_inc(self.lo, 1)

            def sync(self, sp):
                for u in range(4):
                    if u % 2 == 0:
                        self.branch[u // 2].sync(sp)
                    for c in range(2):
                        load_chunk(sp, self.chunk(u) + c)

            def gpsimd(self, pool):
                pool.wait_ge(rows_ps, self.attend.fin.f0 + 4)
                pool.dma_start(nat[:, :, :, :].rearrange("p a b n -> p (a b n)"),
                               dram["b_gate"].partition_broadcast(P)).then_inc(self.bias_in, 16)

        class Norm:

            def __init__(self, name, free=None, banks=None):
                self.name, self.free, self.banks = name, free, banks

            def tensor(self, pe):
                if self.banks:
                    pe.wait_ge(*self.banks)
                norm_tensor(pe, self.name)

            def scalar(self, act):
                norm_scalar(act, self.name)
                rms_scalar(act, self.name)
                act.wait_ge(rs_ready, NORM[self.name] + 1)

            def vector(self, dve):
                norm_vector(dve, self.name)
                dve.wait_ge(rs_ready, NORM[self.name] + 1)

            def sync(self, sp):
                pass

            def gpsimd(self, pool):
                if self.free:
                    pool.wait_ge(*self.free)
                    pool.dma_start(v[:], dram["mem"]).then_inc(mem_in, 16)

        class Tables:
            TWO_PI = 6.283185307179586
            C1 = 6.28125
            C2 = float(np.float32(TWO_PI - C1))
            C3 = TWO_PI - C1 - C2

            def __init__(self):
                self.in_ = sem("tables_in")
                self.neg = sem("tables_neg")
                self.ps = sem("tables_ps")
                self.sb = sem("tables_sb")
                self.out = sem("tables_out")
                self.rel_in = sem("rel_in")
                self.angle = sem("tables_angle")
                self.trig = sem("tables_trig")
                self.scratch = nc.dram_tensor("bias_by_distance", (16, P, RELW + 1), F32, kind="Internal").ap()

            def gpsimd(self, pool):
                pool.dma_start(lg[0:NBUCK + 1, 0, 0:RELW + 1], dram["consts"][0:NBUCK + 1, C_BUCK:NCONST])\
                    .then_inc(self.in_, 16)
                pool.dma_start(pt[0:NBUCK, 0, 0:16], dram["rel_bias"]).then_inc(self.in_, 16)
                pool.dma_start(pos[:, 0:NT].bitcast(I32), dram["positions"]).then_inc(self.in_, 16)
                pool.wait_ge(self.sb, 1)
                pool.dma_start(self.scratch, pt[0:16, 1, 0:RELW + 1].unsqueeze(1).to_broadcast(
                    [16, P, RELW + 1])).then_inc(self.out, 16)
                pool.wait_ge(self.out, 16)
                spread = bass.AP(tensor=self.scratch.tensor, offset=P - 1,
                                 ap=[[RELW, P], [P * (RELW + 1), 16], [1, S]])
                pool.dma_start(rel[:], spread).then_inc(self.rel_in, 16)

            def tensor(self, pe):
                pe.wait_ge(self.in_, 48)
                pe.wait_ge(self.neg, 1)
                nc.tensor.matmul(bankD[1][1][0:16, 0:RELW + 1], pt[0:NBUCK + 1, 0, 0:16],
                                 lg[0:NBUCK + 1, 0, 0:RELW + 1], start=True, stop=True).then_inc(self.ps, 1)

            def scalar(self, act):
                act.wait_ge(self.ps, 1)
                nc.scalar.activation(pt[0:16, 1, 0:RELW + 1], bankD[1][1][0:16, 0:RELW + 1], ACT.Copy)\
                    .then_inc(self.sb, 1)
                act.wait_ge(self.angle, 1)
                nc.scalar.activation(trig[:], nat[:, 0, 0, 0:4 * HALF].rearrange(
                    "p (a t d) -> p a t d", a=2, t=NT), ACT.Sin).then_inc(self.trig, 1)

            def vector(self, dve):
                nc.vector.memset(pt[NBUCK:NBUCK + 1, 0, 0:16], NEG).then_inc(self.neg, 1)
                dve.wait_ge(self.in_, 48)
                dve.wait_ge(consts_in, 32)
                w = 2 * NT * HALF
                angle, turns, red = nat[:, 0, 1, 0:w], nat[:, 1, 0, 0:w], nat[:, 0, 0, 0:w]
                own(dve, dve_own, nc.vector.tensor_copy(pos[:, 2:4], pos[:, 0:NT].bitcast(I32)))
                for t in range(NT):
                    for a in range(2):
                        last = nc.vector.tensor_scalar(
                            angle[:, (2 * a + t) * HALF:(2 * a + t + 1) * HALF],
                            const[:, C_FREQ:C_FREQ + HALF], pos[:, 2 + t:3 + t], None, ALU.mult)
                own(dve, dve_own, last)
                for a, quarter in enumerate((0.25, 0.0)):
                    part = slice(a * w // 2, (a + 1) * w // 2)
                    last = nc.vector.tensor_scalar(turns[:, part], angle[:, part], 1.0 / self.TWO_PI, quarter,
                                                   ALU.mult, ALU.add)
                own(dve, dve_own, last)
                whole = nat[:, 1, 1, 0:w].bitcast(I32)
                own(dve, dve_own, nc.vector.tensor_copy(whole, turns))
                own(dve, dve_own, nc.vector.tensor_copy(turns, whole))
                step = angle
                for c in (self.C1, self.C2, self.C3):
                    own(dve, dve_own, nc.vector.scalar_tensor_tensor(out=red, in0=turns, scalar=-c, in1=step,
                                                                     op0=ALU.mult, op1=ALU.add))
                    step = red
                own(dve, dve_own, nc.vector.tensor_scalar(red[:, 0:w // 2], red[:, 0:w // 2], self.TWO_PI / 4, None,
                                                          ALU.add))
                nc.vector.tensor_scalar(red, red, 3.1415925, -3.1415925, ALU.min, ALU.max)\
                    .then_inc(self.angle, 1)

            def sync(self, sp):
                pass

        class Final:

            def __init__(self):
                self.gain_in = sem("final_gain_in")
                self.made = sem("final_rows")
                self.stored = sem("final_stored")

            def gpsimd(self, pool):
                pool.wait_ge(h_ready, 32)
                pool.dma_start(qt[:, 0:4].rearrange("p k s -> p (k s)"),
                               dram["norm_final"].partition_broadcast(P)).then_inc(self.gain_in, 16)

            def tensor(self, pe):
                pass

            def scalar(self, act):
                rms_scalar(act, "final")

            def vector(self, dve):
                dve.wait_ge(self.gain_in, 16)
                dve.wait_ge(rs_ready, len(NORMS))
                for t in range(NT):
                    nc.vector.scalar_tensor_tensor(out=v[:, t], in0=h[:, t], scalar=rms("final", t),
                                                   in1=qt[:, 0:4].rearrange("p k s -> p (k s)"),
                                                   op0=ALU.mult, op1=ALU.mult).then_inc(self.made, 1)

            def sync(self, sp):
                rows = out.rearrange("(t p) d -> p t d", p=P)
                for t in range(NT):
                    sp.wait_ge(self.made, t + 1)
                    sp.dma_start(rows[:, t], v[:, t]).then_inc(self.stored, 16)
                sp.wait_ge(self.stored, 16 * NT)

        def row(name):
            return lambda t: rms(name, t)

        def latent_row(i):
            c = 2 * len(NORMS) + 2 * i
            return lambda t: rs[:, c + t:c + t + 1]

        def same_half(per):
            return [list(range(h0 + odd, h0 + 2 * per, 2)) for h0 in range(0, 8, 2 * per) for odd in range(2)]

        def moba_dsa():
            groups, fins = [], []
            for b in (1, 0):
                for t in range(NT):
                    keys, per = (t + 1) * P, 4 // (t + 1)
                    for heads in same_half(per):
                        group = []
                        for i, hd in enumerate(heads):
                            half = slice(64 * (hd % 2), 64 * (hd % 2) + 64)
                            k4 = 4 * b + hd // 2
                            bias = rel[:, 8 * b + hd, S - keys:S] if b else \
                                nat[:, 1, len(groups) % 2, i * keys:(i + 1) * keys]
                            group.append(dict(
                                at=i * keys, width=keys, tile=t, head=8 * b + hd, bias=bias,
                                qk=[(qt[half, k4, t * P:(t + 1) * P], kt[half, k4, 0:keys])],
                                v=[v[:, j, TW * b + HD1 * hd:TW * b + HD1 * (hd + 1)] for j in range(t + 1)],
                                out=bankD[t][b][:, HD1 * hd:HD1 * (hd + 1)], col=16 * b + 8 * t + hd))
                        groups.append(group)
                    fins.append((t, b, len(groups) - 1, 16 * b + 8 * t, H1))
            return groups, fins, len(groups) // 2

        def mla_groups():
            groups, fins = [], []
            for t in range(NT):
                keys, per = (t + 1) * P, 4 // (t + 1)
                for heads in same_half(per):
                    group = []
                    for i, hd in enumerate(heads):
                        half, s = slice(64 * (hd % 2), 64 * (hd % 2) + 64), slice(t * P, (t + 1) * P)
                        group.append(dict(
                            at=i * keys, width=keys, tile=t, head=hd,
                            bias=const[:, C_CAUSAL + S - keys:C_CAUSAL + S],
                            qk=[(qt[:, hd, s], kt[:, hd, 0:keys]),
                                (pet[half, hd // 2, s], pet[half, 4, 0:keys])],
                            v=[v[:, j, HD2 * hd:HD2 * (hd + 1)] for j in range(t + 1)],
                            out=bankD[t][hd // 4][:, HD2 * (hd % 4):HD2 * (hd % 4) + HD2], col=8 * t + hd))
                    groups.append(group)
                    if heads[-1] == 7:
                        fins += [(t, b, len(groups) - 1, 8 * t + 4 * b, 4) for b in ((1,) if t else (0, 1))]
                    elif heads[-1] == 3:
                        fins.append((t, 0, len(groups) - 1, 8 * t, 4))
            return groups, fins

        def mem_groups():
            groups, fins = [], []
            for t in range(NT):
                for h0 in (0, 2):
                    groups.append([dict(
                        at=i * S, width=S, bias=const[:, C_CAUSAL:C_CAUSAL + 1].to_broadcast([P, S]),
                        qk=[(qt[:, hd, t * P:(t + 1) * P], kt[:, hd])],
                        v=[v[:, j, HD2 * hd:HD2 * (hd + 1)] for j in range(2)],
                        out=bankD[t][0][:, HD2 * hd:HD2 * (hd + 1)], col=4 * t + hd)
                        for i, hd in enumerate((h0, h0 + 1))])
                fins.append((t, 0, len(groups) - 1, 4 * t, NXH))
            return groups, fins

        all8 = list(range(KC))

        def unit(kind, width=TW, chunks=(4, 4), **kw):
            return Unit(kind, list(range(sum(chunks))), width, chunks, **kw)

        tables = Tables()
        ffn1 = Ffn("ffn1", 11, 2, True, 0.5)

        mix = row("mix")
        mix_units = [unit("idx", 324, (2, 2, 2, 2), rows=mix)]
        for to, base, g, sc in ((qt, 4, QG_B, 0.125), (kt, 4, KG_B, 1.0), (qt, 0, QG_A, 0.125), (kt, 0, KG_A, 1.0)):
            mix_units.append(unit("qk", rows=mix, to=to, base=base, gains=g, scale=sc))
        mix_units += [unit("v", rows=mix, base=TW), unit("v", rows=mix, base=0)]
        mix_in = Project("mix_in", "idx", mix_units, xt_h, xt_l, norm="mix")
        groups, fins, n_moba = moba_dsa()
        mix_attend = Attend("mix", groups, fins, [mix_in.turned_ready, mix_in.evac_ready, (tables.rel_in, 16)],
                            Select(n_moba))
        mixture = Mixture(mix_attend)
        mix_out = OutProject("mix_out", "w_out", all8, xt_h, xt_l, [mixture.ready])

        ffn2 = Ffn("ffn2", 11, 2, True, 0.5)

        latent_units = [unit("latent", QL, rows=row("mla"), gains=QG_L, base=0),
                        unit("dkv", KL + ROPE, rows=row("mla"), gains=KG_L, base=3)]
        latent_units[0].ks_out, latent_units[1].ks_out = 3, 2
        mla_down = Project("mla_down", "dq", latent_units, xt_h, xt_l, norm="mla")
        qrow, krow = latent_row(0), latent_row(1)
        up_units = [unit("q", chunks=(3,), rows=qrow, to=qt, base=4 * i, scale=MLA_SCALE) for i in range(2)]
        up_units.append(unit("pe", chunks=(3,), rows=qrow, to=pet, scale=MLA_SCALE))
        for kind, base in (("q", 0), ("q", 4), ("v", 0), ("v", TW)):
            up_units.append(Unit(kind, [3, 4], TW, (2,), rows=krow, to=kt, base=base))
        mla_up = Project("mla_up", "uq", up_units, ot_h, ot_l, need=[mla_down.split_ready, mla_down.turned_ready])
        groups, fins = mla_groups()
        mla_attend = Attend("mla", groups, fins, [mla_up.turned_ready, mla_up.evac_ready])
        mla_out = OutProject("mla_out", "mla_o", all8, ot_h, ot_l, [mla_attend.ready])

        def memory(i, free):
            r = row(f"mem{i}")
            kv = Project(f"mem_kv{i}", f"xkv{i}", [unit("q", rows=r, to=kt), unit("v", rows=r)], ot_h, ot_l,
                         need=[(xt_lo, 4 * NORM[f"mem{i}"] + 4)])
            q = Project(f"mem_q{i}", f"xq{i}", [unit("q", rows=row(f"cross{i}"), to=qt, scale=MEM_SCALE)],
                        xt_h, xt_l, norm=f"cross{i}")
            attend = Attend(f"mem{i}", *mem_groups(), [kv.turned_ready, kv.evac_ready, q.turned_ready])
            return [Norm(f"mem{i}", free), kv, Norm(f"cross{i}", banks=kv.turned_ready), q, attend,
                    OutProject(f"mem_out{i}", f"xo{i}", all8[:4], ot_h, ot_l, [attend.ready]),
                    Ffn(f"mlp{i}", 8, 4, False, 1.0)]

        memory0 = memory(0, (mla_attend.summed, len(mla_attend.groups)))
        sb_row = row("sb")
        sb_units = [unit("q", rows=sb_row, to=qt, base=4 * i, scale=SB_SCALE) for i in range(2)]
        sb_units += [unit("q", rows=sb_row, to=kt, base=4 * i) for i in range(2)]
        sb_units += [unit("v", rows=sb_row, base=TW * i) for i in range(2)]
        sb_in = Project("sb_in", "sb_qkv", sb_units, xt_h, xt_l, norm="sb")
        stick = Stick("sb", [sb_in.turned_ready, sb_in.evac_ready])
        sb_out = OutProject("sb_out", "sb_o", all8, ot_h, ot_l, [stick.ready])

        phases = [ffn1, Norm("mix"), mix_in, mix_attend, mixture, mix_out, ffn2,
                  Norm("mla"), mla_down, mla_up, mla_attend, mla_out]
        phases += memory0
        phases += [Norm("sb"), sb_in, stick, sb_out]
        phases += memory(1, (stick.summed, H2))
        phases.append(Final())

        block = ctx.enter_context(nc.Block())

        @block.sync
        def _(sp):
            sp.dma_start(h[:], dram["x"]).then_inc(x_in, 16)
            sp.dma_start(gain[:], dram["gains"]).then_inc(consts_in, 16)
            for phase in phases:
                phase.sync(sp)

        @block.gpsimd
        def _(pool):
            tables.gpsimd(pool)
            for phase in phases:
                phase.gpsimd(pool)

        @block.scalar
        def _(act):
            act.dma_start(const[:], dram["consts"][:, 0:C_BUCK]).then_inc(consts_in, 16)
            act.wait_ge(consts_in, 32)
            act.wait_ge(col_set, 3)
            for n in range(RING):
                split_hi(act, n)
            nc.scalar.preload_act_table(ACT.Silu)
            tables.scalar(act)
            for phase in phases:
                phase.scalar(act)

        @block.vector
        def _(dve):
            nc.vector.memset(col[:, 0:1], EPS).then_inc(col_set, 1)
            nc.vector.memset(col[:, 1:2], HD1 * EPS).then_inc(col_set, 1)
            nc.vector.memset(col[:, 2:3], 1.0).then_inc(col_set, 1)
            tables.vector(dve)
            for n in range(RING):
                split_lo(dve, n)
            dve.wait_ge(tables.trig, 1)
            for phase in phases:
                phase.vector(dve)

        @block.tensor
        def _(pe):
            tables.tensor(pe)
            pe.wait_ge(consts_in, 32)
            for phase in phases:
                phase.tensor(pe)


def kernel(**inputs):
    import concourse.bacc as bacc
    from concourse.bass_utils import run_bass_kernel_spmd

    nc = bacc.Bacc("TRN2", target_bir_lowering=False, num_devices=1)
    arrays = host_arrays(inputs)
    dram = {n: nc.dram_tensor(n, a.shape, mybir.dt.from_np(a.dtype), kind="ExternalInput").ap()
            for n, a in arrays.items()}
    out = nc.dram_tensor("out", (S, D), F32, kind="ExternalOutput").ap()
    build(nc, dram, out)
    result = run_bass_kernel_spmd(nc, [arrays], core_ids=[0])
    return result.results[0]["out"].reshape(1, S, D)
```

```python
from contextlib import ExitStack

import numpy as np

import concourse.bass as bass
from concourse import mybir

F32 = mybir.dt.float32
F32R = mybir.dt.float32r
I32 = mybir.dt.int32
ALU = mybir.AluOpType
ACT = mybir.ActivationFunctionType
AX = mybir.AxisListType

P = 128
S = 256
NT = S // P
D = 1024
KC = D // P
TW = 512
NB = D // TW
RING = 4
EPS = 1e-6
NEG = -1e30
TAKEN = -3e38
FF1, FF2 = 2816, 4096
H1, HD1 = 8, 64
TOPK = 64
H2, HD2 = 8, 128
ROPE, HALF = 64, 32
MLA_SCALE = (HD2 + ROPE) ** -0.5
SB_SCALE = HD2 ** -0.5
MEM_SCALE = 128 ** -0.5
NXH = 4
QL, KL = 384, 256
NPARTS, NBUCK = 4, 32

NORMS = ["ffn1", "mix", "ffn2", "mla", "mem0", "cross0", "mlp0", "sb", "mem1", "cross1", "mlp1", "final"]
NORM = {n: i for i, n in enumerate(NORMS)}
RMS_AT = {n: i + 1 for i, n in enumerate(n for n in NORMS if not n.startswith("mem"))}
QG_A, KG_A, QG_B, KG_B, QG_L, KG_L = 96, 97, 98, 99, 100, 103
NGAIN = 105


def weight_plan():
    plan, at = [], {}

    def add(section, array, tiles, width=TW):
        at.setdefault(section, len(plan))
        first = sum(1 for c in plan if c[0] == array)
        plan.extend((array, first + i, n, width) for i, n in enumerate(tiles))

    def ffn(name, steps, out_tiles):
        add(name, name + "_first", [2] * 4)
        add(name + "_mid", name + "_mid", [(8 + out_tiles) // 4] * 4 * (steps - 1))
        add(name + "_tail", name + "_tail", [out_tiles // 4] * 4)

    ffn("ffn1", 11, 4)
    add("idx", "w_idx", [2] * 4, 324)
    add("qkv", "w_qkv", [4] * 12)
    add("br_a", "w_br_a", [4] * 2)
    add("gate_a", "w_gate_a", [4] * 4)
    add("br_b", "w_br_b", [4] * 2)
    add("gate_b", "w_gate_b", [4] * 4)
    add("w_out", "w_out", [4] * 4)
    ffn("ffn2", 11, 4)
    add("dq", "w_dq", [4] * 2, QL)
    add("dkv", "w_dkv", [4] * 2, KL + ROPE)
    add("uq", "w_uq", [3] * 3)
    add("ukv", "w_ukv", [2] * 4)
    for i in range(2):
        if i == 1:
            add("sb_qkv", "w_sb_qkv", [4] * 12)
        add(f"xkv{i}", f"w_xkv{i}", [4] * 4)
        name = ("mla_o", "sb_o")[i]
        add(name, "w_" + name, [4] * 4)
        add(f"xq{i}", f"w_xq{i}", [4] * 2)
        add(f"xo{i}", f"w_xo{i}", [4] * 2)
        ffn(f"mlp{i}", 8, 8)
    return plan, at


PLAN, AT = weight_plan()


def t5_buckets(dist):
    d = np.maximum(dist, 0)
    large = 16 + (np.log(np.maximum(d, 1) / 16.0) / np.log(8.0) * 16).astype(np.int64)
    return np.where(d < 16, d, np.minimum(large, 31))


C_ID, C_CAUSAL, C_STRICT, C_SUFFIX, C_ONES, C_FREQ, C_BUCK = 0, 128, 384, 768, 896, 1024, 1056
RELW = 383
NCONST = C_BUCK + 384


def constants():
    c = np.zeros((P, NCONST), np.float32)
    row, col = np.arange(P)[:, None], np.arange(P)[None, :]
    c[:, C_ID:C_ID + P] = row == col
    c[:, C_CAUSAL + P:C_CAUSAL + 2 * P] = np.where(col <= row, 0.0, NEG)
    strict = np.where(row < col, 0.0, NEG)
    c[:, C_STRICT:C_STRICT + P] = strict
    c[:, C_STRICT + 2 * P:C_STRICT + 3 * P] = strict
    c[:, C_SUFFIX:C_SUFFIX + P] = np.where(row >= col, -1.0, 0.0)
    c[:, C_ONES:C_ONES + P] = -1.0
    exponent = -np.arange(0, ROPE, 2, dtype=np.float32) / np.float32(ROPE)
    c[:, C_FREQ:C_FREQ + HALF] = (10000.0 ** exponent.astype(np.float64)).astype(np.float32)
    dist = 255 - np.arange(RELW)
    for x, (d, b) in enumerate(zip(dist, t5_buckets(dist))):
        c[b if d >= 0 else NBUCK, C_BUCK + x] = 1.0
    return c


def chunked(a, tiles):
    u, p, t, w = a.shape
    return np.ascontiguousarray(
        a.reshape(u, p, t // tiles, tiles * w).transpose(0, 2, 1, 3).reshape(-1, p, tiles * w))


def by_block(w, width=TW):
    k, n = w.shape
    return w.reshape(k // P, P, n // width, width).transpose(2, 1, 0, 3)


def by_row(w, steps):
    k, n = w.shape
    return w.reshape(steps, k // P // steps, P, NB, TW).transpose(0, 2, 1, 3, 4).reshape(steps, P, -1, TW)


def ffn_arrays(name, up, down):
    n, tiles = up.shape[0], down.shape[2]
    last = down[n - 1:].reshape(1, P, tiles // NB, NB, TW).transpose(0, 1, 3, 2, 4).reshape(1, P, tiles, TW)
    return {name + "_first": chunked(up[:1], 2),
            name + "_mid": chunked(np.concatenate([up[1:], down[:n - 1]], axis=2), (8 + tiles) // 4),
            name + "_tail": chunked(last, tiles // 4)}


def host_arrays(x):
    out = {"x": np.ascontiguousarray(x["x"][0].reshape(NT, P, D).transpose(1, 0, 2)),
           "mem": np.ascontiguousarray(x["mem_2"][0].reshape(NT, P, D).transpose(1, 0, 2)),
           "positions": np.ascontiguousarray(x["positions_2"].astype(np.int32)[0].reshape(NT, P).T),
           "consts": constants()}
    for n in ("ffn1", "ffn2"):
        gu = x[n + "_w_gu"][0]
        up = gu.reshape(KC, P, 2, 11, 256).transpose(3, 1, 0, 2, 4).reshape(11, P, KC, TW)
        out.update(ffn_arrays(n, up, by_row(x[n + "_w_down"][0], 11)))
    w = x["w_in"][0]
    out["w_idx"] = chunked(by_block(w[:, 3072:3396], 324), 2)
    order = [3, 4, 0, 1, 5, 2]
    out["w_qkv"] = chunked(by_block(w[:, :3072])[order], 4)
    gates = by_block(w[:, 3396:])
    out["w_gate_a"], out["w_gate_b"] = chunked(gates[:2], 4), chunked(gates[2:], 4)
    out["w_br_a"] = chunked(by_block(x["w_branch_dsa"][0]), 4)
    out["w_br_b"] = chunked(by_block(x["w_branch_moba"][0]), 4)
    out["w_out"] = chunked(by_block(x["w_out"][0]), 4)
    dkv = x["mla_w_dkv_2"][0]
    out["w_dq"] = chunked(by_block(dkv[:, :QL], QL), 4)
    out["w_dkv"] = chunked(by_block(dkv[:, QL:], KL + ROPE), 4)
    uq = x["mla_w_uq_2"][0].reshape(QL, H2, HD2 + ROPE)
    parts = [uq[:, :, :HD2], uq[:, :, HD2:HD2 + HALF], uq[:, :, HD2 + HALF:]]
    out["w_uq"] = chunked(by_block(np.concatenate([p.reshape(QL, -1) for p in parts], axis=1)), 3)
    ukv = x["mla_w_ukv_2"][0].reshape(KL, H2, 2, HD2).transpose(0, 2, 1, 3).reshape(KL, -1)
    out["w_ukv"] = chunked(by_block(ukv), 2)
    out["w_mla_o"] = chunked(by_block(x["mla_w_o_2"][0]), 4)
    out["w_sb_qkv"] = chunked(by_block(x["sb_w_qkv_2"][0]), 4)
    out["w_sb_o"] = chunked(by_block(x["sb_w_o_2"][0]), 4)
    for i in range(2):
        out[f"w_xkv{i}"] = chunked(by_block(x["xa_w_kv_2"][i]), 4)
        out[f"w_xq{i}"] = chunked(by_block(x["xa_w_q_2"][i]), 4)
        out[f"w_xo{i}"] = chunked(by_block(x["xa_w_o_2"][i]), 4)
        out.update(ffn_arrays(f"mlp{i}", by_block(x["mlp_w_in_2"][i]), by_row(x["mlp_w_out_2"][i], 8)))
    gains = [x["ffn1_norm"][0], x["mix_norm"][0], x["ffn2_norm"][0], x["norm_mix_2"][0],
             x["norm_mem_2"][0], x["norm_cross_2"][0], x["norm_mlp_2"][0], x["norm_mix_2"][1],
             x["norm_mem_2"][1], x["norm_cross_2"][1], x["norm_mlp_2"][1], x["norm_final_2"]]
    columns = [g.reshape(KC, P).T for g in gains]
    for n in ("q_norm_dsa", "k_norm_dsa", "q_norm_moba", "k_norm_moba"):
        columns.append(np.concatenate([x[n][0], x[n][0]])[:, None])
    columns += [x["mla_g_q_2"][0].reshape(-1, P).T, x["mla_g_kv_2"][0].reshape(-1, P).T]
    out["gains"] = np.ascontiguousarray(np.concatenate(columns, axis=1))
    out["b_gate"] = np.ascontiguousarray(x["b_gate"])
    out["norm_final"] = np.ascontiguousarray(x["norm_final_2"][None, :])
    out["rel_bias"] = np.ascontiguousarray(x["rel_bias"])
    return out


class Count:

    def __init__(self, sem):
        self.sem, self.n = sem, 0

    def inc(self, ins):
        ins.then_inc(self.sem, 1)
        self.n += 1
        return self.n


def build(nc, dram, out):
    ctx = ExitStack()
    with ctx:
        def sb(name, shape, dt=F32):
            return ctx.enter_context(nc.sbuf_tensor(name, shape, dt))

        def sem(name):
            return ctx.enter_context(nc.semaphore(name))

        w_raw = sb("w_raw", [P, RING, 4 * TW])
        whi = sb("whi", [P, RING, 4 * TW], F32R)
        wlo = sb("wlo", [P, RING, 4 * TW], F32R)
        h = sb("h", [P, NT, D])
        xt_h = sb("xt_h", [P, KC, S], F32R)
        xt_l = sb("xt_l", [P, KC, S], F32R)
        ot_h = sb("ot_h", [P, KC, S], F32R)
        ot_l = sb("ot_l", [P, KC, S], F32R)
        qt = sb("qt", [P, KC, S])
        kt = sb("kt", [P, KC, S])
        v = sb("v", [P, NT, D])
        pet = sb("pet", [P, 5, S])
        rel = sb("rel", [P, 16, S])
        mem = rel[:, 8:16].rearrange("p (t a) s -> p t (a s)", t=NT)
        mem_v = rel[:, 4:8].rearrange("p (t a) s -> p t (a s)", t=NT)
        nat = sb("nat", [P, 2, NT, TW])
        lg = sb("lg", [P, 2, TW])
        pt = sb("pt", [P, 2, TW])
        score = sb("score", [P, NT, S])
        const = sb("const", [P, C_BUCK])
        gain = sb("gain", [P, NGAIN])
        ms = sb("ms", [P, 2 * len(NORMS) + 4])
        rs = sb("rs", [P, 2 * len(NORMS) + 4])
        col = sb("col", [P, 3])
        hs = sb("hs", [P, 2, NT * 8])
        newton = sb("newton", [P, NT * 8])
        nmax = sb("nmax", [P, 32])
        rsum = sb("rsum", [P, 32])
        rinv = sb("rinv", [P, 32])
        top8 = sb("top8", [P, NT, 8])
        wi = sb("wi", [P, NT, NPARTS])
        trig = sb("trig", [P, 2, NT, HALF])
        pos = sb("pos", [P, 4])

        ps = ctx.enter_context(nc.psum_tensor("ps", [P, 8, TW], F32))
        bankA = [ps[:, 0], ps[:, 1]]
        bankT = [ps[:, 2], ps[:, 3]]
        bankD = [[ps[:, 4], ps[:, 5]], [ps[:, 6], ps[:, 7]]]
        ident = const[:, C_ID:C_ID + P]

        w_loaded = [sem(f"w_loaded{s}") for s in range(RING)]
        w_hi = sem("w_hi")
        w_lo = sem("w_lo")
        w_used = sem("w_used")
        consts_in = sem("consts_in")
        x_in = sem("x_in")
        col_set = sem("col_set")
        mem_in = sem("mem_in")
        h_ready = sem("h_ready")
        xt_ps = sem("xt_ps")
        xt_hi = sem("xt_hi")
        xt_lo = sem("xt_lo")
        ms_ready = sem("ms_ready")
        rs_ready = sem("rs_ready")
        rows_made = sem("rows_made")
        rows_ps = sem("rows_ps")
        rows_hi = sem("rows_hi")
        rows_lo = sem("rows_lo")
        all_fins = []
        out_full = sem("out_full")
        out_projects = []
        act_own = Count(sem("act_own"))
        dve_own = Count(sem("dve_own"))

        def own(eng, counter, ins):
            eng.wait_ge(counter.sem, counter.inc(ins))

        ends = {}

        def used(ins, n):
            if n not in ends:
                back = 1
                while n - back in ends:
                    back += 1
                ins.then_inc(w_used, back)

        def slot_of(n):
            return n % RING

        def load_chunk(sp, n, r=0):
            array, k, tiles, width = PLAN[n]
            if n >= RING:
                sp.wait_ge(w_hi, r * RING + (n - RING + 1))
                sp.wait_ge(w_lo, r * RING + (n - RING + 1))
            if isinstance(r, int):
                src = dram[array][k + r * RING]
            else:
                src = dram[array][bass.ds(r * RING + k, 1)].rearrange("a p n -> p (a n)")
            sp.dma_start(w_raw[:, slot_of(n), 0:tiles * width], src).then_inc(w_loaded[slot_of(n)], 16)

        def split_hi(act, n, r=0):
            _, _, tiles, width = PLAN[n]
            s = slot_of(n)
            act.wait_ge(w_loaded[s], r * 16 + 16 * (n // RING + 1))
            if n - RING in ends:
                done, value, each = ends[n - RING]
                act.wait_ge(done, r * each + value)
            elif n >= RING:
                act.wait_ge(w_used, r * RING + (n - RING + 1))
            nc.scalar.activation(whi[:, s, 0:tiles * width], w_raw[:, s, 0:tiles * width],
                                 ACT.Copy).then_inc(w_hi, 1)

        def split_lo(dve, n, r=0):
            _, _, tiles, width = PLAN[n]
            s = slot_of(n)
            dve.wait_ge(w_hi, r * RING + (n + 1))
            nc.vector.tensor_tensor(wlo[:, s, 0:tiles * width], w_raw[:, s, 0:tiles * width],
                                    whi[:, s, 0:tiles * width].bitcast(F32), ALU.subtract).then_inc(w_lo, 1)

        def next_hi(act, n, r=0):
            if n + RING < len(PLAN):
                split_hi(act, n + RING, r)

        def next_lo(dve, n, r=0):
            if n + RING < len(PLAN):
                split_lo(dve, n + RING, r)

        def take_chunk(pe, n, r=0):
            pe.wait_ge(w_hi, r * RING + (n + 1))
            pe.wait_ge(w_lo, r * RING + (n + 1))

        def mm3(acc, hi, lo, s, j, width, start, stop):
            c = slice(j * width, (j + 1) * width)
            nc.tensor.matmul(acc, hi, whi[:, s, c], start=start, stop=False)
            nc.tensor.matmul(acc, hi, wlo[:, s, c], start=False, stop=False)
            return nc.tensor.matmul(acc, lo, whi[:, s, c], start=False, stop=stop)

        def norm_banks(name):
            last = bankA if name.startswith("mem") else [bankD[0][0], bankD[0][1]]
            return [bankT[0], bankT[1], last[0], last[1]]

        def source_ready(eng, name, block):
            if name.startswith("mem"):
                eng.wait_ge(mem_in, 16)
            elif name == "ffn1":
                eng.wait_ge(x_in, 16)
            else:
                updates = [n for n in NORMS[:NORM[name]] if not n.startswith("mem")]
                eng.wait_ge(h_ready, 4 * len(updates) - (2 if block == 0 else 0))

        def norm_tensor(pe, name, half):
            src = mem if name.startswith("mem") else h
            for pair, bank in list(enumerate(norm_banks(name)))[2 * half:2 * half + 2]:
                if pair % 2 == 0:
                    source_ready(pe, name, pair // 2)
                for j in range(2):
                    for t in range(NT):
                        k = 2 * pair + j
                        last = nc.tensor.transpose(bank[:, j * S + t * P:j * S + (t + 1) * P],
                                                   src[:, t, k * P:(k + 1) * P], ident)
                last.then_inc(xt_ps, 1)

        def norm_scalar(act, name, half):
            k0, to = 4 * NORM[name], xt_h
            for pair, bank in list(enumerate(norm_banks(name)))[2 * half:2 * half + 2]:
                act.wait_ge(xt_ps, k0 + pair + 1)
                for j in range(2):
                    k = 2 * pair + j
                    last = nc.scalar.activation(to[:, k], bank[:, j * S:(j + 1) * S], ACT.Copy,
                                                scale=gain[:, 8 * NORM[name] + k:8 * NORM[name] + k + 1])
                last.then_inc(xt_hi, 1)

        def rms_scalar(act, name):
            c = 2 * NORM[name]
            source_ready(act, name, 1)
            for t in range(NT):
                last = nc.scalar.activation(lg[:, :, :].rearrange("p a n -> p (a n)"), h[:, t], ACT.Square,
                                            scale=D ** -0.5, accum_out=ms[:, c + t:c + t + 1])
                if t == 0:
                    own(act, act_own, last)
            last.then_inc(ms_ready, 1)

        def root_vector(dve, name):
            c = 2 * NORM[name]
            dve.wait_ge(ms_ready, RMS_AT[name])
            rsqrt(dve, ms[:, c:c + 2], rs[:, c:c + 2], 1.0, EPS, 2).then_inc(rs_ready, 1)

        def rsqrt(dve, x, y, scale, eps, n):
            a = newton[:, 0:n]
            own(dve, dve_own, nc.vector.tensor_scalar(x, x, scale, eps, ALU.mult, ALU.add))
            own(dve, dve_own, nc.vector.tensor_scalar(a.bitcast(I32), x.bitcast(I32), 1, None,
                                                      ALU.arith_shift_right))
            own(dve, dve_own, nc.vector.tensor_scalar(y.bitcast(I32), a.bitcast(I32), -1.0, float(0x5f3759df),
                                                      ALU.mult, ALU.add))
            for step in range(3):
                own(dve, dve_own, nc.vector.scalar_tensor_tensor(out=a, in0=y, scalar=-0.5, in1=y,
                                                                 op0=ALU.mult, op1=ALU.mult))
                own(dve, dve_own, nc.vector.tensor_tensor(a, a, x, ALU.mult))
                last = nc.vector.scalar_tensor_tensor(out=y, in0=a, scalar=1.5, in1=y,
                                                      op0=ALU.add, op1=ALU.mult)
                if step < 2:
                    own(dve, dve_own, last)
            return last

        def norm_vector(dve, name, half):
            k0, hi, lo = 4 * NORM[name], xt_h, xt_l
            for pair, bank in list(enumerate(norm_banks(name)))[2 * half:2 * half + 2]:
                dve.wait_ge(xt_hi, k0 + pair + 1)
                for j in range(2):
                    k = 2 * pair + j
                    g = gain[:, 8 * NORM[name] + k:8 * NORM[name] + k + 1]
                    last = nc.vector.scalar_tensor_tensor(
                        out=lo[:, k], in0=bank[:, j * S:(j + 1) * S], scalar=g,
                        in1=hi[:, k].bitcast(F32), op0=ALU.mult, op1=ALU.subtract)
                last.then_inc(xt_lo, 1)

        def xt_ready(pe, name, k):
            pe.wait_ge(xt_lo, 4 * NORM[name] + k // 2 + 1)

        def rms(name, t):
            return rs[:, 2 * NORM[name] + t:2 * NORM[name] + t + 1]

        def residual_vector(dve, full, scale, block, full0=0):
            for t in range(NT):
                dve.wait_ge(full, full0 + NT * block + t + 1)
                hb = h[:, t, block * TW:(block + 1) * TW]
                nc.vector.scalar_tensor_tensor(out=hb, in0=bankD[t][block], scalar=scale, in1=hb,
                                               op0=ALU.mult, op1=ALU.add).then_inc(h_ready, 1)

        def tail_scalar(act, chunks, following):
            for n in chunks[:-1]:
                next_hi(act, n)
            if following:
                norm_scalar(act, following, 0)
            next_hi(act, chunks[-1])

        def tail_vector(dve, chunks, following, full, scale, full0=0):
            half = len(chunks) // 2
            for n in chunks[:half - 1]:
                next_lo(dve, n)
            residual_vector(dve, full, scale, 0, full0)
            for n in chunks[half - 1:-1]:
                next_lo(dve, n)
            if following:
                norm_vector(dve, following, 0)
            residual_vector(dve, full, scale, 1, full0)
            next_lo(dve, chunks[-1])

        class Ffn:
            def __init__(self, name, steps, hk, gated, scale, following):
                self.following = following
                self.name, self.steps, self.hk, self.gated, self.scale = name, steps, hk, gated, scale
                self.n0 = AT[name]
                self.tiles = (8 + 2 * hk) // 4
                self.up_full = sem(name + "_up_full")
                self.acted = sem(name + "_acted")
                self.hidden = sem(name + "_hidden")
                self.hid_ps = sem(name + "_hid_ps")
                self.hid_hi = sem(name + "_hid_hi")
                self.hid_lo = sem(name + "_hid_lo")
                self.down_full = sem(name + "_down_full")
                ends[self.n0 + 3] = (self.up_full, NT, 0)
                tail = self.n0 + 4 * steps
                ends[tail + 3] = (self.down_full, NB * NT, 0)
                ends[tail + 1] = (self.down_full, NT, 0)
                if not gated:
                    for i in range(1, steps):
                        ends[self.n0 + 4 * i + 1] = (self.up_full, NT * (i + 1), NT)

            def up(self, pe, i, s, pos, ks, fresh):
                if fresh and ks[0] == 2:
                    norm_tensor(pe, self.name, 1)
                for t in range(NT):
                    if ks[0] == 0 and not fresh:
                        pe.wait_ge(self.hidden if self.gated else self.acted, i * NT + (t - 1))
                    for j, k in enumerate(ks):
                        if fresh and t == 0 and k % 2 == 0:
                            xt_ready(pe, self.name, k)
                        last = mm3(bankA[t], xt_h[:, k, t * P:(t + 1) * P], xt_l[:, k, t * P:(t + 1) * P],
                                   s, pos + j, TW, k == 0, k == KC - 1)
                    if ks[-1] == KC - 1:
                        last.then_inc(self.up_full, 1)
                return last

            def down(self, pe, s, pos, js, first, final):
                for a, j in enumerate(js):
                    k, block = (j % self.hk, j // self.hk) if final else (j // NB, j % NB)
                    for t in range(NT):
                        last = mm3(bankD[t][block], ot_h[:, k, t * P:(t + 1) * P],
                                   ot_l[:, k, t * P:(t + 1) * P], s, pos + a, TW,
                                   first and k == 0, final and k == self.hk - 1)
                        if final and k == self.hk - 1:
                            last.then_inc(self.down_full, 1)
                return last

            def turn(self, pe, i):
                pe.wait_ge(self.hidden, i * NT)
                if not isinstance(i, int) or i > 1:
                    pe.wait_ge(self.hid_lo, i - 1)
                for k in range(self.hk):
                    for t in range(NT):
                        at = (k % 2) * S + t * P
                        last = nc.tensor.transpose(bankT[k // 2][:, at:at + P],
                                                   nat[:, 0, t, k * P:(k + 1) * P], ident)
                last.then_inc(self.hid_ps, 1)

            def step_tensor(self, pe, i, n, r=0, first=False):
                self.turn(pe, i)
                for c in range(4):
                    take_chunk(pe, n + c, r)
                    tiles = list(range(c * self.tiles, (c + 1) * self.tiles))
                    ups, downs = [j for j in tiles if j < KC], [j - KC for j in tiles if j >= KC]
                    if ups:
                        last = self.up(pe, i, slot_of(n + c), 0, ups, False)
                    if downs:
                        if downs[0] == 0:
                            pe.wait_ge(self.hid_lo, i)
                        last = self.down(pe, slot_of(n + c), len(ups), downs, first, False)
                    used(last, n + c)

            def tensor(self, pe):
                for c in range(4):
                    take_chunk(pe, self.n0 + c)
                    if c == 3 and self.name == "ffn1":
                        tables.tensor(pe)
                    used(self.up(pe, 0, slot_of(self.n0 + c), 0, [2 * c, 2 * c + 1], True), self.n0 + c)
                self.step_tensor(pe, 1, self.n0 + 4, first=True)
                with pe.Fori(0, self.steps - 2) as r:
                    self.step_tensor(pe, r + 2, self.n0 + 8, r)
                self.turn(pe, self.steps)
                pe.wait_ge(self.hid_lo, self.steps)
                n, each = self.n0 + 4 * self.steps, self.hk // 2
                for c in range(4):
                    take_chunk(pe, n + c)
                    if c == 3 and self.following:
                        norm_tensor(pe, self.following, 0)
                    used(self.down(pe, slot_of(n + c), 0, list(range(c * each, (c + 1) * each)),
                                   False, True), n + c)

            def take_up_scalar(self, act, i):
                for t in range(NT):
                    act.wait_ge(self.up_full, i * NT + (t + 1))
                    if not isinstance(i, int) or i > 0:
                        act.wait_ge(self.hidden, i * NT + (t - 1))
                    if self.gated:
                        ins = nc.scalar.activation(lg[:, t, 0:256], bankA[t][:, 0:256], ACT.Silu,
                                                   scale=rms(self.name, t))
                    else:
                        ins = nc.scalar.activation(lg[:, t], bankA[t], ACT.Relu, scale=rms(self.name, t))
                    ins.then_inc(self.acted, 1)

            def turned_scalar(self, act, i):
                act.wait_ge(self.hid_ps, i)
                for b in range(self.hk // 2):
                    last = nc.scalar.activation(ot_h[:, 2 * b:2 * b + 2],
                                                bankT[b].rearrange("p (k s) -> p k s", k=2), ACT.Copy)
                last.then_inc(self.hid_hi, 1)

            def step_scalar(self, act, i, n, r=0):
                self.turned_scalar(act, i)
                next_hi(act, n, r)
                next_hi(act, n + 1, r)
                self.take_up_scalar(act, i)
                next_hi(act, n + 2, r)
                next_hi(act, n + 3, r)

            def scalar(self, act):
                norm_scalar(act, self.name, 1)
                rms_scalar(act, self.name)
                for c in range(3):
                    next_hi(act, self.n0 + c)
                if self.name == "ffn1":
                    tables.scalar(act)
                if self.gated:
                    nc.scalar.preload_act_table(ACT.Silu)
                act.wait_ge(rs_ready, RMS_AT[self.name])
                self.take_up_scalar(act, 0)
                next_hi(act, self.n0 + 3)
                with act.Fori(0, self.steps - 2) as r:
                    self.step_scalar(act, r + 1, self.n0 + 4, r)
                self.step_scalar(act, self.steps - 1, self.n0 + 4 * (self.steps - 1))
                self.turned_scalar(act, self.steps)
                tail_scalar(act, [self.n0 + 4 * self.steps + c for c in range(4)], self.following)

            def hide_vector(self, dve, i):
                for t in range(NT):
                    dve.wait_ge(self.acted, i * NT + (t + 1))
                    if not isinstance(i, int) or i > 0:
                        dve.wait_ge(self.hid_ps, i)
                    if self.gated:
                        ins = nc.vector.scalar_tensor_tensor(
                            out=nat[:, 0, t, 0:256], in0=bankA[t][:, 256:512], scalar=rms(self.name, t),
                            in1=lg[:, t, 0:256], op0=ALU.mult, op1=ALU.mult)
                    else:
                        ins = nc.vector.tensor_tensor(nat[:, 0, t], lg[:, t], lg[:, t], ALU.mult)
                    ins.then_inc(self.hidden, 1)

            def turned_vector(self, dve, i):
                dve.wait_ge(self.hid_hi, i)
                for b in range(self.hk // 2):
                    last = nc.vector.tensor_tensor(ot_l[:, 2 * b:2 * b + 2],
                                                   bankT[b].rearrange("p (k s) -> p k s", k=2),
                                                   ot_h[:, 2 * b:2 * b + 2].bitcast(F32), ALU.subtract)
                last.then_inc(self.hid_lo, 1)

            def step_vector(self, dve, i, n, r=0):
                self.turned_vector(dve, i)
                next_lo(dve, n, r)
                next_lo(dve, n + 1, r)
                self.hide_vector(dve, i)
                next_lo(dve, n + 2, r)
                next_lo(dve, n + 3, r)

            def vector(self, dve):
                norm_vector(dve, self.name, 1)
                next_lo(dve, self.n0)
                root_vector(dve, self.name)
                if self.name == "ffn1":
                    tables.vector(dve)
                dve.wait_ge(rs_ready, RMS_AT[self.name])
                for c in range(1, 3):
                    next_lo(dve, self.n0 + c)
                self.hide_vector(dve, 0)
                next_lo(dve, self.n0 + 3)
                with dve.Fori(0, self.steps - 2) as r:
                    self.step_vector(dve, r + 1, self.n0 + 4, r)
                self.step_vector(dve, self.steps - 1, self.n0 + 4 * (self.steps - 1))
                self.turned_vector(dve, self.steps)
                tail_vector(dve, [self.n0 + 4 * self.steps + c for c in range(4)], self.following,
                            self.down_full, self.scale)

            def sync(self, sp):
                n = self.n0
                for c in range(4):
                    load_chunk(sp, n + c)
                with sp.Fori(0, self.steps - 1) as r:
                    for c in range(4):
                        load_chunk(sp, n + 4 + c, r)
                for c in range(4):
                    load_chunk(sp, n + 4 * self.steps + c)

            def gpsimd(self, pool):
                pass

        class Unit:

            def __init__(self, kind, ks, width, chunks, to=None, gains=None, scale=1.0, rows=None, base=0, vals=v):
                self.vals = vals
                self.kind, self.ks, self.width, self.chunks = kind, ks, width, chunks
                self.to, self.gains, self.scale, self.rows, self.base = to, gains, scale, rows, base

        class Project:
            def __init__(self, name, section, units, stat_h, stat_l, norm=None, need=(), scaled=None):
                self.name, self.units, self.norm, self.need = name, units, norm, need
                self.scaled = (rs_ready, RMS_AT[norm]) if norm else scaled
                self.stat_h, self.stat_l = stat_h, stat_l
                self.full = sem(name + "_full")
                self.evac = sem(name + "_evac")
                kinds = [unit.kind for unit in units]
                if {"qk", "dkv", "pe"} & set(kinds):
                    self.made = sem(name + "_made")
                self.turned = sem(name + "_turned")
                self.taken = sem(name + "_taken")
                self.lows = None
                if "latent" in kinds:
                    self.squared = sem(name + "_squared")
                    self.rooted = sem(name + "_rooted")
                if "latent" in kinds:
                    self.lows = sem(name + "_lows")
                n, made, turn, low = AT[section], 0, 0, 0
                for u, unit in enumerate(units):
                    unit.u, unit.n = u, []
                    k = unit.ks[0]
                    for tiles in unit.chunks:
                        unit.n.append((n, list(range(k, k + tiles))))
                        k, n = k + tiles, n + 1
                    ends[n - 1] = (self.full, NT * (u + 1), 0)
                    if unit.kind in ("qk", "dkv", "pe"):
                        unit.made, made = made, made + 1
                    if unit.kind != "v":
                        unit.turn, turn = turn, turn + 1
                    unit.low0 = NT * low
                    if unit.kind in ("latent", "dkv"):
                        low += 1
                self.turns, self.lowest = turn, low
                self.evac_ready = (self.evac, NT * len(units))
                self.turned_ready = (self.taken, NT * turn)
                self.split_ready = (self.lows, NT * low)

            def nat_of(self, unit, t):
                return nat[:, unit.u % 2, t]

            def multiply(self, pe, unit):
                for c, (n, ks) in enumerate(unit.n):
                    take_chunk(pe, n)
                    for part in (ks[:2], ks[2:]) if self.norm and unit.u == 0 else (ks,):
                        if self.norm and unit.u == 0 and part and part[0] == 2:
                            norm_tensor(pe, self.norm, 1)
                        for t in range(NT):
                            if part and part[0] == unit.ks[0] and unit.u > 0:
                                pe.wait_ge(self.evac, NT * (unit.u - 1) + t + 1)
                            for k in part:
                                if self.norm and unit.u == 0 and t == 0 and k % 2 == 0:
                                    xt_ready(pe, self.norm, k)
                                last = mm3(bankA[t][:, 0:unit.width], self.stat_h[:, k, t * P:(t + 1) * P],
                                           self.stat_l[:, k, t * P:(t + 1) * P], slot_of(n), k - ks[0],
                                           unit.width, k == unit.ks[0], k == unit.ks[-1])
                                if k == unit.ks[-1]:
                                    last.then_inc(self.full, 1)
                    used(last, n)

            def turn(self, pe, unit):
                for t in range(NT):
                    if unit.kind in ("qk", "dkv", "pe"):
                        pe.wait_ge(self.made, NT * unit.made + t + 1)
                    else:
                        pe.wait_ge(self.evac, NT * unit.u + t + 1)
                    if unit.turn > 0:
                        pe.wait_ge(self.taken, NT * (unit.turn - 1) + t + 1)
                    if unit.low0:
                        pe.wait_ge(self.lows, unit.low0 - NT + t + 1)
                    blocks = [self.nat_of(unit, t)[:, c * P:(c + 1) * P] for c in range(4)]
                    if unit.kind in ("idx", "latent"):
                        blocks = blocks[:3]
                    if unit.kind == "dkv":
                        blocks = blocks[:2] + [lg[:, t, 0:P]]
                    if unit.kind == "pe":
                        blocks = [lg[:, t, c * P:(c + 1) * P] for c in range(4)]
                    for c, b in enumerate(blocks):
                        last = nc.tensor.transpose(bankT[t][:, c * P:(c + 1) * P], b, ident)
                    last.then_inc(self.turned, 1)

            def tensor(self, pe):
                for s, value in self.need:
                    pe.wait_ge(s, value)
                before = None
                for unit in self.units:
                    self.multiply(pe, unit)
                    if before is not None:
                        self.turn(pe, before)
                    before = unit if unit.kind != "v" else None
                if before is not None:
                    self.turn(pe, before)

            def copy_out(self, act, unit):
                w = unit.width
                if unit.u == 0 and self.scaled:
                    act.wait_ge(*self.scaled)
                for t in range(NT):
                    act.wait_ge(self.full, NT * unit.u + t + 1)
                    row = unit.rows(t)
                    if unit.kind == "v":
                        nc.scalar.activation(unit.vals[:, t, unit.base:unit.base + w], bankA[t], ACT.Copy,
                                             scale=row).then_inc(self.evac, 1)
                    elif unit.kind == "idx":
                        to = self.nat_of(unit, t)
                        nc.scalar.activation(wi[:, t], bankA[t][:, 320:324], ACT.Copy, scale=row)
                        nc.scalar.activation(to[:, 320:384], bankA[t][:, 256:320], ACT.Copy, scale=row)
                        nc.scalar.activation(to[:, 0:320], bankA[t][:, 0:320], ACT.Copy,
                                             scale=row).then_inc(self.evac, 1)
                    else:
                        nc.scalar.activation(self.nat_of(unit, t)[:, 0:w], bankA[t][:, 0:w], ACT.Copy,
                                             scale=row).then_inc(self.evac, 1)

            def latent_squares(self, act, unit):
                n = {"latent": QL, "dkv": KL}[unit.kind]
                c = 2 * len(NORMS) + (0 if unit.kind == "latent" else 2)
                act.wait_ge(self.evac, NT * (unit.u + 1))
                for t in range(NT):
                    last = nc.scalar.activation(
                        score[:, :, :].rearrange("p a n -> p (a n)")[:, 0:n], self.nat_of(unit, t)[:, 0:n],
                        ACT.Square, scale=n ** -0.5, accum_out=ms[:, c + t:c + t + 1])
                    if unit.kind == "dkv" and t == 1:
                        last.then_inc(self.squared, 1)
                    else:
                        own(act, act_own, last)

            def take(self, act, unit):
                if unit.to is qt and unit.kind == "qk":
                    act.wait_ge(tables.out, 16)
                for t in range(NT):
                    act.wait_ge(self.turned, NT * unit.turn + t + 1)
                    bank, s = bankT[t].rearrange("p (c s) -> p c s", c=4), slice(t * P, (t + 1) * P)
                    if unit.kind in ("latent", "dkv"):
                        for c in range(unit.ks_out):
                            last = nc.scalar.activation(ot_h[:, unit.base + c, s], bank[:, c], ACT.Copy,
                                                        scale=gain[:, unit.gains + c:unit.gains + c + 1])
                        if unit.kind == "dkv":
                            last = nc.scalar.activation(pet[:, 4, s], bank[:, 2], ACT.Copy)
                    elif unit.kind == "idx":
                        last = nc.scalar.activation(pet[:, 0:3, s], bank[:, 0:3], ACT.Copy)
                    elif unit.kind == "qk":
                        last = nc.scalar.activation(unit.to[:, unit.base:unit.base + 4, s], bank, ACT.Copy,
                                                    scale=gain[:, unit.gains:unit.gains + 1])
                    else:
                        last = nc.scalar.activation(unit.to[:, unit.base:unit.base + 4, s], bank, ACT.Copy,
                                                    scale=unit.scale)
                    last.then_inc(self.taken, 1)

            def scalar(self, act):
                before = None
                for unit in self.units:
                    self.copy_out(act, unit)
                    for n, _ in unit.n:
                        next_hi(act, n)
                    if unit.kind in ("latent", "dkv"):
                        self.latent_squares(act, unit)
                    if before is not None:
                        self.take(act, before)
                    before = unit if unit.kind != "v" else None
                if before is not None:
                    self.take(act, before)

            def squares(self, dve, unit):
                for t in range(NT):
                    dve.wait_ge(self.evac, NT * unit.u + t + 1)
                    rows = self.nat_of(unit, t)
                    last = nc.vector.tensor_tensor(lg[:, t], rows, rows, ALU.mult)
                own(dve, dve_own, last)
                own(dve, dve_own, nc.vector.tensor_reduce(
                    hs[:, 0], lg[:, :, :].rearrange("p t (h d) -> p (t h) d", d=HD1), AX.X, ALU.add))
                query = unit.scale != 1.0
                own(dve, dve_own, rsqrt(dve, hs[:, 0], hs[:, 1], 1.0 if query else 1.0 / HD1,
                                        HD1 * EPS if query else EPS, NT * 8))

            def normalise(self, dve, unit):
                for t in range(NT):
                    rows = self.nat_of(unit, t).rearrange("p (h d) -> p h d", d=HD1)
                    nc.vector.tensor_tensor(rows, rows, hs[:, 1, 8 * t:8 * t + 8].unsqueeze(2).to_broadcast(
                        [P, 8, HD1]), ALU.mult).then_inc(self.made, 1)

            def rotate(self, dve, unit):
                dve.wait_ge(tables.trig, 1)
                heads = 1 if unit.kind == "dkv" else H2
                at = KL if unit.kind == "dkv" else 0
                for t in range(NT):
                    dve.wait_ge(self.evac, NT * unit.u + t + 1)
                    if unit.made or t:
                        dve.wait_ge(self.made, NT * unit.made + t)
                    w = heads * HALF
                    x1, x2 = (self.nat_of(unit, t)[:, at + a * w:at + (a + 1) * w]
                              .rearrange("p (h d) -> p h d", h=heads) for a in range(2))
                    cos, sin = (trig[:, a, t].unsqueeze(1).to_broadcast([P, heads, HALF]) for a in range(2))
                    part = [pt[:, a // 2, (a % 2) * 256:(a % 2) * 256 + w].rearrange("p (h d) -> p h d", h=heads)
                            for a in range(4)]
                    nc.vector.tensor_tensor(part[0], x1, cos, ALU.mult)
                    nc.vector.tensor_tensor(part[1], x2, sin, ALU.mult)
                    nc.vector.tensor_tensor(part[2], x1, sin, ALU.mult)
                    own(dve, dve_own, nc.vector.tensor_tensor(part[3], x2, cos, ALU.mult))
                    copies = 2 if unit.kind == "dkv" else 1
                    for c in range(copies):
                        to = lg[:, t, c * ROPE:c * ROPE + heads * ROPE].rearrange("p (h d) -> p h d", h=heads)
                        nc.vector.tensor_tensor(to[:, :, 0:HALF], part[0], part[1], ALU.subtract)
                        last = nc.vector.tensor_tensor(to[:, :, HALF:ROPE], part[2], part[3], ALU.add)
                    last.then_inc(self.made, 1)

            def lower(self, dve, unit):
                for t in range(NT):
                    dve.wait_ge(self.taken, NT * unit.turn + t + 1)
                    s = slice(t * P, (t + 1) * P)
                    for c in range(unit.ks_out):
                        g = gain[:, unit.gains + c:unit.gains + c + 1]
                        last = nc.vector.scalar_tensor_tensor(
                            out=ot_l[:, unit.base + c, s], in0=bankT[t][:, c * P:(c + 1) * P], scalar=g,
                            in1=ot_h[:, unit.base + c, s].bitcast(F32), op0=ALU.mult, op1=ALU.subtract)
                    last.then_inc(self.lows, 1)

            def vector(self, dve):
                before = None
                for unit in self.units:
                    if unit.kind == "qk":
                        self.squares(dve, unit)
                    for n, _ in unit.n:
                        next_lo(dve, n)
                    if unit.kind == "qk":
                        self.normalise(dve, unit)
                    if unit.kind in ("dkv", "pe"):
                        self.rotate(dve, unit)
                    if before is not None and before.kind in ("latent", "dkv"):
                        self.lower(dve, before)
                    before = unit
                if before.kind in ("latent", "dkv"):
                    self.lower(dve, before)
                    c = 2 * len(NORMS)
                    dve.wait_ge(self.squared, 1)
                    rsqrt(dve, ms[:, c:c + 4], rs[:, c:c + 4], 1.0, EPS, 4).then_inc(self.rooted, 1)

            def sync(self, sp):
                for unit in self.units:
                    for n, _ in unit.n:
                        load_chunk(sp, n)

            def gpsimd(self, pool):
                pass

        class Finish:
            def __init__(self, fins, done, normalised):
                self.fins, self.done, self.normalised = fins, done, normalised
                self.f0 = sum(len(f) for f in all_fins)
                all_fins.append(fins)
                self.ready = (rows_lo, self.f0 + len(fins))

            def out_rows(self, dve, f):
                t, b, value, at, heads = self.fins[f]
                dve.wait_ge(self.done, value)
                same = [g for g in range(f) if self.fins[g][0] == t]
                if same:
                    dve.wait_ge(rows_ps, self.f0 + same[-1] + 1)
                if self.normalised:
                    own(dve, dve_own, nc.vector.reciprocal(rinv[:, at:at + heads], rsum[:, at:at + heads]))
                    nc.vector.tensor_tensor(
                        nat[:, 0, t].rearrange("p (h d) -> p h d", h=heads),
                        bankD[t][b].rearrange("p (h d) -> p h d", h=heads),
                        rinv[:, at:at + heads].unsqueeze(2).to_broadcast([P, heads, TW // heads]),
                        ALU.mult).then_inc(rows_made, 1)
                else:
                    nc.vector.tensor_copy(nat[:, 0, t], bankD[t][b]).then_inc(rows_made, 1)

            def turn(self, pe, f):
                t, b = self.fins[f][:2]
                pe.wait_ge(rows_made, self.f0 + f + 1)
                for c in range(4):
                    last = nc.tensor.transpose(bankD[t][b][:, c * P:(c + 1) * P],
                                               nat[:, 0, t, c * P:(c + 1) * P], ident)
                last.then_inc(rows_ps, 1)

            def take_hi(self, act, f):
                t, b = self.fins[f][:2]
                act.wait_ge(rows_ps, self.f0 + f + 1)
                nc.scalar.activation(ot_h[:, 4 * b:4 * b + 4, t * P:(t + 1) * P],
                                     bankD[t][b].rearrange("p (c s) -> p c s", c=4), ACT.Copy).then_inc(rows_hi, 1)

            def take_lo(self, dve, f):
                t, b = self.fins[f][:2]
                dve.wait_ge(rows_hi, self.f0 + f + 1)
                nc.vector.tensor_tensor(ot_l[:, 4 * b:4 * b + 4, t * P:(t + 1) * P],
                                        bankD[t][b].rearrange("p (c s) -> p c s", c=4),
                                        ot_h[:, 4 * b:4 * b + 4, t * P:(t + 1) * P].bitcast(F32),
                                        ALU.subtract).then_inc(rows_lo, 1)

        class Attend:
            def __init__(self, name, groups, fins, need, select=None):
                self.groups, self.need, self.select = groups, need, select
                self.scores = sem(name + "_scores")
                self.logits = sem(name + "_logits")
                self.probs = sem(name + "_probs")
                self.p_ps = sem(name + "_p_ps")
                self.p_sb = sem(name + "_p_sb")
                self.summed = sem(name + "_summed")
                self.fin = Finish([(t, b, g + 1, at, hh) for t, b, g, at, hh in fins], self.summed, True)
                self.last = [g for _, _, g, _, _ in fins]
                self.ready = self.fin.ready

            def score(self, pe, g):
                if g >= 2:
                    pe.wait_ge(self.logits, g - 1)
                for head in self.groups[g]:
                    for i, (q, k) in enumerate(head["qk"]):
                        last = nc.tensor.matmul(bankA[g % 2][:, head["at"]:head["at"] + head["width"]], q, k,
                                                start=i == 0, stop=i == len(head["qk"]) - 1)
                last.then_inc(self.scores, 1)

            def turn(self, pe, g):
                pe.wait_ge(self.probs, g + 1)
                if g >= 2:
                    pe.wait_ge(self.p_sb, g - 1)
                for c in range(4):
                    last = nc.tensor.transpose(bankT[g % 2][:, c * P:(c + 1) * P],
                                               lg[:, g % 2, c * P:(c + 1) * P], ident)
                last.then_inc(self.p_ps, 1)

            def value(self, pe, g):
                pe.wait_ge(self.p_sb, g + 1)
                for head in self.groups[g]:
                    for i, val in enumerate(head["v"]):
                        c = head["at"] + i * P
                        last = nc.tensor.matmul(head["out"], pt[:, g % 2, c:c + P], val,
                                                start=i == 0, stop=i == len(head["v"]) - 1)
                last.then_inc(self.summed, 1)

            def tensor(self, pe):
                for s, value in self.need:
                    pe.wait_ge(s, value)
                if self.select:
                    self.select.tensor(pe)
                self.score(pe, 0)
                for g in range(len(self.groups) + 3):
                    if g + 1 < len(self.groups):
                        self.score(pe, g + 1)
                    if g < len(self.groups):
                        self.turn(pe, g)
                    if 1 <= g <= len(self.groups):
                        self.value(pe, g - 1)
                    for f, last in enumerate(self.last):
                        if last == g - 2:
                            self.fin.turn(pe, f)

            def scalar(self, act):
                nc.scalar.preload_act_table_set("natural_log_exp_and_others")
                if self.select:
                    self.select.scalar(act)
                for g in range(len(self.groups) + 4):
                    if g < len(self.groups):
                        act.wait_ge(self.logits, g + 1)
                        for head in self.groups[g]:
                            rows = lg[:, g % 2, head["at"]:head["at"] + head["width"]]
                            c = head["col"]
                            last = nc.scalar.activation(rows, rows, ACT.Exp, bias=nmax[:, c:c + 1], scale=-1.0,
                                                        accum_out=rsum[:, c:c + 1])
                        last.then_inc(self.probs, 1)
                    for f, last in enumerate(self.last):
                        if last == g - 3:
                            self.fin.take_hi(act, f)

            def vector(self, dve):
                if self.select:
                    self.select.vector(dve)
                for g in range(len(self.groups) + 4):
                    if g < len(self.groups):
                        if self.select:
                            self.select.before_logits(dve, g)
                        dve.wait_ge(self.scores, g + 1)
                        if g >= 2:
                            dve.wait_ge(self.p_ps, g - 1)
                        for head in self.groups[g]:
                            c, a, w = head["col"], head["at"], head["width"]
                            last = nc.vector.tensor_tensor_reduce(
                                out=lg[:, g % 2, a:a + w], in0=bankA[g % 2][:, a:a + w], in1=head["bias"],
                                scale=-1.0, scalar=3e38, op0=ALU.add, op1=ALU.min,
                                accum_out=nmax[:, c:c + 1])
                        last.then_inc(self.logits, 1)
                    if 1 <= g <= len(self.groups):
                        dve.wait_ge(self.p_ps, g)
                        if g >= 3:
                            dve.wait_ge(self.summed, g - 2)
                        nc.vector.tensor_copy(pt[:, (g - 1) % 2], bankT[(g - 1) % 2]).then_inc(self.p_sb, 1)
                    for f, last in enumerate(self.last):
                        if last == g - 2:
                            self.fin.out_rows(dve, f)
                        if last == g - 3:
                            self.fin.take_lo(dve, f)
                    if self.select:
                        self.select.after_group(dve, g)

            def sync(self, sp):
                pass

            def gpsimd(self, pool):
                if self.select:
                    self.select.gpsimd(pool, self)

        class Select:
            ROUNDS = TOPK // 8

            def __init__(self, moba_groups):
                self.moba_groups = moba_groups
                self.dots = sem("idx_dots")
                self.relus = sem("idx_relus")
                self.summed = sem("idx_summed")
                self.selected = sem("idx_selected")
                self.biased = sem("idx_biased")
                self.passes = [(0, 0, [0, 2], P), (0, 1, [1, 3], P), (1, 0, [0, 2], S), (1, 1, [1, 3], S)]

            def tensor(self, pe):
                for i, (t, bank, heads, keys) in enumerate(self.passes):
                    if i >= 2:
                        pe.wait_ge(self.relus, i - 1)
                    for j, head in enumerate(heads):
                        half = slice(64 * (head % 2), 64 * (head % 2) + 64)
                        last = nc.tensor.matmul(bankD[bank][0][:, j * keys:(j + 1) * keys],
                                                pet[half, head // 2, t * P:(t + 1) * P],
                                                pet[half, 2, 0:keys], start=True, stop=True)
                    last.then_inc(self.dots, 1)

            def scalar(self, act):
                for i, (t, bank, heads, keys) in enumerate(self.passes):
                    act.wait_ge(self.dots, i + 1)
                    if i >= 2:
                        act.wait_ge(self.summed, i - 1)
                    nc.scalar.activation(pt[:, i % 2, 0:2 * keys], bankD[bank][0][:, 0:2 * keys], ACT.Relu,
                                         scale=0.125 * 0.5)\
                        .then_inc(self.relus, 1)

            def vector(self, dve):
                for i, (t, bank, heads, keys) in enumerate(self.passes):
                    dve.wait_ge(self.relus, i + 1)
                    for j, head in enumerate(heads):
                        to = score[:, t, 0:keys]
                        before = const[:, C_CAUSAL + S - keys:C_CAUSAL + S] if head == 0 else to
                        ins = nc.vector.scalar_tensor_tensor(
                            out=to, in0=pt[:, i % 2, j * keys:(j + 1) * keys],
                            scalar=wi[:, t, head:head + 1], in1=before, op0=ALU.mult, op1=ALU.add)
                        if j < len(heads) - 1:
                            own(dve, dve_own, ins)
                    ins.then_inc(self.summed, 1)
                    dve.wait_ge(self.summed, i + 1)

            def take_eight(self, dve):
                for t in range(NT):
                    last = nc.vector.max(top8[:, t], score[:, t, 0:(t + 1) * P])
                own(dve, dve_own, last)
                for t in range(NT):
                    rows = score[:, t, 0:(t + 1) * P]
                    last = nc.vector.match_replace(out=rows, in_to_replace=top8[:, t], in_values=rows,
                                                   imm_value=TAKEN)
                own(dve, dve_own, last)

            def after_group(self, dve, g):
                for r in range(2 * g, 2 * g + 2):
                    if r < self.ROUNDS:
                        self.take_eight(dve)
                if 2 * g + 2 == self.ROUNDS:
                    for t in range(NT):
                        rows = score[:, t, 0:(t + 1) * P]
                        nc.vector.tensor_scalar(rows, rows, -2e38, NEG, ALU.is_gt, ALU.mult)\
                            .then_inc(self.selected, 1)

            def before_logits(self, dve, g):
                if g >= self.moba_groups:
                    dve.wait_ge(self.biased, g - self.moba_groups + 1)

            def gpsimd(self, pool, attend):
                pool.wait_ge(self.selected, NT)
                for g in range(self.moba_groups, len(attend.groups)):
                    if g >= self.moba_groups + 2:
                        pool.wait_ge(attend.logits, g - 1)
                    first = attend.groups[g][0]
                    keys, n, t = first["width"], len(attend.groups[g]), first["tile"]
                    nc.gpsimd.tensor_tensor(
                        nat[:, 1, g % 2].rearrange("p (h k) -> p h k", h=n),
                        rel[:, first["head"]:first["head"] + 2 * n - 1:2, S - keys:S],
                        score[:, t, 0:keys].unsqueeze(1).to_broadcast([P, n, keys]),
                        ALU.add).then_inc(self.biased, 1)

        class Stick:
            def __init__(self, name, need):
                self.need = need
                self.scores = sem(name + "_scores")
                self.masked = sem(name + "_masked")
                self.logs = sem(name + "_logs")
                self.soft = sem(name + "_soft")
                self.sums = sem(name + "_sums")
                self.expo = sem(name + "_expo")
                self.weights = sem(name + "_weights")
                self.summed = sem(name + "_summed")
                self.fin = Finish([(t, b, 4 * b + 4, 0, 4) for b in range(2) for t in range(NT)],
                                  self.summed, False)
                self.ready = self.fin.ready

            def score(self, pe, g):
                if g >= 2:
                    pe.wait_ge(self.masked, g - 1)
                nc.tensor.matmul(bankA[g % 2][:, 0:S], kt[:, g, 0:P], qt[:, g], start=True, stop=True)
                nc.tensor.matmul(bankA[g % 2][:, S:S + P], kt[:, g, P:S], qt[:, g, P:S],
                                 start=True, stop=True).then_inc(self.scores, 1)

            def suffix(self, pe, g):
                pe.wait_ge(self.soft, g + 1)
                if g >= 2:
                    pe.wait_ge(self.expo, g - 1)
                suffix, ones = const[:, C_SUFFIX:C_SUFFIX + P], const[:, C_ONES:C_ONES + P]
                bank = bankT[g % 2]
                nc.tensor.matmul(bank[:, 0:S], suffix, pt[:, g % 2, 0:S], start=True, stop=False)
                nc.tensor.matmul(bank[:, P:S], ones, pt[:, g % 2, S:S + P], start=False, stop=True)
                nc.tensor.matmul(bank[:, S:S + P], suffix, pt[:, g % 2, S:S + P],
                                 start=True, stop=True).then_inc(self.sums, 1)

            def value(self, pe, g):
                pe.wait_ge(self.weights, g + 1)
                a, c = nat[:, 1, g % 2], slice(HD2 * (g % 4), HD2 * (g % 4) + HD2)
                vals = [v[:, k, HD2 * g:HD2 * (g + 1)] for k in range(2)]
                nc.tensor.matmul(bankD[0][g // 4][:, c], a[:, 0:P], vals[0], start=True, stop=True)
                nc.tensor.matmul(bankD[1][g // 4][:, c], a[:, P:S], vals[0], start=True, stop=False)
                nc.tensor.matmul(bankD[1][g // 4][:, c], a[:, S:S + P], vals[1], start=False,
                                 stop=True).then_inc(self.summed, 1)

            def tensor(self, pe):
                for s, value in self.need:
                    pe.wait_ge(s, value)
                self.score(pe, 0)
                for g in range(H2 + 3):
                    if g + 1 < H2:
                        self.score(pe, g + 1)
                    if g < H2:
                        self.suffix(pe, g)
                    if 1 <= g <= H2:
                        self.value(pe, g - 1)
                    for f in range(4):
                        if self.fin.fins[f][2] == g - 1:
                            self.fin.turn(pe, f)

            def scalar(self, act):
                nc.scalar.preload_act_table_set("natural_log_exp_and_others")
                for g in range(H2 + 4):
                    if g < H2:
                        e = pt[:, g % 2, 0:S + P]
                        act.wait_ge(self.masked, g + 1)
                        if g >= 2:
                            act.wait_ge(self.sums, g - 1)
                        own(act, act_own, nc.scalar.activation(e, lg[:, g % 2, 0:S + P], ACT.Abs))
                        own(act, act_own, nc.scalar.activation(e, e, ACT.Exp, scale=-1.0))
                        nc.scalar.activation(e, e, ACT.Ln, bias=col[:, 2:3]).then_inc(self.logs, 1)
                    if 1 <= g <= H2:
                        b = (g - 1) % 2
                        act.wait_ge(self.expo, g)
                        if g >= 3:
                            act.wait_ge(self.summed, g - 2)
                        nc.scalar.activation(nat[:, 1, b, 0:S + P], lg[:, b, 0:S + P], ACT.Exp)\
                            .then_inc(self.weights, 1)
                    for f in range(4):
                        if self.fin.fins[f][2] == g - 2:
                            self.fin.take_hi(act, f)

            def vector(self, dve):
                for g in range(H2 + 4):
                    if g < H2:
                        dve.wait_ge(self.scores, g + 1)
                        if g >= 2:
                            dve.wait_ge(self.weights, g - 1)
                        nc.vector.tensor_tensor(lg[:, g % 2, 0:S + P], bankA[g % 2][:, 0:S + P],
                                                const[:, C_STRICT:C_STRICT + S + P], ALU.add)\
                            .then_inc(self.masked, 1)
                    if 1 <= g <= H2:
                        b = (g - 1) % 2
                        dve.wait_ge(self.sums, g)
                        nc.vector.tensor_tensor(lg[:, b, 0:S + P], lg[:, b, 0:S + P], bankT[b][:, 0:S + P],
                                                ALU.add).then_inc(self.expo, 1)
                    if g < H2:
                        dve.wait_ge(self.logs, g + 1)
                        nc.vector.scalar_tensor_tensor(
                            out=pt[:, g % 2, 0:S + P], in0=lg[:, g % 2, 0:S + P], scalar=0.0,
                            in1=pt[:, g % 2, 0:S + P], op0=ALU.max, op1=ALU.add).then_inc(self.soft, 1)
                    for f in range(4):
                        if self.fin.fins[f][2] == g - 1:
                            self.fin.out_rows(dve, f)
                        if self.fin.fins[f][2] == g - 2:
                            self.fin.take_lo(dve, f)

            def sync(self, sp):
                pass

            def gpsimd(self, pool):
                pass

        class OutProject:
            def __init__(self, name, section, ks, stat_h, stat_l, need, residual=True, following=None):
                self.following = following
                self.name, self.n0, self.ks, self.need = name, AT[section], ks, need
                self.stat_h, self.stat_l, self.residual = stat_h, stat_l, residual
                self.full0 = NB * NT * len(out_projects)
                out_projects.append(name)
                self.chunks = len(ks) // 2
                ends[self.n0 + self.chunks // 2 - 1] = (out_full, self.full0 + NT, 0)
                ends[self.n0 + self.chunks - 1] = (out_full, self.full0 + NB * NT, 0)

            def tensor(self, pe):
                for s, value in self.need:
                    pe.wait_ge(s, value)
                for c in range(self.chunks):
                    take_chunk(pe, self.n0 + c)
                    for j in range(4):
                        i = 4 * c + j
                        block, k = i // len(self.ks), self.ks[i % len(self.ks)]
                        if self.following and i == 3 * len(self.ks) // 2:
                            norm_tensor(pe, self.following, 0)
                        for t in range(NT):
                            last = mm3(bankD[t][block], self.stat_h[:, k, t * P:(t + 1) * P],
                                       self.stat_l[:, k, t * P:(t + 1) * P], slot_of(self.n0 + c), j, TW,
                                       k == self.ks[0], k == self.ks[-1])
                            if k == self.ks[-1]:
                                last.then_inc(out_full, 1)
                    used(last, self.n0 + c)

            def scalar(self, act):
                tail_scalar(act, [self.n0 + c for c in range(self.chunks)], self.following)

            def vector(self, dve):
                chunks = [self.n0 + c for c in range(self.chunks)]
                if self.residual:
                    tail_vector(dve, chunks, self.following, out_full, 1.0, self.full0)
                else:
                    for n in chunks:
                        next_lo(dve, n)

            def sync(self, sp):
                for c in range(self.chunks):
                    load_chunk(sp, self.n0 + c)

            def gpsimd(self, pool):
                pass

        class Mixture:
            def __init__(self, attend):
                self.attend = attend
                self.full = sem("gate_full")
                self.raw = sem("gate_raw")
                self.gate = sem("gate_sigmoid")
                self.mixed = sem("gate_mixed")
                self.bias_in = sem("gate_bias_in")
                self.ps = sem("mix_ps")
                self.hi = sem("mix_hi")
                self.lo = sem("mix_lo")
                self.branch = []
                for b, section in enumerate(("br_a", "br_b")):
                    need = [attend.ready] if b == 0 else [(self.mixed, NB * NT)]
                    self.branch.append(OutProject(section, section, list(range(4 * b, 4 * b + 4)),
                                                  ot_h, ot_l, need, residual=False))
                for u in range(4):
                    ends[self.chunk(u) + 1] = (self.full, NT * (u + 1), 0)
                self.ready = (self.lo, 4)

            def chunk(self, u):
                return AT["gate_a" if u < 2 else "gate_b"] + 2 * (u % 2)

            def tensor(self, pe):
                for u in range(4):
                    if u % 2 == 0:
                        self.branch[u // 2].tensor(pe)
                    for c in range(2):
                        take_chunk(pe, self.chunk(u) + c)
                        for t in range(NT):
                            if c == 0 and u > 0:
                                pe.wait_ge(self.raw, NT * (u - 1) + t + 1)
                            for j in range(4):
                                k = 4 * c + j
                                last = mm3(bankA[t], xt_h[:, k, t * P:(t + 1) * P],
                                           xt_l[:, k, t * P:(t + 1) * P], slot_of(self.chunk(u) + c), j, TW,
                                           k == 0, k == KC - 1)
                            if c == 1:
                                last.then_inc(self.full, 1)
                        used(last, self.chunk(u) + c)
                pe.wait_ge(self.mixed, 4 * NT)
                for pair, bank in enumerate(bankT + bankA):
                    for j in range(2):
                        for t in range(NT):
                            k = 2 * pair + j
                            last = nc.tensor.transpose(bank[:, j * S + t * P:j * S + (t + 1) * P],
                                                       v[:, t, k * P:(k + 1) * P], ident)
                    last.then_inc(self.ps, 1)

            def scalar(self, act):
                nc.scalar.preload_act_table(ACT.Sigmoid)
                for u in range(4):
                    if u % 2 == 0:
                        self.branch[u // 2].scalar(act)
                    for t in range(NT):
                        act.wait_ge(self.raw, NT * u + t + 1)
                        nc.scalar.activation(lg[:, t], lg[:, t], ACT.Sigmoid).then_inc(self.gate, 1)
                    for c in range(2):
                        next_hi(act, self.chunk(u) + c)
                for pair, bank in enumerate(bankT + bankA):
                    act.wait_ge(self.ps, pair + 1)
                    nc.scalar.activation(xt_h[:, 2 * pair:2 * pair + 2],
                                         bank.rearrange("p (k s) -> p k s", k=2), ACT.Copy).then_inc(self.hi, 1)

            def vector(self, dve):
                dve.wait_ge(self.bias_in, 16)
                for u in range(4):
                    b, block = u // 2, u % 2
                    if block == 0:
                        self.branch[b].vector(dve)
                    for t in range(NT):
                        if u > 0:
                            dve.wait_ge(self.mixed, NT * (u - 1) + t + 1)
                        dve.wait_ge(self.full, NT * u + t + 1)
                        nc.vector.scalar_tensor_tensor(out=lg[:, t], in0=bankA[t], scalar=rms("mix", t),
                                                       in1=nat[:, b, block], op0=ALU.mult, op1=ALU.add)\
                            .then_inc(self.raw, 1)
                    for c in range(2):
                        next_lo(dve, self.chunk(u) + c)
                    for t in range(NT):
                        dve.wait_ge(self.gate, NT * u + t + 1)
                        dve.wait_ge(out_full, self.branch[b].full0 + NT * block + t + 1)
                        to = v[:, t, block * TW:(block + 1) * TW]
                        if b == 0:
                            nc.vector.tensor_tensor(to, lg[:, t], bankD[t][block], ALU.mult)\
                                .then_inc(self.mixed, 1)
                        else:
                            own(dve, dve_own, nc.vector.tensor_tensor(lg[:, t], lg[:, t], bankD[t][block],
                                                                      ALU.mult))
                            nc.vector.tensor_tensor(to, to, lg[:, t], ALU.add).then_inc(self.mixed, 1)
                for pair, bank in enumerate(bankT + bankA):
                    dve.wait_ge(self.hi, pair + 1)
                    nc.vector.tensor_tensor(xt_l[:, 2 * pair:2 * pair + 2],
                                            bank.rearrange("p (k s) -> p k s", k=2),
                                            xt_h[:, 2 * pair:2 * pair + 2].bitcast(F32),
                                            ALU.subtract).then_inc(self.lo, 1)

            def sync(self, sp):
                for u in range(4):
                    if u % 2 == 0:
                        self.branch[u // 2].sync(sp)
                    for c in range(2):
                        load_chunk(sp, self.chunk(u) + c)

            def gpsimd(self, pool):
                pool.wait_ge(rows_ps, self.attend.fin.f0 + 4)
                pool.dma_start(nat[:, :, :, :].rearrange("p a b n -> p (a b n)"),
                               dram["b_gate"].partition_broadcast(P)).then_inc(self.bias_in, 16)

        class Norm:

            def __init__(self, name, need=()):
                self.name, self.mem, self.need = name, name.startswith("mem"), need

            def tensor(self, pe):
                if self.mem:
                    for s, value in self.need:
                        pe.wait_ge(s, value)
                    norm_tensor(pe, self.name, 0)
                    norm_tensor(pe, self.name, 1)

            def scalar(self, act):
                if self.mem:
                    norm_scalar(act, self.name, 0)
                norm_scalar(act, self.name, 1)
                if not self.mem:
                    rms_scalar(act, self.name)

            def vector(self, dve):
                if self.mem:
                    norm_vector(dve, self.name, 0)
                norm_vector(dve, self.name, 1)
                if not self.mem:
                    root_vector(dve, self.name)

            def sync(self, sp):
                pass

            def gpsimd(self, pool):
                pass

        class Memory:

            def __init__(self, attend):
                self.attend = attend
                self.squared = sem("mem_squared")
                self.rooted = sem("mem_rooted")
                self.c = 2 * NORM["mem0"]

            def tensor(self, pe):
                pass

            def scalar(self, act):
                act.wait_ge(mem_in, 16)
                for t in range(NT):
                    nc.scalar.activation(ot_h[:, 4 * t:4 * t + 4].rearrange("p k s -> p (k s)"), mem[:, t],
                                         ACT.Square, scale=D ** -0.5,
                                         accum_out=ms[:, self.c + t:self.c + t + 1]).then_inc(self.squared, 1)

            def vector(self, dve):
                dve.wait_ge(self.squared, NT)
                rsqrt(dve, ms[:, self.c:self.c + 2], rs[:, self.c:self.c + 2], 1.0, EPS, 2)\
                    .then_inc(self.rooted, 1)

            def sync(self, sp):
                pass

            def gpsimd(self, pool):
                pool.wait_ge(self.attend.logits, len(self.attend.groups))
                pool.dma_start(mem, dram["mem"]).then_inc(mem_in, 16)

        onehot = kt[0:NBUCK + 1, 0:2].rearrange("p k s -> p (k s)")[:, 0:RELW + 1]
        tab = qt[0:NBUCK + 1, 0, 0:16]
        byd = qt[0:16, 2:4].rearrange("p k s -> p (k s)")[:, 0:RELW + 1]

        class Tables:
            TWO_PI = 6.283185307179586
            C1 = 6.28125
            C2 = float(np.float32(TWO_PI - C1))
            C3 = TWO_PI - C1 - C2

            def __init__(self):
                self.in_ = sem("tables_in")
                self.neg = sem("tables_neg")
                self.ps = sem("tables_ps")
                self.sb = sem("tables_sb")
                self.out = sem("tables_out")
                self.rel_in = sem("rel_in")
                self.angle = sem("tables_angle")
                self.trig = sem("tables_trig")
                self.scratch = nc.dram_tensor("bias_by_distance", (16, P, RELW + 1), F32, kind="Internal").ap()

            def gpsimd(self, pool):
                pool.dma_start(onehot, dram["consts"][0:NBUCK + 1, C_BUCK:NCONST])\
                    .then_inc(self.in_, 16)
                pool.dma_start(tab[0:NBUCK], dram["rel_bias"]).then_inc(self.in_, 16)
                pool.dma_start(pos[:, 0:NT].bitcast(I32), dram["positions"]).then_inc(self.in_, 16)
                pool.wait_ge(self.sb, 1)
                pool.dma_start(self.scratch, byd.unsqueeze(1).to_broadcast(
                    [16, P, RELW + 1])).then_inc(self.out, 16)
                pool.wait_ge(self.out, 16)
                spread = bass.AP(tensor=self.scratch.tensor, offset=P - 1,
                                 ap=[[RELW, P], [P * (RELW + 1), 16], [1, S]])
                pool.dma_start(rel[:], spread).then_inc(self.rel_in, 16)

            def tensor(self, pe):
                pe.wait_ge(self.in_, 48)
                pe.wait_ge(self.neg, 1)
                nc.tensor.matmul(bankD[1][1][0:16, 0:RELW + 1], tab,
                                 onehot, start=True, stop=True).then_inc(self.ps, 1)

            def scalar(self, act):
                act.wait_ge(self.ps, 1)
                nc.scalar.activation(byd, bankD[1][1][0:16, 0:RELW + 1], ACT.Copy)\
                    .then_inc(self.sb, 1)
                act.wait_ge(self.angle, 1)
                nc.scalar.activation(trig[:], v[:, 0, 0:4 * HALF].rearrange(
                    "p (a t d) -> p a t d", a=2, t=NT), ACT.Sin).then_inc(self.trig, 1)

            def vector(self, dve):
                dve.wait_ge(self.in_, 48)
                dve.wait_ge(consts_in, 32)
                w = 2 * NT * HALF
                angle, turns, red = v[:, 0, 256:256 + w], v[:, 0, 512:512 + w], v[:, 0, 0:w]
                own(dve, dve_own, nc.vector.tensor_copy(pos[:, 2:4], pos[:, 0:NT].bitcast(I32)))
                for t in range(NT):
                    for a in range(2):
                        last = nc.vector.tensor_scalar(
                            angle[:, (2 * a + t) * HALF:(2 * a + t + 1) * HALF],
                            const[:, C_FREQ:C_FREQ + HALF], pos[:, 2 + t:3 + t], None, ALU.mult)
                own(dve, dve_own, last)
                for a, quarter in enumerate((0.25, 0.0)):
                    part = slice(a * w // 2, (a + 1) * w // 2)
                    last = nc.vector.tensor_scalar(turns[:, part], angle[:, part], 1.0 / self.TWO_PI, quarter,
                                                   ALU.mult, ALU.add)
                own(dve, dve_own, last)
                whole = v[:, 0, 768:768 + w].bitcast(I32)
                own(dve, dve_own, nc.vector.tensor_copy(whole, turns))
                own(dve, dve_own, nc.vector.tensor_copy(turns, whole))
                step = angle
                for c in (self.C1, self.C2, self.C3):
                    own(dve, dve_own, nc.vector.scalar_tensor_tensor(out=red, in0=turns, scalar=-c, in1=step,
                                                                     op0=ALU.mult, op1=ALU.add))
                    step = red
                own(dve, dve_own, nc.vector.tensor_scalar(red[:, 0:w // 2], red[:, 0:w // 2], self.TWO_PI / 4, None,
                                                          ALU.add))
                nc.vector.tensor_scalar(red, red, 3.1415925, -3.1415925, ALU.min, ALU.max)\
                    .then_inc(self.angle, 1)

            def sync(self, sp):
                pass

        class Final:

            def __init__(self):
                self.gain_in = sem("final_gain_in")
                self.made = sem("final_rows")
                self.stored = sem("final_stored")

            def gpsimd(self, pool):
                pool.wait_ge(h_ready, 32)
                pool.dma_start(qt[:, 0:4].rearrange("p k s -> p (k s)"),
                               dram["norm_final"].partition_broadcast(P)).then_inc(self.gain_in, 16)

            def tensor(self, pe):
                pass

            def scalar(self, act):
                rms_scalar(act, "final")

            def vector(self, dve):
                root_vector(dve, "final")
                dve.wait_ge(self.gain_in, 16)
                dve.wait_ge(rs_ready, RMS_AT["final"])
                for t in range(NT):
                    nc.vector.scalar_tensor_tensor(out=v[:, t], in0=h[:, t], scalar=rms("final", t),
                                                   in1=qt[:, 0:4].rearrange("p k s -> p (k s)"),
                                                   op0=ALU.mult, op1=ALU.mult).then_inc(self.made, 1)

            def sync(self, sp):
                rows = out.rearrange("(t p) d -> p t d", p=P)
                for t in range(NT):
                    sp.wait_ge(self.made, t + 1)
                    sp.dma_start(rows[:, t], v[:, t]).then_inc(self.stored, 16)
                sp.wait_ge(self.stored, 16 * NT)

        def row(name):
            return lambda t: rms(name, t)

        def latent_row(i):
            c = 2 * len(NORMS) + 2 * i
            return lambda t: rs[:, c + t:c + t + 1]

        def same_half(per):
            return [list(range(h0 + odd, h0 + 2 * per, 2)) for h0 in range(0, 8, 2 * per) for odd in range(2)]

        def moba_dsa():
            groups, fins = [], []
            for b in (1, 0):
                for t in range(NT):
                    keys, per = (t + 1) * P, 4 // (t + 1)
                    for heads in same_half(per):
                        group = []
                        for i, hd in enumerate(heads):
                            half = slice(64 * (hd % 2), 64 * (hd % 2) + 64)
                            k4 = 4 * b + hd // 2
                            bias = rel[:, 8 * b + hd, S - keys:S] if b else \
                                nat[:, 1, len(groups) % 2, i * keys:(i + 1) * keys]
                            group.append(dict(
                                at=i * keys, width=keys, tile=t, head=8 * b + hd, bias=bias,
                                qk=[(qt[half, k4, t * P:(t + 1) * P], kt[half, k4, 0:keys])],
                                v=[v[:, j, TW * b + HD1 * hd:TW * b + HD1 * (hd + 1)] for j in range(t + 1)],
                                out=bankD[t][b][:, HD1 * hd:HD1 * (hd + 1)], col=16 * b + 8 * t + hd))
                        groups.append(group)
                    fins.append((t, b, len(groups) - 1, 16 * b + 8 * t, H1))
            return groups, fins, len(groups) // 2

        def mla_groups():
            groups, fins = [], []
            for t in range(NT):
                keys, per = (t + 1) * P, 4 // (t + 1)
                for heads in same_half(per):
                    group = []
                    for i, hd in enumerate(heads):
                        half, s = slice(64 * (hd % 2), 64 * (hd % 2) + 64), slice(t * P, (t + 1) * P)
                        group.append(dict(
                            at=i * keys, width=keys, tile=t, head=hd,
                            bias=const[:, C_CAUSAL + S - keys:C_CAUSAL + S],
                            qk=[(qt[:, hd, s], kt[:, hd, 0:keys]),
                                (pet[half, hd // 2, s], pet[half, 4, 0:keys])],
                            v=[v[:, j, HD2 * hd:HD2 * (hd + 1)] for j in range(t + 1)],
                            out=bankD[t][hd // 4][:, HD2 * (hd % 4):HD2 * (hd % 4) + HD2], col=8 * t + hd))
                    groups.append(group)
                    if heads[-1] == 7:
                        fins += [(t, b, len(groups) - 1, 8 * t + 4 * b, 4) for b in ((1,) if t else (0, 1))]
                    elif heads[-1] == 3:
                        fins.append((t, 0, len(groups) - 1, 8 * t, 4))
            return groups, fins

        def mem_groups():
            groups, fins = [], []
            for t in range(NT):
                for h0 in (0, 2):
                    groups.append([dict(
                        at=i * S, width=S, bias=const[:, C_CAUSAL:C_CAUSAL + 1].to_broadcast([P, S]),
                        qk=[(qt[:, hd, t * P:(t + 1) * P], rel[:, hd])],
                        v=[mem_v[:, j, HD2 * hd:HD2 * (hd + 1)] for j in range(2)],
                        out=bankD[t][0][:, HD2 * hd:HD2 * (hd + 1)], col=4 * t + hd)
                        for i, hd in enumerate((h0, h0 + 1))])
                fins.append((t, 0, len(groups) - 1, 4 * t, NXH))
            return groups, fins

        all8 = list(range(KC))

        def unit(kind, width=TW, chunks=(4, 4), **kw):
            return Unit(kind, list(range(sum(chunks))), width, chunks, **kw)

        tables = Tables()
        ffn1 = Ffn("ffn1", 11, 2, True, 0.5, "mix")

        mix = row("mix")
        mix_units = [unit("idx", 324, (2, 2, 2, 2), rows=mix)]
        for to, base, g, sc in ((qt, 4, QG_B, 0.125), (kt, 4, KG_B, 1.0), (qt, 0, QG_A, 0.125), (kt, 0, KG_A, 1.0)):
            mix_units.append(unit("qk", rows=mix, to=to, base=base, gains=g, scale=sc))
        mix_units += [unit("v", rows=mix, base=TW), unit("v", rows=mix, base=0)]
        mix_in = Project("mix_in", "idx", mix_units, xt_h, xt_l, norm="mix")
        groups, fins, n_moba = moba_dsa()
        mix_attend = Attend("mix", groups, fins, [mix_in.turned_ready, mix_in.evac_ready, (tables.rel_in, 16)],
                            Select(n_moba))
        mixture = Mixture(mix_attend)
        mix_out = OutProject("mix_out", "w_out", all8, xt_h, xt_l, [mixture.ready], following="ffn2")
        mem_root = Memory(mix_attend)

        ffn2 = Ffn("ffn2", 11, 2, True, 0.5, "mla")

        latent_units = [unit("latent", QL, rows=row("mla"), gains=QG_L, base=0),
                        unit("dkv", KL + ROPE, rows=row("mla"), gains=KG_L, base=3)]
        latent_units[0].ks_out, latent_units[1].ks_out = 3, 2
        mla_down = Project("mla_down", "dq", latent_units, xt_h, xt_l, norm="mla")
        qrow, krow = latent_row(0), latent_row(1)
        up_units = [unit("q", chunks=(3,), rows=qrow, to=qt, base=4 * i, scale=MLA_SCALE) for i in range(2)]
        up_units.append(unit("pe", chunks=(3,), rows=qrow, to=pet, scale=MLA_SCALE))
        for kind, base in (("q", 0), ("q", 4), ("v", 0), ("v", TW)):
            up_units.append(Unit(kind, [3, 4], TW, (2,), rows=krow, to=kt, base=base))
        mla_up = Project("mla_up", "uq", up_units, ot_h, ot_l, need=[mla_down.split_ready, mla_down.turned_ready],
                         scaled=(mla_down.rooted, 1))

        def memory_keys(i, need):
            r = row("mem0")
            kv = Project(f"mem_kv{i}", f"xkv{i}",
                         [unit("q", rows=r, to=rel), unit("v", rows=r, vals=mem_v)], xt_h, xt_l,
                         need=[(xt_lo, 4 * NORM[f"mem{i}"] + 4)], scaled=(mem_root.rooted, 1))
            return [Norm(f"mem{i}", need), kv]

        def memory(i, kv, following):
            q = Project(f"mem_q{i}", f"xq{i}", [unit("q", rows=row(f"cross{i}"), to=qt, scale=MEM_SCALE)],
                        xt_h, xt_l, norm=f"cross{i}")
            attend = Attend(f"mem{i}", *mem_groups(), [kv.turned_ready, kv.evac_ready, q.turned_ready])
            out = OutProject(f"mem_out{i}", f"xo{i}", all8[:4], ot_h, ot_l, [attend.ready], following=f"mlp{i}")
            return [Norm(f"cross{i}"), q, attend, out, Ffn(f"mlp{i}", 8, 4, False, 1.0, following)]

        mem_keys0 = memory_keys(0, [mla_up.turned_ready, mla_up.evac_ready])
        groups, fins = mla_groups()
        mla_attend = Attend("mla", groups, fins, [mem_keys0[1].turned_ready, mem_keys0[1].evac_ready])
        mla_out = OutProject("mla_out", "mla_o", all8, ot_h, ot_l, [mla_attend.ready], following="cross0")
        memory0 = memory(0, mem_keys0[1], "sb")
        sb_row = row("sb")
        sb_units = [unit("q", rows=sb_row, to=qt, base=4 * i, scale=SB_SCALE) for i in range(2)]
        sb_units += [unit("q", rows=sb_row, to=kt, base=4 * i) for i in range(2)]
        sb_units += [unit("v", rows=sb_row, base=TW * i) for i in range(2)]
        sb_in = Project("sb_in", "sb_qkv", sb_units, xt_h, xt_l, norm="sb")
        mem_keys1 = memory_keys(1, [sb_in.turned_ready, sb_in.evac_ready])
        stick = Stick("sb", [mem_keys1[1].turned_ready, mem_keys1[1].evac_ready])
        sb_out = OutProject("sb_out", "sb_o", all8, ot_h, ot_l, [stick.ready], following="cross1")

        phases = [ffn1, Norm("mix"), mix_in, mix_attend, mixture, mix_out, mem_root, ffn2,
                  Norm("mla"), mla_down, mla_up] + mem_keys0 + [mla_attend, mla_out]
        phases += memory0
        phases += [Norm("sb"), sb_in] + mem_keys1 + [stick, sb_out]
        phases += memory(1, mem_keys1[1], None)
        phases.append(Final())

        block = ctx.enter_context(nc.Block())

        @block.sync
        def _(sp):
            sp.dma_start(h[:], dram["x"]).then_inc(x_in, 16)
            sp.dma_start(gain[:], dram["gains"]).then_inc(consts_in, 16)
            for phase in phases:
                phase.sync(sp)

        @block.gpsimd
        def _(pool):
            tables.gpsimd(pool)
            for phase in phases:
                phase.gpsimd(pool)

        @block.scalar
        def _(act):
            act.dma_start(const[:], dram["consts"][:, 0:C_BUCK]).then_inc(consts_in, 16)
            act.wait_ge(consts_in, 32)
            act.wait_ge(col_set, 3)
            norm_scalar(act, "ffn1", 0)
            for n in range(RING):
                split_hi(act, n)
            for phase in phases:
                phase.scalar(act)

        @block.vector
        def _(dve):
            nc.vector.memset(col[:, 0:1], EPS).then_inc(col_set, 1)
            nc.vector.memset(col[:, 1:2], HD1 * EPS).then_inc(col_set, 1)
            nc.vector.memset(col[:, 2:3], 1.0).then_inc(col_set, 1)
            nc.vector.memset(tab[NBUCK:NBUCK + 1], NEG).then_inc(tables.neg, 1)
            norm_vector(dve, "ffn1", 0)
            for n in range(RING):
                split_lo(dve, n)
            for phase in phases:
                phase.vector(dve)

        @block.tensor
        def _(pe):
            pe.wait_ge(consts_in, 32)
            norm_tensor(pe, "ffn1", 0)
            for phase in phases:
                phase.tensor(pe)


def kernel(**inputs):
    import concourse.bacc as bacc
    from concourse.bass_utils import run_bass_kernel_spmd

    nc = bacc.Bacc("TRN2", target_bir_lowering=False, num_devices=1)
    arrays = host_arrays(inputs)
    dram = {n: nc.dram_tensor(n, a.shape, mybir.dt.from_np(a.dtype), kind="ExternalInput").ap()
            for n, a in arrays.items()}
    out = nc.dram_tensor("out", (S, D), F32, kind="ExternalOutput").ap()
    build(nc, dram, out)
    result = run_bass_kernel_spmd(nc, [arrays], core_ids=[0])
    return result.results[0]["out"].reshape(1, S, D)
```

```python
from contextlib import ExitStack

import numpy as np

import concourse.bass as bass
from concourse import mybir

F32 = mybir.dt.float32
F32R = mybir.dt.float32r
I32 = mybir.dt.int32
ALU = mybir.AluOpType
ACT = mybir.ActivationFunctionType
AX = mybir.AxisListType

P = 128
S = 256
NT = S // P
D = 1024
KC = D // P
TW = 512
NB = D // TW
RING = 4
EPS = 1e-6
NEG = -1e30
TAKEN = -3e38
FF1, FF2 = 2816, 4096
H1, HD1 = 8, 64
TOPK = 64
H2, HD2 = 8, 128
ROPE, HALF = 64, 32
MLA_SCALE = (HD2 + ROPE) ** -0.5
SB_SCALE = HD2 ** -0.5
MEM_SCALE = 128 ** -0.5
NXH = 4
QL, KL = 384, 256
NPARTS, NBUCK = 4, 32

NORMS = ["ffn1", "mix", "ffn2", "mla", "mem0", "cross0", "mlp0", "sb", "mem1", "cross1", "mlp1", "final"]
NORM = {n: i for i, n in enumerate(NORMS)}
RMS_AT = {n: i + 1 for i, n in enumerate(n for n in NORMS if not n.startswith("mem"))}
QG_A, KG_A, QG_B, KG_B, QG_L, KG_L = 96, 97, 98, 99, 100, 103
NGAIN = 105


def weight_plan():
    plan, at = [], {}

    def add(section, array, tiles, width=TW):
        at.setdefault(section, len(plan))
        first = sum(1 for c in plan if c[0] == array)
        plan.extend((array, first + i, n, width) for i, n in enumerate(tiles))

    def ffn(name, steps, out_tiles):
        add(name, name + "_first", [2] * 4)
        add(name + "_mid", name + "_mid", [(8 + out_tiles) // 4] * 4 * (steps - 1))
        add(name + "_tail", name + "_tail", [out_tiles // 4] * 4)

    ffn("ffn1", 11, 4)
    add("qkv", "w_qkv", [4] * 2)
    add("idx", "w_idx", [2] * 4, 324)
    add("qkv_rest", "w_qkv", [4] * 10)
    add("gate_b0", "w_gate_b", [4] * 2)
    add("gate_b1", "w_gate_b", [4] * 2)
    add("gate_a0", "w_gate_a", [4] * 2)
    add("br_a", "w_br_a", [4] * 2)
    add("gate_a1", "w_gate_a", [4] * 2)
    add("br_b", "w_br_b", [4] * 2)
    add("w_out", "w_out", [4] * 4)
    ffn("ffn2", 11, 4)
    add("dq", "w_dq", [4] * 2, QL)
    add("dkv", "w_dkv", [4] * 2, KL + ROPE)
    add("uq", "w_uq", [3] * 3)
    add("ukv", "w_ukv", [2] * 4)
    for i in range(2):
        if i == 1:
            add("sb_qkv", "w_sb_qkv", [4] * 12)
        for part in ("keys", "values"):
            add(f"mem_{part}{i}", f"w_xkv{i}", [4] * 2)
        name = ("mla_o", "sb_o")[i]
        add(name, "w_" + name, [4] * 4)
        add(f"xq{i}", f"w_xq{i}", [4] * 2)
        add(f"xo{i}", f"w_xo{i}", [4] * 2)
        ffn(f"mlp{i}", 8, 8)
    return plan, at


PLAN, AT = weight_plan()


def t5_buckets(dist):
    d = np.maximum(dist, 0)
    large = 16 + (np.log(np.maximum(d, 1) / 16.0) / np.log(8.0) * 16).astype(np.int64)
    return np.where(d < 16, d, np.minimum(large, 31))


C_ID, C_CAUSAL, C_STRICT, C_SUFFIX, C_ONES, C_FREQ, C_BUCK = 0, 128, 384, 768, 896, 1024, 1056
RELW = 383
NCONST = C_BUCK + 384


def constants():
    c = np.zeros((P, NCONST), np.float32)
    row, col = np.arange(P)[:, None], np.arange(P)[None, :]
    c[:, C_ID:C_ID + P] = row == col
    c[:, C_CAUSAL + P:C_CAUSAL + 2 * P] = np.where(col <= row, 0.0, NEG)
    strict = np.where(row < col, 0.0, NEG)
    c[:, C_STRICT:C_STRICT + P] = strict
    c[:, C_STRICT + 2 * P:C_STRICT + 3 * P] = strict
    c[:, C_SUFFIX:C_SUFFIX + P] = np.where(row >= col, -1.0, 0.0)
    c[:, C_ONES:C_ONES + P] = -1.0
    exponent = -np.arange(0, ROPE, 2, dtype=np.float32) / np.float32(ROPE)
    c[:, C_FREQ:C_FREQ + HALF] = (10000.0 ** exponent.astype(np.float64)).astype(np.float32)
    dist = 255 - np.arange(RELW)
    for x, (d, b) in enumerate(zip(dist, t5_buckets(dist))):
        c[b if d >= 0 else NBUCK, C_BUCK + x] = 1.0
    return c


def chunked(a, tiles):
    u, p, t, w = a.shape
    return np.ascontiguousarray(
        a.reshape(u, p, t // tiles, tiles * w).transpose(0, 2, 1, 3).reshape(-1, p, tiles * w))


def by_block(w, width=TW):
    k, n = w.shape
    return w.reshape(k // P, P, n // width, width).transpose(2, 1, 0, 3)


def by_row(w, steps):
    k, n = w.shape
    return w.reshape(steps, k // P // steps, P, NB, TW).transpose(0, 2, 1, 3, 4).reshape(steps, P, -1, TW)


def ffn_arrays(name, up, down):
    n, tiles = up.shape[0], down.shape[2]
    last = down[n - 1:].reshape(1, P, tiles // NB, NB, TW).transpose(0, 1, 3, 2, 4).reshape(1, P, tiles, TW)
    return {name + "_first": chunked(up[:1], 2),
            name + "_mid": chunked(np.concatenate([up[1:], down[:n - 1]], axis=2), (8 + tiles) // 4),
            name + "_tail": chunked(last, tiles // 4)}


def host_arrays(x):
    out = {"x": np.ascontiguousarray(x["x"][0].reshape(NT, P, D).transpose(1, 0, 2)),
           "mem": np.ascontiguousarray(x["mem_2"][0].reshape(NT, P, D).transpose(1, 0, 2)),
           "positions": np.ascontiguousarray(x["positions_2"].astype(np.int32)[0].reshape(NT, P).T),
           "consts": constants()}
    for n in ("ffn1", "ffn2"):
        gu = x[n + "_w_gu"][0]
        up = gu.reshape(KC, P, 2, 11, 256).transpose(3, 1, 0, 2, 4).reshape(11, P, KC, TW)
        out.update(ffn_arrays(n, up, by_row(x[n + "_w_down"][0], 11)))
    w = x["w_in"][0]
    out["w_idx"] = chunked(by_block(w[:, 3072:3396], 324), 2)
    order = [3, 4, 0, 1, 5, 2]
    out["w_qkv"] = chunked(by_block(w[:, :3072])[order], 4)
    gates = by_block(w[:, 3396:])
    out["w_gate_a"], out["w_gate_b"] = chunked(gates[:2], 4), chunked(gates[2:], 4)
    out["w_br_a"] = chunked(by_block(x["w_branch_dsa"][0]), 4)
    out["w_br_b"] = chunked(by_block(x["w_branch_moba"][0]), 4)
    out["w_out"] = chunked(by_block(x["w_out"][0]), 4)
    dkv = x["mla_w_dkv_2"][0]
    out["w_dq"] = chunked(by_block(dkv[:, :QL], QL), 4)
    out["w_dkv"] = chunked(by_block(dkv[:, QL:], KL + ROPE), 4)
    uq = x["mla_w_uq_2"][0].reshape(QL, H2, HD2 + ROPE)
    parts = [uq[:, :, :HD2], uq[:, :, HD2:HD2 + HALF], uq[:, :, HD2 + HALF:]]
    out["w_uq"] = chunked(by_block(np.concatenate([p.reshape(QL, -1) for p in parts], axis=1)), 3)
    ukv = x["mla_w_ukv_2"][0].reshape(KL, H2, 2, HD2).transpose(0, 2, 1, 3).reshape(KL, -1)
    out["w_ukv"] = chunked(by_block(ukv), 2)
    out["w_mla_o"] = chunked(by_block(x["mla_w_o_2"][0]), 4)
    out["w_sb_qkv"] = chunked(by_block(x["sb_w_qkv_2"][0]), 4)
    out["w_sb_o"] = chunked(by_block(x["sb_w_o_2"][0]), 4)
    for i in range(2):
        out[f"w_xkv{i}"] = chunked(by_block(x["xa_w_kv_2"][i]), 4)
        out[f"w_xq{i}"] = chunked(by_block(x["xa_w_q_2"][i]), 4)
        out[f"w_xo{i}"] = chunked(by_block(x["xa_w_o_2"][i]), 4)
        out.update(ffn_arrays(f"mlp{i}", by_block(x["mlp_w_in_2"][i]), by_row(x["mlp_w_out_2"][i], 8)))
    gains = [x["ffn1_norm"][0], x["mix_norm"][0], x["ffn2_norm"][0], x["norm_mix_2"][0],
             x["norm_mem_2"][0], x["norm_cross_2"][0], x["norm_mlp_2"][0], x["norm_mix_2"][1],
             x["norm_mem_2"][1], x["norm_cross_2"][1], x["norm_mlp_2"][1], x["norm_final_2"]]
    columns = [g.reshape(KC, P).T for g in gains]
    for n in ("q_norm_dsa", "k_norm_dsa", "q_norm_moba", "k_norm_moba"):
        columns.append(np.concatenate([x[n][0], x[n][0]])[:, None])
    columns += [x["mla_g_q_2"][0].reshape(-1, P).T, x["mla_g_kv_2"][0].reshape(-1, P).T]
    out["gains"] = np.ascontiguousarray(np.concatenate(columns, axis=1))
    out["b_gate"] = np.ascontiguousarray(x["b_gate"])
    out["norm_final"] = np.ascontiguousarray(x["norm_final_2"][None, :])
    out["rel_bias"] = np.ascontiguousarray(x["rel_bias"])
    return out


class Count:

    def __init__(self, sem):
        self.sem, self.n = sem, 0

    def inc(self, ins):
        ins.then_inc(self.sem, 1)
        self.n += 1
        return self.n


def build(nc, dram, out):
    ctx = ExitStack()
    with ctx:
        def sb(name, shape, dt=F32):
            return ctx.enter_context(nc.sbuf_tensor(name, shape, dt))

        def sem(name):
            return ctx.enter_context(nc.semaphore(name))

        w_raw = sb("w_raw", [P, RING, 4 * TW])
        whi = sb("whi", [P, RING, 4 * TW], F32R)
        wlo = sb("wlo", [P, RING, 4 * TW], F32R)
        h = sb("h", [P, NT, D])
        xt_h = sb("xt_h", [P, KC, S], F32R)
        xt_l = sb("xt_l", [P, KC, S], F32R)
        ot_h = sb("ot_h", [P, KC, S], F32R)
        ot_l = sb("ot_l", [P, KC, S], F32R)
        qt = sb("qt", [P, KC, S])
        kt = sb("kt", [P, KC, S])
        v = sb("v", [P, NT, D])
        pet = sb("pet", [P, 5, S])
        rel = sb("rel", [P, 16, S])
        mem = rel[:, 8:16].rearrange("p (t a) s -> p t (a s)", t=NT)
        mem_v = rel[:, 4:8].rearrange("p (t a) s -> p t (a s)", t=NT)
        nat = sb("nat", [P, 2, NT, TW])
        lg = sb("lg", [P, 2, TW])
        pt = sb("pt", [P, 2, TW])
        score = sb("score", [P, NT, S])
        const = sb("const", [P, C_BUCK])
        gain = sb("gain", [P, NGAIN])
        ms = sb("ms", [P, 2 * len(NORMS) + 4])
        rs = sb("rs", [P, 2 * len(NORMS) + 4])
        one = sb("one", [P, 1])
        hs = sb("hs", [P, 2, NT * 8])
        newton = sb("newton", [P, NT * 8])
        nmax = sb("nmax", [P, 32])
        rsum = sb("rsum", [P, 32])
        rinv = sb("rinv", [P, 32])
        top8 = sb("top8", [P, NT, 8])
        wi = sb("wi", [P, NT, NPARTS])
        trig = sb("trig", [P, 2, NT, HALF])
        pos = sb("pos", [P, 4])

        ps = ctx.enter_context(nc.psum_tensor("ps", [P, 8, TW], F32))
        bankA = [ps[:, 0], ps[:, 1]]
        bankT = [ps[:, 2], ps[:, 3]]
        bankD = [[ps[:, 4], ps[:, 5]], [ps[:, 6], ps[:, 7]]]
        ident = const[:, C_ID:C_ID + P]

        w_loaded = [sem(f"w_loaded{s}") for s in range(RING)]
        w_hi = sem("w_hi")
        w_lo = sem("w_lo")
        w_used = sem("w_used")
        consts_in = sem("consts_in")
        x_in = [sem(f"x_in{block}") for block in range(NB)]
        one_set = sem("one_set")
        mem_in = sem("mem_in")
        h_ready = sem("h_ready")
        xt_ps = sem("xt_ps")
        xt_hi = sem("xt_hi")
        xt_lo = sem("xt_lo")
        ms_ready = sem("ms_ready")
        rs_ready = sem("rs_ready")
        rows_made = sem("rows_made")
        rows_ps = sem("rows_ps")
        rows_hi = sem("rows_hi")
        rows_lo = sem("rows_lo")
        all_fins = []
        fill_full = sem("fill_full")
        fill_copied = sem("fill_copied")
        fill_ps = sem("fill_ps")
        fill_taken = sem("fill_taken")
        fills, turned_fills = [], []
        out_full = sem("out_full")
        out_projects = []
        act_own = Count(sem("act_own"))
        dve_own = Count(sem("dve_own"))

        def own(eng, counter, ins):
            eng.wait_ge(counter.sem, counter.inc(ins))

        ends = {}

        def used(ins, n):
            if n not in ends:
                back = 1
                while n - back in ends:
                    back += 1
                ins.then_inc(w_used, back)

        def slot_of(n):
            return n % RING

        def load_chunk(sp, n, r=0):
            array, k, tiles, width = PLAN[n]
            if n >= RING:
                sp.wait_ge(w_hi, r * RING + (n - RING + 1))
                sp.wait_ge(w_lo, r * RING + (n - RING + 1))
            if isinstance(r, int):
                src = dram[array][k + r * RING]
            else:
                src = dram[array][bass.ds(r * RING + k, 1)].rearrange("a p n -> p (a n)")
            sp.dma_start(w_raw[:, slot_of(n), 0:tiles * width], src).then_inc(w_loaded[slot_of(n)], 16)

        def split_hi(act, n, r=0):
            _, _, tiles, width = PLAN[n]
            s = slot_of(n)
            act.wait_ge(w_loaded[s], r * 16 + 16 * (n // RING + 1))
            if n - RING in ends:
                done, value, each = ends[n - RING]
                act.wait_ge(done, r * each + value)
            elif n >= RING:
                act.wait_ge(w_used, r * RING + (n - RING + 1))
            nc.scalar.activation(whi[:, s, 0:tiles * width], w_raw[:, s, 0:tiles * width],
                                 ACT.Copy).then_inc(w_hi, 1)

        def split_lo(dve, n, r=0):
            _, _, tiles, width = PLAN[n]
            s = slot_of(n)
            dve.wait_ge(w_hi, r * RING + (n + 1))
            nc.vector.tensor_tensor(wlo[:, s, 0:tiles * width], w_raw[:, s, 0:tiles * width],
                                    whi[:, s, 0:tiles * width].bitcast(F32), ALU.subtract).then_inc(w_lo, 1)

        def next_hi(act, n, r=0):
            if n + RING < len(PLAN):
                split_hi(act, n + RING, r)

        def next_lo(dve, n, r=0):
            if n + RING < len(PLAN):
                split_lo(dve, n + RING, r)

        def take_chunk(pe, n, r=0):
            pe.wait_ge(w_hi, r * RING + (n + 1))
            pe.wait_ge(w_lo, r * RING + (n + 1))

        def mm3(acc, hi, lo, s, j, width, start, stop):
            c = slice(j * width, (j + 1) * width)
            nc.tensor.matmul(acc, hi, whi[:, s, c], start=start, stop=False)
            nc.tensor.matmul(acc, hi, wlo[:, s, c], start=False, stop=False)
            return nc.tensor.matmul(acc, lo, whi[:, s, c], start=False, stop=stop)

        def norm_banks(name):
            if name == "mem0":
                return bankD[1] + bankD[0]
            if name == "mem1":
                return [bankD[t][block] for block in (1, 0) for t in range(NT)]
            return bankT + bankD[0]

        def source_ready(eng, name, block):
            if name.startswith("mem"):
                eng.wait_ge(mem_in, 16)
            elif name == "ffn1":
                for b in range(block + 1):
                    eng.wait_ge(x_in[b], 16)
            else:
                updates = [n for n in NORMS[:NORM[name]] if not n.startswith("mem")]
                eng.wait_ge(h_ready, 4 * len(updates) - (2 if block == 0 else 0))

        def norm_tensor(pe, name, half):
            src = mem if name.startswith("mem") else h
            for pair, bank in list(enumerate(norm_banks(name)))[2 * half:2 * half + 2]:
                if pair % 2 == 0:
                    source_ready(pe, name, pair // 2)
                for j in range(2):
                    for t in range(NT):
                        k = 2 * pair + j
                        last = nc.tensor.transpose(bank[:, j * S + t * P:j * S + (t + 1) * P],
                                                   src[:, t, k * P:(k + 1) * P], ident)
                last.then_inc(xt_ps, 1)

        def norm_scalar(act, name, half):
            k0, to = 4 * NORM[name], xt_h
            for pair, bank in list(enumerate(norm_banks(name)))[2 * half:2 * half + 2]:
                act.wait_ge(xt_ps, k0 + pair + 1)
                for j in range(2):
                    k = 2 * pair + j
                    last = nc.scalar.activation(to[:, k], bank[:, j * S:(j + 1) * S], ACT.Copy,
                                                scale=gain[:, 8 * NORM[name] + k:8 * NORM[name] + k + 1])
                last.then_inc(xt_hi, 1)

        def rms_scalar(act, name):
            c = 2 * NORM[name]
            source_ready(act, name, 1)
            for t in range(NT):
                last = nc.scalar.activation(lg[:, :, :].rearrange("p a n -> p (a n)"), h[:, t], ACT.Square,
                                            scale=D ** -0.5, accum_out=ms[:, c + t:c + t + 1])
                if t == 0:
                    own(act, act_own, last)
            last.then_inc(ms_ready, 1)

        def root_vector(dve, name):
            c = 2 * NORM[name]
            dve.wait_ge(ms_ready, RMS_AT[name])
            rsqrt(dve, ms[:, c:c + 2], rs[:, c:c + 2], 1.0, EPS, 2).then_inc(rs_ready, 1)

        def rsqrt(dve, x, y, scale, eps, n):
            a = newton[:, 0:n]
            own(dve, dve_own, nc.vector.tensor_scalar(x, x, scale, eps, ALU.mult, ALU.add))
            own(dve, dve_own, nc.vector.tensor_scalar(a.bitcast(I32), x.bitcast(I32), 1, None,
                                                      ALU.arith_shift_right))
            own(dve, dve_own, nc.vector.tensor_scalar(y.bitcast(I32), a.bitcast(I32), -1.0, float(0x5f3759df),
                                                      ALU.mult, ALU.add))
            for step in range(3):
                own(dve, dve_own, nc.vector.scalar_tensor_tensor(out=a, in0=y, scalar=-0.5, in1=y,
                                                                 op0=ALU.mult, op1=ALU.mult))
                own(dve, dve_own, nc.vector.tensor_tensor(a, a, x, ALU.mult))
                last = nc.vector.scalar_tensor_tensor(out=y, in0=a, scalar=1.5, in1=y,
                                                      op0=ALU.add, op1=ALU.mult)
                if step < 2:
                    own(dve, dve_own, last)
            return last

        def norm_vector(dve, name, half):
            k0, hi, lo = 4 * NORM[name], xt_h, xt_l
            for pair, bank in list(enumerate(norm_banks(name)))[2 * half:2 * half + 2]:
                dve.wait_ge(xt_hi, k0 + pair + 1)
                for j in range(2):
                    k = 2 * pair + j
                    g = gain[:, 8 * NORM[name] + k:8 * NORM[name] + k + 1]
                    last = nc.vector.scalar_tensor_tensor(
                        out=lo[:, k], in0=bank[:, j * S:(j + 1) * S], scalar=g,
                        in1=hi[:, k].bitcast(F32), op0=ALU.mult, op1=ALU.subtract)
                last.then_inc(xt_lo, 1)

        def xt_ready(pe, name, k):
            pe.wait_ge(xt_lo, 4 * NORM[name] + k // 2 + 1)

        def rms(name, t):
            return rs[:, 2 * NORM[name] + t:2 * NORM[name] + t + 1]

        def residual_vector(dve, full, scale, block, full0=0):
            for t in range(NT):
                dve.wait_ge(full, full0 + NT * block + t + 1)
                hb = h[:, t, block * TW:(block + 1) * TW]
                nc.vector.scalar_tensor_tensor(out=hb, in0=bankD[t][block], scalar=scale, in1=hb,
                                               op0=ALU.mult, op1=ALU.add).then_inc(h_ready, 1)

        def tail_scalar(act, chunks, following):
            for n in chunks[:-1]:
                next_hi(act, n)
            if following:
                norm_scalar(act, following, 0)
            next_hi(act, chunks[-1])
            if following:
                norm_scalar(act, following, 1)

        def tail_vector(dve, chunks, following, full, scale, full0=0):
            half = len(chunks) // 2
            for n in chunks[:half - 1]:
                next_lo(dve, n)
            residual_vector(dve, full, scale, 0, full0)
            for n in chunks[half - 1:-1]:
                next_lo(dve, n)
            if following:
                norm_vector(dve, following, 0)
            residual_vector(dve, full, scale, 1, full0)
            next_lo(dve, chunks[-1])
            if following:
                norm_vector(dve, following, 1)

        class Ffn:
            def __init__(self, name, steps, hk, gated, scale, following):
                self.following = following
                self.name, self.steps, self.hk, self.gated, self.scale = name, steps, hk, gated, scale
                self.n0 = AT[name]
                self.tiles = (8 + 2 * hk) // 4
                self.up_full = sem(name + "_up_full")
                self.acted = sem(name + "_acted")
                self.hidden = sem(name + "_hidden")
                self.hid_ps = sem(name + "_hid_ps")
                self.hid_hi = sem(name + "_hid_hi")
                self.hid_lo = sem(name + "_hid_lo")
                self.down_full = sem(name + "_down_full")
                ends[self.n0 + 3] = (self.up_full, NT, 0)
                tail = self.n0 + 4 * steps
                ends[tail + 3] = (self.down_full, NB * NT, 0)
                ends[tail + 1] = (self.down_full, NT, 0)
                if not gated:
                    for i in range(1, steps):
                        ends[self.n0 + 4 * i + 1] = (self.up_full, NT * (i + 1), NT)

            def up(self, pe, i, s, pos, ks, fresh):
                if fresh and ks[0] == 2:
                    norm_tensor(pe, self.name, 1)
                for t in range(NT):
                    if ks[0] == 0 and not fresh:
                        pe.wait_ge(self.hidden if self.gated else self.acted, i * NT + (t - 1))
                    for j, k in enumerate(ks):
                        if fresh and t == 0 and k % 2 == 0:
                            xt_ready(pe, self.name, k)
                        last = mm3(bankA[t], xt_h[:, k, t * P:(t + 1) * P], xt_l[:, k, t * P:(t + 1) * P],
                                   s, pos + j, TW, k == 0, k == KC - 1)
                    if ks[-1] == KC - 1:
                        last.then_inc(self.up_full, 1)
                return last

            def down(self, pe, s, pos, js, first, final):
                for a, j in enumerate(js):
                    k, block = (j % self.hk, j // self.hk) if final else (j // NB, j % NB)
                    for t in range(NT):
                        last = mm3(bankD[t][block], ot_h[:, k, t * P:(t + 1) * P],
                                   ot_l[:, k, t * P:(t + 1) * P], s, pos + a, TW,
                                   first and k == 0, final and k == self.hk - 1)
                        if final and k == self.hk - 1:
                            last.then_inc(self.down_full, 1)
                return last

            def turn(self, pe, i):
                pe.wait_ge(self.hidden, i * NT)
                if not isinstance(i, int) or i > 1:
                    pe.wait_ge(self.hid_lo, i - 1)
                for k in range(self.hk):
                    for t in range(NT):
                        at = (k % 2) * S + t * P
                        last = nc.tensor.transpose(bankT[k // 2][:, at:at + P],
                                                   nat[:, 0, t, k * P:(k + 1) * P], ident)
                last.then_inc(self.hid_ps, 1)

            def step_tensor(self, pe, i, n, r=0, first=False):
                if not first:
                    self.turn(pe, i)
                for c in range(4):
                    if first and c == 1:
                        self.turn(pe, i)
                    take_chunk(pe, n + c, r)
                    tiles = list(range(c * self.tiles, (c + 1) * self.tiles))
                    ups, downs = [j for j in tiles if j < KC], [j - KC for j in tiles if j >= KC]
                    if ups:
                        last = self.up(pe, i, slot_of(n + c), 0, ups, False)
                    if downs:
                        if downs[0] == 0:
                            pe.wait_ge(self.hid_lo, i)
                        last = self.down(pe, slot_of(n + c), len(ups), downs, first, False)
                    used(last, n + c)

            def tensor(self, pe):
                for c in range(4):
                    take_chunk(pe, self.n0 + c)
                    if c == 3 and self.name == "ffn1":
                        tables.tensor(pe)
                    used(self.up(pe, 0, slot_of(self.n0 + c), 0, [2 * c, 2 * c + 1], True), self.n0 + c)
                self.step_tensor(pe, 1, self.n0 + 4, first=True)
                with pe.Fori(0, self.steps - 2) as r:
                    self.step_tensor(pe, r + 2, self.n0 + 8, r)
                self.turn(pe, self.steps)
                pe.wait_ge(self.hid_lo, self.steps)
                n, each = self.n0 + 4 * self.steps, self.hk // 2
                for c in range(4):
                    take_chunk(pe, n + c)
                    if c == 3 and self.following:
                        norm_tensor(pe, self.following, 0)
                    used(self.down(pe, slot_of(n + c), 0, list(range(c * each, (c + 1) * each)),
                                   False, True), n + c)

            def take_up_scalar(self, act, i):
                for t in range(NT):
                    act.wait_ge(self.up_full, i * NT + (t + 1))
                    if not isinstance(i, int) or i > 0:
                        act.wait_ge(self.hidden, i * NT + (t - 1))
                    if self.gated:
                        ins = nc.scalar.activation(lg[:, t, 0:256], bankA[t][:, 0:256], ACT.Silu,
                                                   scale=rms(self.name, t))
                    else:
                        ins = nc.scalar.activation(lg[:, t], bankA[t], ACT.Relu, scale=rms(self.name, t))
                    ins.then_inc(self.acted, 1)

            def turned_scalar(self, act, i):
                act.wait_ge(self.hid_ps, i)
                for b in range(self.hk // 2):
                    last = nc.scalar.activation(ot_h[:, 2 * b:2 * b + 2],
                                                bankT[b].rearrange("p (k s) -> p k s", k=2), ACT.Copy)
                last.then_inc(self.hid_hi, 1)

            def step_scalar(self, act, i, n, r=0):
                self.turned_scalar(act, i)
                next_hi(act, n, r)
                next_hi(act, n + 1, r)
                self.take_up_scalar(act, i)
                next_hi(act, n + 2, r)
                next_hi(act, n + 3, r)

            def scalar(self, act):
                if self.name == "ffn1":
                    norm_scalar(act, self.name, 1)
                rms_scalar(act, self.name)
                if self.gated:
                    nc.scalar.preload_act_table(ACT.Silu)
                for c in range(2):
                    next_hi(act, self.n0 + c)
                act.wait_ge(rs_ready, RMS_AT[self.name])
                self.take_up_scalar(act, 0)
                for c in range(2, 4):
                    next_hi(act, self.n0 + c)
                if self.name == "ffn1":
                    tables.bias_scalar(act)
                with act.Fori(0, self.steps - 2) as r:
                    self.step_scalar(act, r + 1, self.n0 + 4, r)
                self.step_scalar(act, self.steps - 1, self.n0 + 4 * (self.steps - 1))
                self.turned_scalar(act, self.steps)
                tail_scalar(act, [self.n0 + 4 * self.steps + c for c in range(4)], self.following)

            def hide_vector(self, dve, i):
                for t in range(NT):
                    dve.wait_ge(self.acted, i * NT + (t + 1))
                    if not isinstance(i, int) or i > 0:
                        dve.wait_ge(self.hid_ps, i)
                    if self.gated:
                        ins = nc.vector.scalar_tensor_tensor(
                            out=nat[:, 0, t, 0:256], in0=bankA[t][:, 256:512], scalar=rms(self.name, t),
                            in1=lg[:, t, 0:256], op0=ALU.mult, op1=ALU.mult)
                    else:
                        ins = nc.vector.tensor_tensor(nat[:, 0, t], lg[:, t], lg[:, t], ALU.mult)
                    ins.then_inc(self.hidden, 1)

            def turned_vector(self, dve, i):
                dve.wait_ge(self.hid_hi, i)
                for b in range(self.hk // 2):
                    last = nc.vector.tensor_tensor(ot_l[:, 2 * b:2 * b + 2],
                                                   bankT[b].rearrange("p (k s) -> p k s", k=2),
                                                   ot_h[:, 2 * b:2 * b + 2].bitcast(F32), ALU.subtract)
                last.then_inc(self.hid_lo, 1)

            def step_vector(self, dve, i, n, r=0):
                self.turned_vector(dve, i)
                next_lo(dve, n, r)
                next_lo(dve, n + 1, r)
                self.hide_vector(dve, i)
                next_lo(dve, n + 2, r)
                next_lo(dve, n + 3, r)

            def vector(self, dve):
                if self.name == "ffn1":
                    norm_vector(dve, self.name, 1)
                root_vector(dve, self.name)
                dve.wait_ge(rs_ready, RMS_AT[self.name])
                for c in range(2):
                    next_lo(dve, self.n0 + c)
                self.hide_vector(dve, 0)
                for c in range(2, 4):
                    next_lo(dve, self.n0 + c)
                with dve.Fori(0, self.steps - 2) as r:
                    self.step_vector(dve, r + 1, self.n0 + 4, r)
                self.step_vector(dve, self.steps - 1, self.n0 + 4 * (self.steps - 1))
                self.turned_vector(dve, self.steps)
                tail_vector(dve, [self.n0 + 4 * self.steps + c for c in range(4)], self.following,
                            self.down_full, self.scale)

            def sync(self, sp):
                n = self.n0
                for c in range(4):
                    load_chunk(sp, n + c)
                    if c == 0 and self.name == "ffn1":
                        sp.dma_start(h[:, :, TW:D], dram["x"][:, :, TW:D]).then_inc(x_in[1], 16)
                with sp.Fori(0, self.steps - 1) as r:
                    for c in range(4):
                        load_chunk(sp, n + 4 + c, r)
                for c in range(4):
                    load_chunk(sp, n + 4 * self.steps + c)

            def gpsimd(self, pool):
                pass

        class Unit:

            def __init__(self, kind, ks, width, chunks, to=None, gains=None, scale=1.0, rows=None, base=0, vals=v):
                self.vals = vals
                self.kind, self.ks, self.width, self.chunks = kind, ks, width, chunks
                self.to, self.gains, self.scale, self.rows, self.base = to, gains, scale, rows, base

        class Project:
            def __init__(self, name, section, units, stat_h, stat_l, norm=None, need=(), scaled=None,
                         before=None, before_need=(), hand_on=False, aside=None):
                self.aside, self.aside_at = aside or (None, None)
                self.before, self.before_need, self.hand_on = before, before_need, hand_on
                self.name, self.units, self.norm, self.need = name, units, norm, need
                self.scaled = (rs_ready, RMS_AT[norm]) if norm else scaled
                self.stat_h, self.stat_l = stat_h, stat_l
                self.full = sem(name + "_full")
                self.evac = sem(name + "_evac")
                kinds = [unit.kind for unit in units]
                if {"qk", "dkv", "pe"} & set(kinds):
                    self.made = sem(name + "_made")
                self.turned = sem(name + "_turned")
                self.taken = sem(name + "_taken")
                self.lows = None
                if "latent" in kinds:
                    self.squared = sem(name + "_squared")
                    self.rooted = sem(name + "_rooted")
                if "latent" in kinds:
                    self.lows = sem(name + "_lows")
                n, made, turn, low = AT[section], 0, 0, 0
                for u, unit in enumerate(units):
                    unit.u, unit.n = u, []
                    k = unit.ks[0]
                    for tiles in unit.chunks:
                        unit.n.append((n, list(range(k, k + tiles))))
                        k, n = k + tiles, n + 1
                    ends[n - 1] = (self.full, NT * (u + 1), 0)
                    if unit.kind in ("qk", "dkv", "pe"):
                        unit.made, made = made, made + 1
                    if unit.kind != "v":
                        unit.turn, turn = turn, turn + 1
                    unit.low0 = NT * low
                    if unit.kind in ("latent", "dkv"):
                        low += 1
                self.turns, self.lowest = turn, low
                self.evac_ready = (self.evac, NT * len(units))
                self.turned_ready = (self.taken, NT * turn)
                self.split_ready = (self.lows, NT * low)

            def nat_of(self, unit, t):
                return nat[:, unit.u % 2, t]

            def multiply(self, pe, unit, before=None):
                for c, (n, ks) in enumerate(unit.n):
                    take_chunk(pe, n)
                    for part in (ks[:2], ks[2:]) if self.norm and unit.u == 0 else (ks,):
                        if self.norm and unit.u == 0 and part and part[0] == 2:
                            norm_tensor(pe, self.norm, 1)
                        for t in range(NT):
                            if part and part[0] == unit.ks[0] and unit.u > 0:
                                pe.wait_ge(self.evac, NT * (unit.u - 1) + t + 1)
                            for k in part:
                                if self.norm and unit.u == 0 and t == 0 and k % 2 == 0:
                                    xt_ready(pe, self.norm, k)
                                last = mm3(bankA[t][:, 0:unit.width], self.stat_h[:, k, t * P:(t + 1) * P],
                                           self.stat_l[:, k, t * P:(t + 1) * P], slot_of(n), k - ks[0],
                                           unit.width, k == unit.ks[0], k == unit.ks[-1])
                                if k == unit.ks[-1]:
                                    last.then_inc(self.full, 1)
                    used(last, n)
                    if before and self.hand_on and c == 0:
                        self.turn(pe, before)

            def turn(self, pe, unit):
                for t in range(NT):
                    if unit.kind in ("qk", "dkv", "pe"):
                        pe.wait_ge(self.made, NT * unit.made + t + 1)
                    else:
                        pe.wait_ge(self.evac, NT * unit.u + t + 1)
                    if unit.turn > 0:
                        pe.wait_ge(self.taken, NT * (unit.turn - 1) + t + 1)
                    if unit.low0:
                        pe.wait_ge(self.lows, unit.low0 - NT + t + 1)
                    blocks = [self.nat_of(unit, t)[:, c * P:(c + 1) * P] for c in range(4)]
                    if unit.kind in ("idx", "latent"):
                        blocks = blocks[:3]
                    if unit.kind == "dkv":
                        blocks = blocks[:2] + [lg[:, t, 0:P]]
                    if unit.kind == "pe":
                        blocks = [lg[:, t, c * P:(c + 1) * P] for c in range(4)]
                    for c, b in enumerate(blocks):
                        last = nc.tensor.transpose(bankT[t][:, c * P:(c + 1) * P], b, ident)
                    last.then_inc(self.turned, 1)

            def tensor(self, pe):
                for s, value in self.need:
                    pe.wait_ge(s, value)
                before = None
                for unit in self.units:
                    self.multiply(pe, unit, before)
                    if unit.u == self.aside_at:
                        self.aside.tensor(pe)
                    if self.before and unit.u == 1:
                        for s, value in self.before_need:
                            pe.wait_ge(s, value)
                    if before is not None and not self.hand_on:
                        self.turn(pe, before)
                    before = unit if unit.kind != "v" else None
                    if self.before and unit.u == 0:
                        self.before.turn(pe, self.before.units[-1])
                if before is not None and not self.hand_on:
                    self.turn(pe, before)

            def copy_out(self, act, unit):
                w = unit.width
                if unit.u == 0 and self.scaled:
                    act.wait_ge(*self.scaled)
                for t in range(NT):
                    act.wait_ge(self.full, NT * unit.u + t + 1)
                    row = unit.rows(t)
                    if unit.kind == "v":
                        nc.scalar.activation(unit.vals[:, t, unit.base:unit.base + w], bankA[t], ACT.Copy,
                                             scale=row).then_inc(self.evac, 1)
                    elif unit.kind == "idx":
                        to = self.nat_of(unit, t)
                        nc.scalar.activation(wi[:, t], bankA[t][:, 320:324], ACT.Copy, scale=row)
                        nc.scalar.activation(to[:, 320:384], bankA[t][:, 256:320], ACT.Copy, scale=row)
                        nc.scalar.activation(to[:, 0:320], bankA[t][:, 0:320], ACT.Copy,
                                             scale=row).then_inc(self.evac, 1)
                    else:
                        nc.scalar.activation(self.nat_of(unit, t)[:, 0:w], bankA[t][:, 0:w], ACT.Copy,
                                             scale=row).then_inc(self.evac, 1)

            def latent_squares(self, act, unit):
                n = {"latent": QL, "dkv": KL}[unit.kind]
                c = 2 * len(NORMS) + (0 if unit.kind == "latent" else 2)
                act.wait_ge(self.evac, NT * (unit.u + 1))
                for t in range(NT):
                    last = nc.scalar.activation(
                        score[:, :, :].rearrange("p a n -> p (a n)")[:, 0:n], self.nat_of(unit, t)[:, 0:n],
                        ACT.Square, scale=n ** -0.5, accum_out=ms[:, c + t:c + t + 1])
                    if unit.kind == "dkv" and t == 1:
                        last.then_inc(self.squared, 1)
                    else:
                        own(act, act_own, last)

            def take(self, act, unit):
                if unit.to is qt and unit.kind == "qk":
                    act.wait_ge(tables.out, 16)
                for t in range(NT):
                    act.wait_ge(self.turned, NT * unit.turn + t + 1)
                    bank, s = bankT[t].rearrange("p (c s) -> p c s", c=4), slice(t * P, (t + 1) * P)
                    if unit.kind in ("latent", "dkv"):
                        for c in range(unit.ks_out):
                            last = nc.scalar.activation(ot_h[:, unit.base + c, s], bank[:, c], ACT.Copy,
                                                        scale=gain[:, unit.gains + c:unit.gains + c + 1])
                        if unit.kind == "dkv":
                            last = nc.scalar.activation(pet[:, 4, s], bank[:, 2], ACT.Copy)
                    elif unit.kind == "idx":
                        last = nc.scalar.activation(pet[:, 0:3, s], bank[:, 0:3], ACT.Copy)
                    elif unit.kind == "qk":
                        last = nc.scalar.activation(unit.to[:, unit.base:unit.base + 4, s], bank, ACT.Copy,
                                                    scale=gain[:, unit.gains:unit.gains + 1])
                    else:
                        last = nc.scalar.activation(unit.to[:, unit.base:unit.base + 4, s], bank, ACT.Copy,
                                                    scale=unit.scale)
                    last.then_inc(self.taken, 1)

            def scalar(self, act):
                before = None
                for unit in self.units:
                    for n, _ in unit.n[:-1]:
                        next_hi(act, n)
                    if before is not None and self.hand_on:
                        self.take(act, before)
                    self.copy_out(act, unit)
                    if unit.u == self.aside_at:
                        self.aside.scalar(act)
                    next_hi(act, unit.n[-1][0])
                    if unit.kind in ("latent", "dkv"):
                        self.latent_squares(act, unit)
                    if before is not None and not self.hand_on:
                        self.take(act, before)
                    before = unit if unit.kind != "v" else None
                if before is not None:
                    self.take(act, before)

            def squares(self, dve, unit):
                for t in range(NT):
                    dve.wait_ge(self.evac, NT * unit.u + t + 1)
                    rows = self.nat_of(unit, t)
                    last = nc.vector.tensor_tensor(lg[:, t], rows, rows, ALU.mult)
                own(dve, dve_own, last)
                own(dve, dve_own, nc.vector.tensor_reduce(
                    hs[:, 0], lg[:, :, :].rearrange("p t (h d) -> p (t h) d", d=HD1), AX.X, ALU.add))
                query = unit.scale != 1.0
                own(dve, dve_own, rsqrt(dve, hs[:, 0], hs[:, 1], 1.0 if query else 1.0 / HD1,
                                        HD1 * EPS if query else EPS, NT * 8))

            def normalise(self, dve, unit):
                for t in range(NT):
                    rows = self.nat_of(unit, t).rearrange("p (h d) -> p h d", d=HD1)
                    nc.vector.tensor_tensor(rows, rows, hs[:, 1, 8 * t:8 * t + 8].unsqueeze(2).to_broadcast(
                        [P, 8, HD1]), ALU.mult).then_inc(self.made, 1)

            def rotate(self, dve, unit):
                dve.wait_ge(tables.trig, 1)
                heads = 1 if unit.kind == "dkv" else H2
                at = KL if unit.kind == "dkv" else 0
                for t in range(NT):
                    dve.wait_ge(self.evac, NT * unit.u + t + 1)
                    if unit.made or t:
                        dve.wait_ge(self.made, NT * unit.made + t)
                    w = heads * HALF
                    x1, x2 = (self.nat_of(unit, t)[:, at + a * w:at + (a + 1) * w]
                              .rearrange("p (h d) -> p h d", h=heads) for a in range(2))
                    cos, sin = (trig[:, a, t].unsqueeze(1).to_broadcast([P, heads, HALF]) for a in range(2))
                    part = [pt[:, a // 2, (a % 2) * 256:(a % 2) * 256 + w].rearrange("p (h d) -> p h d", h=heads)
                            for a in range(4)]
                    nc.vector.tensor_tensor(part[0], x1, cos, ALU.mult)
                    nc.vector.tensor_tensor(part[1], x2, sin, ALU.mult)
                    nc.vector.tensor_tensor(part[2], x1, sin, ALU.mult)
                    own(dve, dve_own, nc.vector.tensor_tensor(part[3], x2, cos, ALU.mult))
                    copies = 2 if unit.kind == "dkv" else 1
                    for c in range(copies):
                        to = lg[:, t, c * ROPE:c * ROPE + heads * ROPE].rearrange("p (h d) -> p h d", h=heads)
                        nc.vector.tensor_tensor(to[:, :, 0:HALF], part[0], part[1], ALU.subtract)
                        last = nc.vector.tensor_tensor(to[:, :, HALF:ROPE], part[2], part[3], ALU.add)
                    last.then_inc(self.made, 1)

            def lower(self, dve, unit):
                for t in range(NT):
                    dve.wait_ge(self.taken, NT * unit.turn + t + 1)
                    s = slice(t * P, (t + 1) * P)
                    for c in range(unit.ks_out):
                        g = gain[:, unit.gains + c:unit.gains + c + 1]
                        last = nc.vector.scalar_tensor_tensor(
                            out=ot_l[:, unit.base + c, s], in0=bankT[t][:, c * P:(c + 1) * P], scalar=g,
                            in1=ot_h[:, unit.base + c, s].bitcast(F32), op0=ALU.mult, op1=ALU.subtract)
                    last.then_inc(self.lows, 1)

            def vector(self, dve):
                before = None
                for unit in self.units:
                    for n, _ in unit.n[:-1]:
                        next_lo(dve, n)
                    if unit.kind == "qk":
                        self.squares(dve, unit)
                    if before is not None and before.kind in ("latent", "dkv"):
                        self.lower(dve, before)
                    if unit.kind in ("dkv", "pe"):
                        self.rotate(dve, unit)
                    if unit.u == self.aside_at:
                        self.aside.vector(dve)
                    next_lo(dve, unit.n[-1][0])
                    if unit.kind == "qk":
                        self.normalise(dve, unit)
                    before = unit
                if before.kind in ("latent", "dkv"):
                    c = 2 * len(NORMS)
                    dve.wait_ge(self.squared, 1)
                    rsqrt(dve, ms[:, c:c + 4], rs[:, c:c + 4], 1.0, EPS, 4).then_inc(self.rooted, 1)
                    self.lower(dve, before)

            def sync(self, sp):
                for unit in self.units:
                    for n, _ in unit.n:
                        load_chunk(sp, n)

            def gpsimd(self, pool):
                pass

        class Fill:

            def __init__(self, section, banks, free, to, to_free, rows, groups, keys=None):
                self.n0, self.banks, self.free, self.to, self.to_free = AT[section], banks, free, to, to_free
                self.rows, self.groups, self.keys = rows, groups, keys
                self.normed = None
                self.full0 = NT * len(fills)
                fills.append(section)
                self.ready = (fill_copied, self.full0 + NT)
                ends[self.n0 + 1] = (fill_full, self.full0 + NT, 0)
                if keys is not None:
                    self.turned0 = NT * len(turned_fills)
                    turned_fills.append(section)
                    self.ready = (fill_taken, self.turned0 + NT)

            def tensor(self, pe, step):
                if step < 4:
                    c, t = divmod(step, NT)
                    n = self.n0 + c
                    if t == 0 and self.normed:
                        pe.wait_ge(xt_lo, 4 * NORM[self.normed] + 2 * (c + 1))
                    if step == 0:
                        for s, value in self.free:
                            pe.wait_ge(s, value)
                    if t == 0:
                        take_chunk(pe, n)
                    for j in range(4):
                        k = 4 * c + j
                        last = mm3(self.banks[t], xt_h[:, k, t * P:(t + 1) * P], xt_l[:, k, t * P:(t + 1) * P],
                                   slot_of(n), j, TW, k == 0, k == KC - 1)
                    if c == 1:
                        last.then_inc(fill_full, 1)
                    elif t == NT - 1:
                        used(last, n)
                elif step == 5 and self.keys is not None:
                    for t in range(NT):
                        pe.wait_ge(fill_copied, self.full0 + t + 1)
                        for c in range(4):
                            last = nc.tensor.transpose(self.banks[t][:, c * P:(c + 1) * P],
                                                       self.to(t)[:, c * P:(c + 1) * P], ident)
                        last.then_inc(fill_ps, 1)

            def scalar(self, act, step):
                if step == 2:
                    next_hi(act, self.n0)
                elif step == 4:
                    for s, value in self.to_free:
                        act.wait_ge(s, value)
                    for t in range(NT):
                        act.wait_ge(fill_full, self.full0 + t + 1)
                        nc.scalar.activation(self.to(t), self.banks[t], ACT.Copy, scale=self.rows(t))\
                            .then_inc(fill_copied, 1)
                elif step == 7:
                    next_hi(act, self.n0 + 1)
                elif step == 6 and self.keys is not None:
                    for t in range(NT):
                        act.wait_ge(fill_ps, self.turned0 + t + 1)
                        nc.scalar.activation(self.keys[:, :, t * P:(t + 1) * P],
                                             self.banks[t].rearrange("p (c s) -> p c s", c=4), ACT.Copy)\
                            .then_inc(fill_taken, 1)

            def sync(self, sp):
                for c in range(2):
                    load_chunk(sp, self.n0 + c)

            def vector(self, dve, step):
                if step == 2:
                    next_lo(dve, self.n0)
                elif step == 7:
                    next_lo(dve, self.n0 + 1)

        def fill_steps(fillers, g):
            return [(f, step) for f in fillers for step, at in enumerate(f.groups) if at == g]

        class Finish:
            def __init__(self, fins, done, normalised):
                self.fins, self.done, self.normalised = fins, done, normalised
                self.f0 = sum(len(f) for f in all_fins)
                all_fins.append(fins)
                self.ready = (rows_lo, self.f0 + len(fins))

            def out_rows(self, dve, f):
                t, b, value, at, heads = self.fins[f]
                dve.wait_ge(self.done, value)
                same = [g for g in range(f) if self.fins[g][0] == t]
                if same:
                    dve.wait_ge(rows_ps, self.f0 + same[-1] + 1)
                if self.normalised:
                    own(dve, dve_own, nc.vector.reciprocal(rinv[:, at:at + heads], rsum[:, at:at + heads]))
                    nc.vector.tensor_tensor(
                        nat[:, 0, t].rearrange("p (h d) -> p h d", h=heads),
                        bankD[t][b].rearrange("p (h d) -> p h d", h=heads),
                        rinv[:, at:at + heads].unsqueeze(2).to_broadcast([P, heads, TW // heads]),
                        ALU.mult).then_inc(rows_made, 1)
                else:
                    nc.vector.tensor_copy(nat[:, 0, t], bankD[t][b]).then_inc(rows_made, 1)

            def turn(self, pe, f):
                t, b = self.fins[f][:2]
                pe.wait_ge(rows_made, self.f0 + f + 1)
                for c in range(4):
                    last = nc.tensor.transpose(bankD[t][b][:, c * P:(c + 1) * P],
                                               nat[:, 0, t, c * P:(c + 1) * P], ident)
                last.then_inc(rows_ps, 1)

            def take_hi(self, act, f):
                t, b = self.fins[f][:2]
                act.wait_ge(rows_ps, self.f0 + f + 1)
                nc.scalar.activation(ot_h[:, 4 * b:4 * b + 4, t * P:(t + 1) * P],
                                     bankD[t][b].rearrange("p (c s) -> p c s", c=4), ACT.Copy).then_inc(rows_hi, 1)

            def take_lo(self, dve, f):
                t, b = self.fins[f][:2]
                dve.wait_ge(rows_hi, self.f0 + f + 1)
                nc.vector.tensor_tensor(ot_l[:, 4 * b:4 * b + 4, t * P:(t + 1) * P],
                                        bankD[t][b].rearrange("p (c s) -> p c s", c=4),
                                        ot_h[:, 4 * b:4 * b + 4, t * P:(t + 1) * P].bitcast(F32),
                                        ALU.subtract).then_inc(rows_lo, 1)

        class Attend:
            def __init__(self, name, groups, fins, need, select=None, fillers=(), bank_free=None):
                self.fillers, self.bank_free = fillers, bank_free or {}
                self.groups, self.need, self.select = groups, need, select
                self.scores = sem(name + "_scores")
                self.logits = sem(name + "_logits")
                self.probs = sem(name + "_probs")
                self.p_ps = sem(name + "_p_ps")
                self.p_sb = sem(name + "_p_sb")
                self.summed = sem(name + "_summed")
                self.fin = Finish([(t, b, g + 1, at, hh) for t, b, g, at, hh in fins], self.summed, True)
                self.last = [g for _, _, g, _, _ in fins]
                self.ready = self.fin.ready

            def score(self, pe, g):
                if g >= 2:
                    pe.wait_ge(self.logits, g - 1)
                for head in self.groups[g]:
                    for i, (q, k) in enumerate(head["qk"]):
                        last = nc.tensor.matmul(bankA[g % 2][:, head["at"]:head["at"] + head["width"]], q, k,
                                                start=i == 0, stop=i == len(head["qk"]) - 1)
                last.then_inc(self.scores, 1)

            def turn(self, pe, g):
                pe.wait_ge(self.probs, g + 1)
                if g >= 2:
                    pe.wait_ge(self.p_sb, g - 1)
                for c in range(4):
                    last = nc.tensor.transpose(bankT[g % 2][:, c * P:(c + 1) * P],
                                               lg[:, g % 2, c * P:(c + 1) * P], ident)
                last.then_inc(self.p_ps, 1)

            def value(self, pe, g):
                pe.wait_ge(self.p_sb, g + 1)
                if g in self.bank_free:
                    pe.wait_ge(*self.bank_free[g])
                for head in self.groups[g]:
                    for i, val in enumerate(head["v"]):
                        c = head["at"] + i * P
                        last = nc.tensor.matmul(head["out"], pt[:, g % 2, c:c + P], val,
                                                start=i == 0, stop=i == len(head["v"]) - 1)
                last.then_inc(self.summed, 1)

            def tensor(self, pe):
                for s, value in self.need:
                    pe.wait_ge(s, value)
                if self.select:
                    self.select.tensor(pe, (0, 1))
                self.score(pe, 0)
                for g in range(len(self.groups) + 3):
                    if g + 1 < len(self.groups):
                        self.score(pe, g + 1)
                    for filler, step in fill_steps(self.fillers, g):
                        filler.tensor(pe, step)
                        if self.select and step == g == 0:
                            self.select.tensor(pe, (2, 3))
                    if self.select and g == 0:
                        pe.wait_ge(self.select.relus, 4)
                    if g < len(self.groups):
                        self.turn(pe, g)
                    if 1 <= g <= len(self.groups):
                        self.value(pe, g - 1)
                    for f, last in enumerate(self.last):
                        if last == g - 2:
                            self.fin.turn(pe, f)

            def scalar(self, act):
                nc.scalar.preload_act_table_set("natural_log_exp_and_others")
                if self.select:
                    self.select.scalar(act)
                for g in range(len(self.groups) + 4):
                    if g < len(self.groups):
                        act.wait_ge(self.logits, g + 1)
                        for head in self.groups[g]:
                            rows = lg[:, g % 2, head["at"]:head["at"] + head["width"]]
                            c = head["col"]
                            last = nc.scalar.activation(rows, rows, ACT.Exp, bias=nmax[:, c:c + 1], scale=-1.0,
                                                        accum_out=rsum[:, c:c + 1])
                        last.then_inc(self.probs, 1)
                    for filler, step in fill_steps(self.fillers, g):
                        filler.scalar(act, step)
                    for f, last in enumerate(self.last):
                        if last == g - 3:
                            self.fin.take_hi(act, f)

            def vector(self, dve):
                if self.select:
                    self.select.vector(dve)
                for g in range(len(self.groups) + 4):
                    if g < len(self.groups):
                        if self.select:
                            self.select.before_logits(dve, g)
                        dve.wait_ge(self.scores, g + 1)
                        if g >= 2:
                            dve.wait_ge(self.p_ps, g - 1)
                        for head in self.groups[g]:
                            c, a, w = head["col"], head["at"], head["width"]
                            last = nc.vector.tensor_tensor_reduce(
                                out=lg[:, g % 2, a:a + w], in0=bankA[g % 2][:, a:a + w], in1=head["bias"],
                                scale=-1.0, scalar=3e38, op0=ALU.add, op1=ALU.min,
                                accum_out=nmax[:, c:c + 1])
                        last.then_inc(self.logits, 1)
                    if 1 <= g <= len(self.groups):
                        dve.wait_ge(self.p_ps, g)
                        if g >= 3:
                            dve.wait_ge(self.summed, g - 2)
                        nc.vector.tensor_copy(pt[:, (g - 1) % 2], bankT[(g - 1) % 2]).then_inc(self.p_sb, 1)
                    for f, last in enumerate(self.last):
                        if last == g - 2:
                            self.fin.out_rows(dve, f)
                        if last == g - 3:
                            self.fin.take_lo(dve, f)
                    for filler, step in fill_steps(self.fillers, g):
                        filler.vector(dve, step)
                    if self.select:
                        self.select.after_group(dve, g)

            def sync(self, sp):
                for filler in self.fillers:
                    filler.sync(sp)

            def gpsimd(self, pool):
                if self.select:
                    self.select.gpsimd(pool, self)

        class Select:
            ROUNDS = TOPK // 8

            def __init__(self, moba_groups):
                self.moba_groups = moba_groups
                self.dots = sem("idx_dots")
                self.relus = sem("idx_relus")
                self.summed = sem("idx_summed")
                self.selected = sem("idx_selected")
                self.biased = sem("idx_biased")
                self.passes = [(0, 0, [0, 2], P), (0, 1, [1, 3], P), (1, 0, [0, 2], S), (1, 1, [1, 3], S)]

            def tensor(self, pe, passes):
                for i in passes:
                    t, bank, heads, keys = self.passes[i]
                    if i >= 2:
                        pe.wait_ge(self.relus, i - 1)
                    for j, head in enumerate(heads):
                        half = slice(64 * (head % 2), 64 * (head % 2) + 64)
                        last = nc.tensor.matmul(bankT[bank][:, j * keys:(j + 1) * keys],
                                                pet[half, head // 2, t * P:(t + 1) * P],
                                                pet[half, 2, 0:keys], start=True, stop=True)
                    last.then_inc(self.dots, 1)

            def scalar(self, act):
                for i, (t, bank, heads, keys) in enumerate(self.passes):
                    act.wait_ge(self.dots, i + 1)
                    if i >= 2:
                        act.wait_ge(self.summed, i - 1)
                    nc.scalar.activation(pt[:, i % 2, 0:2 * keys], bankT[bank][:, 0:2 * keys], ACT.Relu,
                                         scale=0.125 * 0.5)\
                        .then_inc(self.relus, 1)

            def vector(self, dve):
                for i, (t, bank, heads, keys) in enumerate(self.passes):
                    dve.wait_ge(self.relus, i + 1)
                    for j, head in enumerate(heads):
                        to = score[:, t, 0:keys]
                        before = const[:, C_CAUSAL + S - keys:C_CAUSAL + S] if head == 0 else to
                        ins = nc.vector.scalar_tensor_tensor(
                            out=to, in0=pt[:, i % 2, j * keys:(j + 1) * keys],
                            scalar=wi[:, t, head:head + 1], in1=before, op0=ALU.mult, op1=ALU.add)
                        if j < len(heads) - 1:
                            own(dve, dve_own, ins)
                    ins.then_inc(self.summed, 1)
                    dve.wait_ge(self.summed, i + 1)

            def take_eight(self, dve):
                for t in range(NT):
                    last = nc.vector.max(top8[:, t], score[:, t, 0:(t + 1) * P])
                own(dve, dve_own, last)
                for t in range(NT):
                    rows = score[:, t, 0:(t + 1) * P]
                    last = nc.vector.match_replace(out=rows, in_to_replace=top8[:, t], in_values=rows,
                                                   imm_value=TAKEN)
                own(dve, dve_own, last)

            def after_group(self, dve, g):
                for r in range(2 * g, 2 * g + 2):
                    if r < self.ROUNDS:
                        self.take_eight(dve)
                if 2 * g + 2 == self.ROUNDS:
                    for t in range(NT):
                        rows = score[:, t, 0:(t + 1) * P]
                        nc.vector.tensor_scalar(rows, rows, -2e38, NEG, ALU.is_gt, ALU.mult)\
                            .then_inc(self.selected, 1)

            def before_logits(self, dve, g):
                if g >= self.moba_groups:
                    dve.wait_ge(self.biased, g - self.moba_groups + 1)

            def gpsimd(self, pool, attend):
                pool.wait_ge(self.selected, NT)
                for g in range(self.moba_groups, len(attend.groups)):
                    if g >= self.moba_groups + 2:
                        pool.wait_ge(attend.logits, g - 1)
                    first = attend.groups[g][0]
                    keys, n, t = first["width"], len(attend.groups[g]), first["tile"]
                    nc.gpsimd.tensor_tensor(
                        nat[:, 1, g % 2].rearrange("p (h k) -> p h k", h=n),
                        rel[:, first["head"]:first["head"] + 2 * n - 1:2, S - keys:S],
                        score[:, t, 0:keys].unsqueeze(1).to_broadcast([P, n, keys]),
                        ALU.add).then_inc(self.biased, 1)

        class Stick:
            def __init__(self, name, need, fillers, bank_free):
                self.need, self.fillers, self.bank_free = need, fillers, bank_free
                self.scores = sem(name + "_scores")
                self.masked = sem(name + "_masked")
                self.logs = sem(name + "_logs")
                self.soft = sem(name + "_soft")
                self.sums = sem(name + "_sums")
                self.expo = sem(name + "_expo")
                self.weights = sem(name + "_weights")
                self.summed = sem(name + "_summed")
                self.fin = Finish([(t, b, 4 * b + 4, 0, 4) for b in range(2) for t in range(NT)],
                                  self.summed, False)
                self.ready = self.fin.ready

            def score(self, pe, g):
                if g >= 2:
                    pe.wait_ge(self.masked, g - 1)
                nc.tensor.matmul(bankA[g % 2][:, 0:S], kt[:, g, 0:P], qt[:, g], start=True, stop=True)
                nc.tensor.matmul(bankA[g % 2][:, S:S + P], kt[:, g, P:S], qt[:, g, P:S],
                                 start=True, stop=True).then_inc(self.scores, 1)

            def suffix(self, pe, g):
                pe.wait_ge(self.soft, g + 1)
                if g >= 2:
                    pe.wait_ge(self.expo, g - 1)
                suffix, ones = const[:, C_SUFFIX:C_SUFFIX + P], const[:, C_ONES:C_ONES + P]
                bank = bankT[g % 2]
                nc.tensor.matmul(bank[:, 0:S], suffix, pt[:, g % 2, 0:S], start=True, stop=False)
                nc.tensor.matmul(bank[:, P:S], ones, pt[:, g % 2, S:S + P], start=False, stop=True)
                nc.tensor.matmul(bank[:, S:S + P], suffix, pt[:, g % 2, S:S + P],
                                 start=True, stop=True).then_inc(self.sums, 1)

            def value(self, pe, g):
                pe.wait_ge(self.weights, g + 1)
                if g in self.bank_free:
                    pe.wait_ge(*self.bank_free[g])
                a, c = nat[:, 1, g % 2], slice(HD2 * (g % 4), HD2 * (g % 4) + HD2)
                vals = [v[:, k, HD2 * g:HD2 * (g + 1)] for k in range(2)]
                nc.tensor.matmul(bankD[0][g // 4][:, c], a[:, 0:P], vals[0], start=True, stop=True)
                nc.tensor.matmul(bankD[1][g // 4][:, c], a[:, P:S], vals[0], start=True, stop=False)
                nc.tensor.matmul(bankD[1][g // 4][:, c], a[:, S:S + P], vals[1], start=False,
                                 stop=True).then_inc(self.summed, 1)

            def tensor(self, pe):
                for s, value in self.need:
                    pe.wait_ge(s, value)
                self.score(pe, 0)
                for g in range(H2 + 3):
                    if g + 1 < H2:
                        self.score(pe, g + 1)
                    for filler, step in fill_steps(self.fillers, g):
                        filler.tensor(pe, step)
                    if g < H2:
                        self.suffix(pe, g)
                    if 1 <= g <= H2:
                        self.value(pe, g - 1)
                    for f in range(4):
                        if self.fin.fins[f][2] == g - 1:
                            self.fin.turn(pe, f)

            def scalar(self, act):
                nc.scalar.preload_act_table_set("natural_log_exp_and_others")
                for g in range(H2 + 4):
                    if g < H2:
                        e = pt[:, g % 2, 0:S + P]
                        act.wait_ge(self.masked, g + 1)
                        if g >= 2:
                            act.wait_ge(self.sums, g - 1)
                        own(act, act_own, nc.scalar.activation(e, lg[:, g % 2, 0:S + P], ACT.Abs))
                        own(act, act_own, nc.scalar.activation(e, e, ACT.Exp, scale=-1.0))
                        nc.scalar.activation(e, e, ACT.Ln, bias=one[:]).then_inc(self.logs, 1)
                    if 1 <= g <= H2:
                        b = (g - 1) % 2
                        act.wait_ge(self.expo, g)
                        if g >= 3:
                            act.wait_ge(self.summed, g - 2)
                        nc.scalar.activation(nat[:, 1, b, 0:S + P], lg[:, b, 0:S + P], ACT.Exp)\
                            .then_inc(self.weights, 1)
                    for filler, step in fill_steps(self.fillers, g):
                        filler.scalar(act, step)
                    for f in range(4):
                        if self.fin.fins[f][2] == g - 2:
                            self.fin.take_hi(act, f)

            def vector(self, dve):
                for g in range(H2 + 4):
                    if g < H2:
                        dve.wait_ge(self.scores, g + 1)
                        if g >= 2:
                            dve.wait_ge(self.weights, g - 1)
                        nc.vector.tensor_tensor(lg[:, g % 2, 0:S + P], bankA[g % 2][:, 0:S + P],
                                                const[:, C_STRICT:C_STRICT + S + P], ALU.add)\
                            .then_inc(self.masked, 1)
                    if 1 <= g <= H2:
                        b = (g - 1) % 2
                        dve.wait_ge(self.sums, g)
                        nc.vector.tensor_tensor(lg[:, b, 0:S + P], lg[:, b, 0:S + P], bankT[b][:, 0:S + P],
                                                ALU.add).then_inc(self.expo, 1)
                    if g < H2:
                        dve.wait_ge(self.logs, g + 1)
                        nc.vector.scalar_tensor_tensor(
                            out=pt[:, g % 2, 0:S + P], in0=lg[:, g % 2, 0:S + P], scalar=0.0,
                            in1=pt[:, g % 2, 0:S + P], op0=ALU.max, op1=ALU.add).then_inc(self.soft, 1)
                    for filler, step in fill_steps(self.fillers, g):
                        filler.vector(dve, step)
                    for f in range(4):
                        if self.fin.fins[f][2] == g - 1:
                            self.fin.out_rows(dve, f)
                        if self.fin.fins[f][2] == g - 2:
                            self.fin.take_lo(dve, f)

            def sync(self, sp):
                for filler in self.fillers:
                    filler.sync(sp)

            def gpsimd(self, pool):
                pass

        class OutProject:
            def __init__(self, name, section, ks, stat_h, stat_l, need, residual=True, following=None,
                         need_last=(), pairs=None):
                self.need_last, self.pairs = need_last, pairs
                self.following = following
                self.name, self.n0, self.ks, self.need = name, AT[section], ks, need
                self.stat_h, self.stat_l, self.residual = stat_h, stat_l, residual
                self.full0 = NB * NT * len(out_projects)
                out_projects.append(name)
                self.chunks = len(ks) // 2
                ends[self.n0 + self.chunks // 2 - 1] = (out_full, self.full0 + NT, 0)
                ends[self.n0 + self.chunks - 1] = (out_full, self.full0 + NB * NT, 0)

            def tensor(self, pe):
                for s, value in self.need:
                    pe.wait_ge(s, value)
                for c in range(self.chunks):
                    take_chunk(pe, self.n0 + c)
                    for j in range(4):
                        i = 4 * c + j
                        block, k = i // len(self.ks), self.ks[i % len(self.ks)]
                        if i == len(self.ks):
                            for s, value in self.need_last:
                                pe.wait_ge(s, value)
                        if self.pairs and block == 0 and k % 2 == 0:
                            pe.wait_ge(self.pairs, k // 2 + 1)
                        if self.following and i == 3 * len(self.ks) // 2:
                            norm_tensor(pe, self.following, 0)
                        for t in range(NT):
                            last = mm3(bankD[t][block], self.stat_h[:, k, t * P:(t + 1) * P],
                                       self.stat_l[:, k, t * P:(t + 1) * P], slot_of(self.n0 + c), j, TW,
                                       k == self.ks[0], k == self.ks[-1])
                            if k == self.ks[-1]:
                                last.then_inc(out_full, 1)
                    used(last, self.n0 + c)

            def scalar(self, act):
                tail_scalar(act, [self.n0 + c for c in range(self.chunks)], self.following)

            def vector(self, dve):
                chunks = [self.n0 + c for c in range(self.chunks)]
                if self.residual:
                    tail_vector(dve, chunks, self.following, out_full, 1.0, self.full0)
                else:
                    for n in chunks:
                        next_lo(dve, n)

            def sync(self, sp):
                for c in range(self.chunks):
                    load_chunk(sp, self.n0 + c)

            def gpsimd(self, pool):
                pass

        class Mixture:

            def __init__(self, attend, gates_b):
                self.attend, self.gates_b = attend, gates_b
                self.full = sem("gate_full")
                self.raw = sem("gate_raw")
                self.gate = sem("gate_sigmoid")
                self.mixed = sem("gate_mixed")
                self.bias_in = sem("gate_bias_in")
                self.ps = sem("mix_ps")
                self.hi = sem("mix_hi")
                self.lo = sem("mix_lo")
                self.branch_a = OutProject("br_a", "br_a", list(range(4)), ot_h, ot_l,
                                           [attend.ready, gates_b[1].ready], residual=False)
                self.branch_b = OutProject("br_b", "br_b", list(range(4, 8)), ot_h, ot_l, [(self.mixed, NT)],
                                           residual=False, need_last=[(self.mixed, 2 * NT)])
                for u in range(NB):
                    ends[self.chunk(u) + 1] = (self.full, NT * (u + 1), 0)

            def chunk(self, u):
                return AT[f"gate_a{u}"]

            def gate_tensor(self, pe, u):
                if u == 0:
                    pe.wait_ge(self.attend.logits, len(self.attend.groups))
                for c in range(2):
                    take_chunk(pe, self.chunk(u) + c)
                    for t in range(NT):
                        if c == 0 and u > 0:
                            pe.wait_ge(self.raw, NB * NT + t + 1)
                        for j in range(4):
                            k = 4 * c + j
                            last = mm3(bankA[t], xt_h[:, k, t * P:(t + 1) * P],
                                       xt_l[:, k, t * P:(t + 1) * P], slot_of(self.chunk(u) + c), j, TW,
                                       k == 0, k == KC - 1)
                        if c == 1:
                            last.then_inc(self.full, 1)
                    used(last, self.chunk(u) + c)

            def tensor(self, pe):
                self.gate_tensor(pe, 0)
                self.branch_a.tensor(pe)
                self.gate_tensor(pe, 1)
                self.branch_b.tensor(pe)
                for pair, bank in enumerate(bankT + bankA):
                    pe.wait_ge(self.mixed, NB * NT + NT * (pair // 2 + 1))
                    for j in range(2):
                        for t in range(NT):
                            k = 2 * pair + j
                            last = nc.tensor.transpose(bank[:, j * S + t * P:j * S + (t + 1) * P],
                                                       v[:, t, k * P:(k + 1) * P], ident)
                    last.then_inc(self.ps, 1)

            def gates_scalar(self, act, first, gates):
                for i, rows in enumerate(gates):
                    act.wait_ge(self.raw, first + i + 1)
                    nc.scalar.activation(rows, rows, ACT.Sigmoid).then_inc(self.gate, 1)

            def scalar(self, act):
                nc.scalar.preload_act_table(ACT.Sigmoid)
                self.gates_scalar(act, 0, [gates.to(t) for gates in self.gates_b for t in range(NT)])
                for u in range(NB):
                    next_hi(act, self.chunk(u))
                    self.gates_scalar(act, NB * NT + NT * u, [lg[:, t] for t in range(NT)])
                    next_hi(act, self.chunk(u) + 1)
                    (self.branch_a, self.branch_b)[u].scalar(act)
                for pair, bank in enumerate(bankT + bankA):
                    act.wait_ge(self.ps, pair + 1)
                    nc.scalar.activation(xt_h[:, 2 * pair:2 * pair + 2],
                                         bank.rearrange("p (k s) -> p k s", k=2), ACT.Copy).then_inc(self.hi, 1)

            def raw_vector(self, dve, u):
                for t in range(NT):
                    if u > 0:
                        dve.wait_ge(self.mixed, NT * (u - 1) + t + 1)
                    dve.wait_ge(self.full, NT * u + t + 1)
                    nc.vector.scalar_tensor_tensor(out=lg[:, t], in0=bankA[t], scalar=rms("mix", t),
                                                   in1=nat[:, 0, u], op0=ALU.mult, op1=ALU.add)\
                        .then_inc(self.raw, 1)

            def mix_a(self, dve, block):
                for t in range(NT):
                    dve.wait_ge(self.gate, NB * NT + NT * block + t + 1)
                    dve.wait_ge(out_full, self.branch_a.full0 + NT * block + t + 1)
                    nc.vector.tensor_tensor(v[:, t, block * TW:(block + 1) * TW], lg[:, t], bankD[t][block],
                                            ALU.mult).then_inc(self.mixed, 1)

            def mix_b(self, dve, block):
                for t in range(NT):
                    dve.wait_ge(self.gate, NT * block + t + 1)
                    dve.wait_ge(out_full, self.branch_b.full0 + NT * block + t + 1)
                    to, gates = v[:, t, block * TW:(block + 1) * TW], self.gates_b[block].to(t)
                    own(dve, dve_own, nc.vector.tensor_tensor(gates, gates, bankD[t][block], ALU.mult))
                    nc.vector.tensor_tensor(to, to, gates, ALU.add).then_inc(self.mixed, 1)

            def vector(self, dve):
                dve.wait_ge(self.bias_in, 16)
                for block, fill in enumerate(self.gates_b):
                    for t in range(NT):
                        dve.wait_ge(fill_copied, fill.full0 + t + 1)
                        nc.vector.tensor_tensor(fill.to(t), fill.to(t), nat[:, 1, block], ALU.add)\
                            .then_inc(self.raw, 1)
                next_lo(dve, self.chunk(0))
                self.raw_vector(dve, 0)
                next_lo(dve, self.chunk(0) + 1)
                next_lo(dve, self.branch_a.n0)
                self.mix_a(dve, 0)
                next_lo(dve, self.branch_a.n0 + 1)
                next_lo(dve, self.chunk(1))
                self.raw_vector(dve, 1)
                self.mix_a(dve, 1)
                next_lo(dve, self.chunk(1) + 1)
                next_lo(dve, self.branch_b.n0)
                self.mix_b(dve, 0)
                self.mix_b(dve, 1)
                next_lo(dve, self.branch_b.n0 + 1)
                for pair, bank in enumerate(bankT + bankA):
                    dve.wait_ge(self.hi, pair + 1)
                    nc.vector.tensor_tensor(xt_l[:, 2 * pair:2 * pair + 2],
                                            bank.rearrange("p (k s) -> p k s", k=2),
                                            xt_h[:, 2 * pair:2 * pair + 2].bitcast(F32),
                                            ALU.subtract).then_inc(self.lo, 1)

            def sync(self, sp):
                for section in ("gate_a0", "br_a", "gate_a1", "br_b"):
                    for c in range(2):
                        load_chunk(sp, AT[section] + c)

            def gpsimd(self, pool):
                pool.wait_ge(rows_ps, self.attend.fin.f0 + 4)
                pool.dma_start(nat[:, :, :, :].rearrange("p a b n -> p (a b n)"),
                               dram["b_gate"].partition_broadcast(P)).then_inc(self.bias_in, 16)

        class Norm:

            def __init__(self, name, need=()):
                self.name, self.mem, self.need = name, name.startswith("mem"), need

            def tensor(self, pe):
                if self.mem:
                    for s, value in self.need:
                        pe.wait_ge(s, value)
                    norm_tensor(pe, self.name, 0)
                    norm_tensor(pe, self.name, 1)

            def scalar(self, act):
                if self.mem:
                    norm_scalar(act, self.name, 0)
                    norm_scalar(act, self.name, 1)
                else:
                    rms_scalar(act, self.name)

            def vector(self, dve):
                if self.mem:
                    norm_vector(dve, self.name, 0)
                    norm_vector(dve, self.name, 1)
                else:
                    root_vector(dve, self.name)

            def sync(self, sp):
                pass

            def gpsimd(self, pool):
                pass

        class Memory:

            def __init__(self, attend):
                self.attend = attend
                self.squared = sem("mem_squared")
                self.rooted = sem("mem_rooted")
                self.c = 2 * NORM["mem0"]

            def tensor(self, pe):
                pass

            def scalar(self, act):
                act.wait_ge(mem_in, 16)
                for t in range(NT):
                    nc.scalar.activation(ot_h[:, 4 * t:4 * t + 4].rearrange("p k s -> p (k s)"), mem[:, t],
                                         ACT.Square, scale=D ** -0.5,
                                         accum_out=ms[:, self.c + t:self.c + t + 1]).then_inc(self.squared, 1)

            def vector(self, dve):
                dve.wait_ge(self.squared, NT)
                rsqrt(dve, ms[:, self.c:self.c + 2], rs[:, self.c:self.c + 2], 1.0, EPS, 2)\
                    .then_inc(self.rooted, 1)

            def sync(self, sp):
                pass

            def gpsimd(self, pool):
                pool.wait_ge(self.attend.logits, len(self.attend.groups))
                pool.dma_start(mem, dram["mem"]).then_inc(mem_in, 16)

        onehot = kt[0:NBUCK + 1, 0:2].rearrange("p k s -> p (k s)")[:, 0:RELW + 1]
        tab = qt[0:NBUCK + 1, 0, 0:16]
        byd = qt[0:16, 2:4].rearrange("p k s -> p (k s)")[:, 0:RELW + 1]

        class Tables:
            TWO_PI = 6.283185307179586
            C1 = 6.28125
            C2 = float(np.float32(TWO_PI - C1))
            C3 = TWO_PI - C1 - C2

            def __init__(self):
                self.in_ = sem("tables_in")
                self.neg = sem("tables_neg")
                self.ps = sem("tables_ps")
                self.sb = sem("tables_sb")
                self.out = sem("tables_out")
                self.rel_in = sem("rel_in")
                self.angle = sem("tables_angle")
                self.trig = sem("tables_trig")
                self.scratch = nc.dram_tensor("bias_by_distance", (16, P, RELW + 1), F32, kind="Internal").ap()

            def gpsimd(self, pool):
                pool.dma_start(onehot, dram["consts"][0:NBUCK + 1, C_BUCK:NCONST])\
                    .then_inc(self.in_, 16)
                pool.dma_start(tab[0:NBUCK], dram["rel_bias"]).then_inc(self.in_, 16)
                pool.wait_ge(self.sb, 1)
                pool.dma_start(self.scratch, byd.unsqueeze(1).to_broadcast(
                    [16, P, RELW + 1])).then_inc(self.out, 16)
                pool.wait_ge(self.out, 16)
                spread = bass.AP(tensor=self.scratch.tensor, offset=P - 1,
                                 ap=[[RELW, P], [P * (RELW + 1), 16], [1, S]])
                pool.dma_start(rel[:], spread).then_inc(self.rel_in, 16)

            def tensor(self, pe):
                pe.wait_ge(self.in_, 32)
                pe.wait_ge(self.neg, 1)
                nc.tensor.matmul(bankD[1][1][0:16, 0:RELW + 1], tab,
                                 onehot, start=True, stop=True).then_inc(self.ps, 1)

            def bias_scalar(self, act):
                act.wait_ge(self.ps, 1)
                nc.scalar.activation(byd, bankD[1][1][0:16, 0:RELW + 1], ACT.Copy)\
                    .then_inc(self.sb, 1)

            def scalar(self, act):
                act.wait_ge(self.angle, 1)
                nc.scalar.activation(trig[:], v[:, 0, 0:4 * HALF].rearrange(
                    "p (a t d) -> p a t d", a=2, t=NT), ACT.Sin).then_inc(self.trig, 1)

            def vector(self, dve):
                dve.wait_ge(consts_in, 48)
                w = 2 * NT * HALF
                angle, turns, red = v[:, 0, 256:256 + w], v[:, 0, 512:512 + w], v[:, 0, 0:w]
                own(dve, dve_own, nc.vector.tensor_copy(pos[:, 2:4], pos[:, 0:NT].bitcast(I32)))
                for t in range(NT):
                    for a in range(2):
                        last = nc.vector.tensor_scalar(
                            angle[:, (2 * a + t) * HALF:(2 * a + t + 1) * HALF],
                            const[:, C_FREQ:C_FREQ + HALF], pos[:, 2 + t:3 + t], None, ALU.mult)
                own(dve, dve_own, last)
                for a, quarter in enumerate((0.25, 0.0)):
                    part = slice(a * w // 2, (a + 1) * w // 2)
                    last = nc.vector.tensor_scalar(turns[:, part], angle[:, part], 1.0 / self.TWO_PI, quarter,
                                                   ALU.mult, ALU.add)
                own(dve, dve_own, last)
                whole = v[:, 0, 768:768 + w].bitcast(I32)
                own(dve, dve_own, nc.vector.tensor_copy(whole, turns))
                own(dve, dve_own, nc.vector.tensor_copy(turns, whole))
                step = angle
                for c in (self.C1, self.C2, self.C3):
                    own(dve, dve_own, nc.vector.scalar_tensor_tensor(out=red, in0=turns, scalar=-c, in1=step,
                                                                     op0=ALU.mult, op1=ALU.add))
                    step = red
                own(dve, dve_own, nc.vector.tensor_scalar(red[:, 0:w // 2], red[:, 0:w // 2], self.TWO_PI / 4, None,
                                                          ALU.add))
                nc.vector.tensor_scalar(red, red, 3.1415925, -3.1415925, ALU.min, ALU.max)\
                    .then_inc(self.angle, 1)

            def sync(self, sp):
                pass

        class Final:

            def __init__(self):
                self.gain_in = sem("final_gain_in")
                self.made = sem("final_rows")
                self.stored = sem("final_stored")

            def gpsimd(self, pool):
                pool.wait_ge(h_ready, 32)
                pool.dma_start(qt[:, 0:4].rearrange("p k s -> p (k s)"),
                               dram["norm_final"].partition_broadcast(P)).then_inc(self.gain_in, 16)

            def tensor(self, pe):
                pass

            def scalar(self, act):
                rms_scalar(act, "final")

            def vector(self, dve):
                root_vector(dve, "final")
                dve.wait_ge(self.gain_in, 16)
                dve.wait_ge(rs_ready, RMS_AT["final"])
                for t in range(NT):
                    nc.vector.scalar_tensor_tensor(out=v[:, t], in0=h[:, t], scalar=rms("final", t),
                                                   in1=qt[:, 0:4].rearrange("p k s -> p (k s)"),
                                                   op0=ALU.mult, op1=ALU.mult).then_inc(self.made, 1)

            def sync(self, sp):
                rows = out.rearrange("(t p) d -> p t d", p=P)
                for t in range(NT):
                    sp.wait_ge(self.made, t + 1)
                    sp.dma_start(rows[:, t], v[:, t]).then_inc(self.stored, 16)
                sp.wait_ge(self.stored, 16 * NT)

        def row(name):
            return lambda t: rms(name, t)

        def latent_row(i):
            c = 2 * len(NORMS) + 2 * i
            return lambda t: rs[:, c + t:c + t + 1]

        def same_half(per):
            return [list(range(h0 + odd, h0 + 2 * per, 2)) for h0 in range(0, 8, 2 * per) for odd in range(2)]

        def moba_dsa():
            groups, fins = [], []
            for b in (1, 0):
                for t in range(NT):
                    keys, per = (t + 1) * P, 4 // (t + 1)
                    for heads in same_half(per):
                        group = []
                        for i, hd in enumerate(heads):
                            half = slice(64 * (hd % 2), 64 * (hd % 2) + 64)
                            k4 = 4 * b + hd // 2
                            bias = rel[:, 8 * b + hd, S - keys:S] if b else \
                                nat[:, 1, len(groups) % 2, i * keys:(i + 1) * keys]
                            group.append(dict(
                                at=i * keys, width=keys, tile=t, head=8 * b + hd, bias=bias,
                                qk=[(qt[half, k4, t * P:(t + 1) * P], kt[half, k4, 0:keys])],
                                v=[v[:, j, TW * b + HD1 * hd:TW * b + HD1 * (hd + 1)] for j in range(t + 1)],
                                out=bankD[t][b][:, HD1 * hd:HD1 * (hd + 1)], col=16 * b + 8 * t + hd))
                        groups.append(group)
                    fins.append((t, b, len(groups) - 1, 16 * b + 8 * t, H1))
            return groups, fins, len(groups) // 2

        def mla_groups():
            groups, fins = [], []
            for t in range(NT):
                keys, per = (t + 1) * P, 4 // (t + 1)
                for heads in same_half(per):
                    group = []
                    for i, hd in enumerate(heads):
                        half, s = slice(64 * (hd % 2), 64 * (hd % 2) + 64), slice(t * P, (t + 1) * P)
                        group.append(dict(
                            at=i * keys, width=keys, tile=t, head=hd,
                            bias=const[:, C_CAUSAL + S - keys:C_CAUSAL + S],
                            qk=[(qt[:, hd, s], kt[:, hd, 0:keys]),
                                (pet[half, hd // 2, s], pet[half, 4, 0:keys])],
                            v=[v[:, j, HD2 * hd:HD2 * (hd + 1)] for j in range(t + 1)],
                            out=bankD[t][hd // 4][:, HD2 * (hd % 4):HD2 * (hd % 4) + HD2], col=8 * t + hd))
                    groups.append(group)
                    if heads[-1] == 7:
                        fins += [(t, b, len(groups) - 1, 8 * t + 4 * b, 4) for b in ((1,) if t else (0, 1))]
                    elif heads[-1] == 3:
                        fins.append((t, 0, len(groups) - 1, 8 * t, 4))
            return groups, fins

        def mem_groups():
            groups, fins = [], []
            for t in range(NT):
                for h0 in (0, 2):
                    groups.append([dict(
                        at=i * S, width=S, bias=const[:, C_CAUSAL:C_CAUSAL + 1].to_broadcast([P, S]),
                        qk=[(qt[:, hd, t * P:(t + 1) * P], rel[:, hd])],
                        v=[mem_v[:, j, HD2 * hd:HD2 * (hd + 1)] for j in range(2)],
                        out=bankD[t][0][:, HD2 * hd:HD2 * (hd + 1)], col=4 * t + hd)
                        for i, hd in enumerate((h0, h0 + 1))])
                fins.append((t, 0, len(groups) - 1, 4 * t, NXH))
            return groups, fins

        def mem_norm(i):
            return Norm(f"mem{i}", [(xt_lo, 4 * NORM[f"mem{i}"])])

        all8 = list(range(KC))

        def unit(kind, width=TW, chunks=(4, 4), **kw):
            return Unit(kind, list(range(sum(chunks))), width, chunks, **kw)

        tables = Tables()
        ffn1 = Ffn("ffn1", 11, 2, True, 0.5, "mix")

        mix = row("mix")
        mix_units = [unit("idx", 324, (2, 2, 2, 2), rows=mix)]
        for to, base, g, sc in ((qt, 4, QG_B, 0.125), (kt, 4, KG_B, 1.0), (qt, 0, QG_A, 0.125), (kt, 0, KG_A, 1.0)):
            mix_units.append(unit("qk", rows=mix, to=to, base=base, gains=g, scale=sc))
        mix_units[0:2] = mix_units[1::-1]
        mix_units += [unit("v", rows=mix, base=TW), unit("v", rows=mix, base=0)]
        mix_in = Project("mix_in", "qkv", mix_units, xt_h, xt_l, norm="mix")
        groups, fins, n_moba = moba_dsa()
        mix_attend = Attend("mix", groups, fins, [mix_in.turned_ready, mix_in.evac_ready, (tables.rel_in, 16)],
                            Select(n_moba))
        gates_b = [Fill(section, [bankD[t][block] for t in range(NT)], [free],
                        lambda t, to=to: to[:, 4 + 2 * t:6 + 2 * t].rearrange("p k s -> p (k s)"),
                        [(mix_attend.scores, n_moba)], mix, steps)
                   for section, block, free, to, steps in (
                       ("gate_b0", 0, (xt_lo, 4 * NORM["mix"] + 4), qt, (0, 1, 2, 3, 5, None, None, 4)),
                       ("gate_b1", 1, (rows_lo, mix_attend.fin.f0 + NT), kt, (9, 10, 11, 12, 13, None, None, 13)))]
        mix_attend.fillers = gates_b
        mix_attend.bank_free = {n_moba: gates_b[0].ready}
        mixture = Mixture(mix_attend, gates_b)
        mix_out = OutProject("mix_out", "w_out", all8, xt_h, xt_l, [], following="ffn2", pairs=mixture.lo)
        mem_root = Memory(mix_attend)

        ffn2 = Ffn("ffn2", 11, 2, True, 0.5, "mla")

        latent_units = [unit("latent", QL, rows=row("mla"), gains=QG_L, base=0),
                        unit("dkv", KL + ROPE, rows=row("mla"), gains=KG_L, base=3)]
        latent_units[0].ks_out, latent_units[1].ks_out = 3, 2
        mla_down = Project("mla_down", "dq", latent_units, xt_h, xt_l, norm="mla", hand_on=True)
        qrow, krow = latent_row(0), latent_row(1)
        up_units = [unit("q", chunks=(3,), rows=qrow, to=qt, base=4 * i, scale=MLA_SCALE) for i in range(2)]
        up_units.append(unit("pe", chunks=(3,), rows=qrow, to=pet, scale=MLA_SCALE))
        for kind, base in (("q", 0), ("q", 4), ("v", 0), ("v", TW)):
            up_units.append(Unit(kind, [3, 4], TW, (2,), rows=krow, to=kt, base=base))
        mla_up = Project("mla_up", "uq", up_units, ot_h, ot_l, need=[mla_down.evac_ready, (mla_down.lows, NT)],
                         scaled=(mla_down.rooted, 1), before=mla_down,
                         before_need=[mla_down.split_ready, mla_down.turned_ready], aside=(mem_norm(0), 1))

        def memory(i, fills, following):
            q = Project(f"mem_q{i}", f"xq{i}", [unit("q", rows=row(f"cross{i}"), to=qt, scale=MEM_SCALE)],
                        xt_h, xt_l, norm=f"cross{i}")
            attend = Attend(f"mem{i}", *mem_groups(), [fills[0].ready, fills[1].ready, q.turned_ready])
            out = OutProject(f"mem_out{i}", f"xo{i}", all8[:4], ot_h, ot_l, [attend.ready], following=f"mlp{i}")
            return [Norm(f"cross{i}"), q, attend, out, Ffn(f"mlp{i}", 8, 4, False, 1.0, following)]

        def memory_fills(i, free, nat_half, steps_k, rows_free, steps_v):
            k_banks, v_banks = free
            keys = Fill(f"mem_keys{i}", k_banks, [],
                        lambda t: nat[:, nat_half, t], [(mem_root.rooted, 1)], row("mem0"), steps_k, rel[:, 0:4])
            keys.normed = f"mem{i}"
            return (keys,
                    Fill(f"mem_values{i}", v_banks, [rows_free], lambda t: mem_v[:, t], [], row("mem0"),
                         steps_v + (None, None, steps_v[-1])))

        groups, fins = mla_groups()
        fills0 = memory_fills(0, (bankD[1], bankD[0]), 1, (0, 0, 1, 1, 1, 2, 2, 3),
                              (rows_lo, sum(len(f) for f in all_fins) + 2), (5, 6, 7, 8, 9))
        mla_attend = Attend("mla", groups, fins, [mla_up.turned_ready, mla_up.evac_ready], fillers=fills0,
                            bank_free={2: fills0[0].ready})
        mla_out = OutProject("mla_out", "mla_o", all8, ot_h, ot_l, [mla_attend.ready, fills0[1].ready],
                             following="cross0")
        memory0 = memory(0, fills0, "sb")
        sb_row = row("sb")
        sb_units = [unit("q", rows=sb_row, to=qt, base=4 * i, scale=SB_SCALE) for i in range(2)]
        sb_units += [unit("q", rows=sb_row, to=kt, base=4 * i) for i in range(2)]
        sb_units += [unit("v", rows=sb_row, base=TW * i) for i in range(2)]
        sb_in = Project("sb_in", "sb_qkv", sb_units, xt_h, xt_l, norm="sb", aside=(mem_norm(1), 5))
        fills1 = memory_fills(1, tuple([bankD[t][block] for t in range(NT)] for block in (1, 0)), 0,
                              (0, 0, 1, 2, 2, 3, 3, 5), (rows_lo, sum(len(f) for f in all_fins) + 2), (7, 8, 9, 10, 11))
        stick = Stick("sb", [sb_in.turned_ready, sb_in.evac_ready], fills1, {4: fills1[0].ready})
        sb_out = OutProject("sb_out", "sb_o", all8, ot_h, ot_l, [stick.ready, fills1[1].ready],
                            following="cross1")

        phases = [ffn1, Norm("mix"), mix_in, mix_attend, mixture, mem_root, mix_out, ffn2,
                  Norm("mla"), mla_down, mla_up, mla_attend, mla_out]
        phases += memory0
        phases += [Norm("sb"), sb_in, stick, sb_out]
        phases += memory(1, fills1, None)
        phases.append(Final())

        block = ctx.enter_context(nc.Block())

        @block.sync
        def _(sp):
            sp.dma_start(h[:, :, 0:TW], dram["x"][:, :, 0:TW]).then_inc(x_in[0], 16)
            sp.dma_start(gain[:], dram["gains"]).then_inc(consts_in, 16)
            for phase in phases:
                phase.sync(sp)

        @block.gpsimd
        def _(pool):
            tables.gpsimd(pool)
            for phase in phases:
                phase.gpsimd(pool)

        @block.scalar
        def _(act):
            nc.scalar.preload_act_table(ACT.Sin)
            act.dma_start(pos[:, 0:NT].bitcast(I32), dram["positions"]).then_inc(consts_in, 16)
            act.dma_start(const[:], dram["consts"][:, 0:C_BUCK]).then_inc(consts_in, 16)
            act.wait_ge(consts_in, 48)
            act.wait_ge(one_set, 1)
            norm_scalar(act, "ffn1", 0)
            for n in range(RING):
                split_hi(act, n)
                if n == 1:
                    tables.scalar(act)
            for phase in phases:
                phase.scalar(act)

        @block.vector
        def _(dve):
            nc.vector.memset(one[:], 1.0).then_inc(one_set, 1)
            nc.vector.memset(tab[NBUCK:NBUCK + 1], NEG).then_inc(tables.neg, 1)
            tables.vector(dve)
            norm_vector(dve, "ffn1", 0)
            for n in range(RING):
                split_lo(dve, n)
            for phase in phases:
                phase.vector(dve)

        @block.tensor
        def _(pe):
            pe.wait_ge(consts_in, 48)
            norm_tensor(pe, "ffn1", 0)
            for phase in phases:
                phase.tensor(pe)


def kernel(**inputs):
    import concourse.bacc as bacc
    from concourse.bass_utils import run_bass_kernel_spmd

    nc = bacc.Bacc("TRN2", target_bir_lowering=False, num_devices=1)
    arrays = host_arrays(inputs)
    dram = {n: nc.dram_tensor(n, a.shape, mybir.dt.from_np(a.dtype), kind="ExternalInput").ap()
            for n, a in arrays.items()}
    out = nc.dram_tensor("out", (S, D), F32, kind="ExternalOutput").ap()
    build(nc, dram, out)
    result = run_bass_kernel_spmd(nc, [arrays], core_ids=[0])
    return result.results[0]["out"].reshape(1, S, D)
```
